# Optimizing a Trainium2 kernel written in Bass

```python
import math
import jax, jax.numpy as jnp
from jax import lax
import numpy as np

D_MODEL = 1024
BATCH = 1
SEQ = 512
DEPTH = 1
DEC_BATCH = 8
DEC_SEQ = 16
PAST_LEN = 512

CHUNK = 64
Q_BLOCK = 128
A_HEADS = 4
A_DH = D_MODEL // 16
A_DV = 2 * A_DH
A_WIDTH = A_HEADS * A_DV
G_HEADS = 4
G_DK = D_MODEL // 16
G_DV = D_MODEL // 8
G_WIDTH = G_HEADS * G_DV
G_RANK = 16
G_TAU = 16.0
MIX_WIDTH = A_WIDTH + G_WIDTH
SPLIT_SIZES = (A_HEADS * 2 * A_DH, A_HEADS * 2 * A_DH, A_WIDTH, G_HEADS * G_DK, G_HEADS * G_DK, G_WIDTH, G_RANK, G_WIDTH)
IN_WIDTH = 3088
N_GROUPS = 4
EXPERTS_PER_GROUP = 8
N_EXPERTS = N_GROUPS * EXPERTS_PER_GROUP
TOP_K_INNER = 2
D_EXPERT = D_MODEL // 4
EPS = 1e-6

kernel_name = 'hymba_diffattn_gla_hmoe_stream_step'

def rms_norm(x, gain):
    xf = x.astype(jnp.float32)
    y = xf * lax.rsqrt(jnp.mean(xf * xf, axis=-1, keepdims=True) + EPS)
    return (y * gain.astype(jnp.float32)).astype(x.dtype)

def diff_lambda(lq1, lk1, lq2, lk2, lam_init):
    f32 = jnp.float32
    return (jnp.exp(jnp.sum(lq1.astype(f32) * lk1.astype(f32)))
            - jnp.exp(jnp.sum(lq2.astype(f32) * lk2.astype(f32))) + lam_init)

def diff_attend(q, k, v, lam, mask):
    s = jnp.einsum('bqhmd,bkhmd->bhmqk', q, k, preferred_element_type=jnp.float32) * (A_DH ** -0.5)
    if mask is not None:
        s = jnp.where(mask, s, -jnp.inf)
    p = jax.nn.softmax(s, axis=-1)
    p = p[:, :, 0] - lam * p[:, :, 1]
    return jnp.einsum('bhqk,bkhv->bqhv', p.astype(v.dtype), v)

def diff_attention_prompt(q, k, v, lam):
    B, L = q.shape[0], q.shape[1]
    nqb = L // Q_BLOCK
    q_blocks = jnp.moveaxis(q.reshape(B, nqb, Q_BLOCK, A_HEADS, 2, A_DH), 1, 0)
    key_chunk = jnp.arange(L) // CHUNK

    def one_block(args):
        qb, i = args
        q_chunk = (i * Q_BLOCK + jnp.arange(Q_BLOCK)) // CHUNK
        mask = key_chunk[None, :] <= q_chunk[:, None]
        return diff_attend(qb, k, v, lam, mask)

    o = lax.map(one_block, (q_blocks, jnp.arange(nqb)))
    return jnp.moveaxis(o, 0, 1).reshape(B, L, A_HEADS, A_DV)

def gla_chunk(S, q, k, v, la):
    C = q.shape[1]
    b = jnp.cumsum(la, axis=1)
    causal = jnp.tril(jnp.ones((C, C), dtype=bool))[None, :, :, None, None]
    decay = jnp.exp(jnp.where(causal, b[:, :, None] - b[:, None, :], -jnp.inf))
    scores = jnp.einsum('bthd,btshd,bshd->bhts', q, decay, k)
    o = (jnp.einsum('bhts,bshv->bthv', scores, v)
         + jnp.einsum('bthd,bhdv->bthv', q * jnp.exp(b), S))
    b_last = b[:, -1]
    S_new = (jnp.exp(b_last)[..., None] * S
             + jnp.einsum('bshd,bshv->bhdv', k * jnp.exp(b_last[:, None] - b), v))
    return S_new, o

def gla_prompt(q, k, v, la):
    B, L = q.shape[0], q.shape[1]
    n_chunks = L // CHUNK

    def to_chunks(t):
        return jnp.moveaxis(t.reshape((B, n_chunks, CHUNK) + t.shape[2:]), 1, 0)

    S0 = jnp.zeros((B, G_HEADS, G_DK, G_DV), jnp.float32)
    S, o = lax.scan(lambda S, xs: gla_chunk(S, *xs), S0,
                    (to_chunks(q), to_chunks(k), to_chunks(v), to_chunks(la)))
    return S, jnp.moveaxis(o, 0, 1).reshape(B, L, G_HEADS, G_DV)

def token_mixer(h, w_in, q_gain, k_gain, lam, lam_init, a_out_gain, w_a2, b_a,
                g_out_gain, w_out, cache_k=None, cache_v=None, state=None):
    B, L, _ = h.shape
    f32 = jnp.float32
    z = jnp.einsum('bld,de->ble', h, w_in)
    split_idx = [int(i) for i in np.cumsum(SPLIT_SIZES)[:-1]]
    aq, ak, av, gq, gk, gv, ga, gr = jnp.split(z, split_idx, axis=-1)
    aq = rms_norm(aq.reshape(B, L, A_HEADS, 2, A_DH), q_gain)
    ak = rms_norm(ak.reshape(B, L, A_HEADS, 2, A_DH), k_gain)
    av = av.reshape(B, L, A_HEADS, A_DV)
    if cache_k is None:
        ao = diff_attention_prompt(aq, ak, av, lam)
    else:
        keys = jnp.concatenate([cache_k.astype(ak.dtype), ak], axis=1)
        vals = jnp.concatenate([cache_v.astype(av.dtype), av], axis=1)
        ao = diff_attend(aq, keys, vals, lam, None)
    ao = (rms_norm(ao, a_out_gain) * (1.0 - lam_init)).reshape(B, L, A_WIDTH)
    gq = gq.reshape(B, L, G_HEADS, G_DK).astype(f32) * (G_DK ** -0.5)
    gk = gk.reshape(B, L, G_HEADS, G_DK).astype(f32)
    gv = gv.reshape(B, L, G_HEADS, G_DV).astype(f32)
    la = (jax.nn.log_sigmoid(jnp.einsum('blr,rk->blk', ga, w_a2).astype(f32) + b_a.astype(f32))
          / G_TAU).reshape(B, L, G_HEADS, G_DK)
    if state is None:
        s_new, go = gla_prompt(gq, gk, gv, la)
    else:
        s_new, go = gla_chunk(state.astype(f32), gq, gk, gv, la)
    go = rms_norm(go.astype(h.dtype), g_out_gain).reshape(B, L, G_WIDTH) * jax.nn.silu(gr)
    out = jnp.einsum('ble,ed->bld', jnp.concatenate([ao, go], axis=-1), w_out)
    return out, ak, av, s_new.astype(h.dtype)

def hier_moe(h, w_group, b_group, w_erouter, b_erouter, w_gate, w_up, w_down):
    B, L, D = h.shape
    hf = h.reshape(B * L, D)
    N = hf.shape[0]
    f32 = jnp.float32
    g_logits = (hf @ w_group + b_group).astype(f32)
    g_prob = jax.nn.softmax(g_logits, axis=-1)
    _, g_idx = lax.top_k(g_logits, 1)
    g_w = jnp.take_along_axis(g_prob, g_idx, axis=-1)
    e_logits = (hf @ w_erouter + b_erouter).astype(f32).reshape(N, N_GROUPS, EXPERTS_PER_GROUP)
    e_sel = jnp.take_along_axis(e_logits, g_idx[:, :, None], axis=1)[:, 0]
    top_v, top_i = lax.top_k(e_sel, TOP_K_INNER)
    weights = g_w * jax.nn.softmax(top_v, axis=-1)
    expert_id = g_idx * EXPERTS_PER_GROUP + top_i
    combine = jnp.sum(jax.nn.one_hot(expert_id, N_EXPERTS, dtype=f32) * weights[..., None], axis=1)
    combine = combine.astype(h.dtype)
    y = jnp.zeros_like(hf)
    for e in range(N_EXPERTS):
        ye = (jax.nn.silu(hf @ w_gate[e]) * (hf @ w_up[e])) @ w_down[e]
        y = y + combine[:, e:e + 1] * ye
    return y.reshape(B, L, D)

def setup_inputs(seed: int = 0) -> dict:
    key = jax.random.key(seed)
    ks = jax.random.split(key, 26)
    f32 = jnp.float32

    def nrm(k, shape, scale):
        return jax.random.normal(k, shape, f32) * scale

    def gain(k, shape):
        return 1.0 + 0.02 * jax.random.normal(k, shape, f32)

    return {
        'x_prompt': nrm(ks[0], (BATCH, SEQ, D_MODEL), 1.0),
        'x_sample': nrm(ks[1], (DEC_BATCH, DEC_SEQ, D_MODEL), 1.0),
        'cache_k': nrm(ks[2], (DEPTH, DEC_BATCH, PAST_LEN, A_HEADS, 2, A_DH), 1.0),
        'cache_v': nrm(ks[3], (DEPTH, DEC_BATCH, PAST_LEN, A_HEADS, A_DV), 1.0),
        'state_gla': nrm(ks[4], (DEPTH, DEC_BATCH, G_HEADS, G_DK, G_DV), 1.0),
        'norm1_gain': gain(ks[5], (DEPTH, D_MODEL)),
        'w_in': nrm(ks[6], (DEPTH, D_MODEL, IN_WIDTH), D_MODEL ** -0.5),
        'a_q_gain': gain(ks[7], (DEPTH, A_DH)),
        'a_k_gain': gain(ks[8], (DEPTH, A_DH)),
        'lambda_q1': nrm(ks[9], (DEPTH, A_DH), 0.1),
        'lambda_k1': nrm(ks[10], (DEPTH, A_DH), 0.1),
        'lambda_q2': nrm(ks[11], (DEPTH, A_DH), 0.1),
        'lambda_k2': nrm(ks[12], (DEPTH, A_DH), 0.1),
        'a_out_gain': gain(ks[13], (DEPTH, A_DV)),
        'w_a2': nrm(ks[14], (DEPTH, G_RANK, G_HEADS * G_DK), G_RANK ** -0.5),
        'b_a': nrm(ks[15], (DEPTH, G_HEADS * G_DK), 0.1),
        'g_out_gain': gain(ks[16], (DEPTH, G_DV)),
        'w_out': nrm(ks[17], (DEPTH, MIX_WIDTH, D_MODEL), MIX_WIDTH ** -0.5),
        'norm2_gain': gain(ks[18], (DEPTH, D_MODEL)),
        'w_group': nrm(ks[19], (DEPTH, D_MODEL, N_GROUPS), D_MODEL ** -0.5),
        'b_group': nrm(ks[20], (DEPTH, N_GROUPS), 0.01),
        'w_erouter': nrm(ks[21], (DEPTH, D_MODEL, N_EXPERTS), D_MODEL ** -0.5),
        'b_erouter': nrm(ks[22], (DEPTH, N_EXPERTS), 0.01),
        'w_gate': nrm(ks[23], (DEPTH, N_EXPERTS, D_MODEL, D_EXPERT), D_MODEL ** -0.5),
        'w_up': nrm(ks[24], (DEPTH, N_EXPERTS, D_MODEL, D_EXPERT), D_MODEL ** -0.5),
        'w_down': nrm(ks[25], (DEPTH, N_EXPERTS, D_EXPERT, D_MODEL), D_EXPERT ** -0.5),
    }

def reference(x_prompt, x_sample, cache_k, cache_v, state_gla, norm1_gain, w_in, a_q_gain,
              a_k_gain, lambda_q1, lambda_k1, lambda_q2, lambda_k2, a_out_gain, w_a2, b_a,
              g_out_gain, w_out, norm2_gain, w_group, b_group, w_erouter, b_erouter,
              w_gate, w_up, w_down):
    y_p = x_prompt
    y_s = x_sample
    kp_l, vp_l, sp_l, ks_l, vs_l, ss_l = [], [], [], [], [], []
    for l in range(DEPTH):
        lam_init = 0.8 - 0.6 * math.exp(-0.3 * l)
        lam = diff_lambda(lambda_q1[l], lambda_k1[l], lambda_q2[l], lambda_k2[l], lam_init)
        mix_w = (w_in[l], a_q_gain[l], a_k_gain[l], lam, lam_init, a_out_gain[l], w_a2[l], b_a[l],
                 g_out_gain[l], w_out[l])
        moe_w = (w_group[l], b_group[l], w_erouter[l], b_erouter[l], w_gate[l], w_up[l], w_down[l])
        mix, kp, vp, sp = token_mixer(rms_norm(y_p, norm1_gain[l]), *mix_w)
        y_p = y_p + mix
        y_p = y_p + hier_moe(rms_norm(y_p, norm2_gain[l]), *moe_w)
        mix, kn, vn, sn = token_mixer(rms_norm(y_s, norm1_gain[l]), *mix_w,
                                      cache_k=cache_k[l], cache_v=cache_v[l], state=state_gla[l])
        y_s = y_s + mix
        y_s = y_s + hier_moe(rms_norm(y_s, norm2_gain[l]), *moe_w)
        kp_l.append(kp); vp_l.append(vp); sp_l.append(sp)
        ks_l.append(kn); vs_l.append(vn); ss_l.append(sn)
    return (y_p, y_s, jnp.stack(kp_l), jnp.stack(vp_l), jnp.stack(sp_l),
            jnp.stack(ks_l), jnp.stack(vs_l), jnp.stack(ss_l))


_drawn_inputs = setup_inputs


def setup_inputs(seed=0):
    import zlib

    import numpy as np

    out = dict(_drawn_inputs(seed))
    spreads = {}
    factors = {'a_q_gain': 2.796,
     'a_k_gain': 2.78,
     'lambda_q1': 2.744,
     'lambda_k1': 6.165,
     'b_group': 4.62,
     'b_erouter': 5.695}
    for name, (base, spread) in spreads.items():
        noise = np.random.default_rng([zlib.crc32(name.encode()), seed]).standard_normal(out[name].shape)
        drawn = base * np.exp(spread * noise) if base else spread * noise
        out[name] = __import__('jax').numpy.asarray(drawn.astype(out[name].dtype))
    for name, factor in factors.items():
        out[name] = (out[name] * factor).astype(out[name].dtype)
    return out
```

```python
from contextlib import ExitStack

import concourse.bass as bass
from concourse import mybir

F32 = mybir.dt.float32
I32 = mybir.dt.int32
U32 = mybir.dt.uint32
ALU = mybir.AluOpType
ACT = mybir.ActivationFunctionType
AX = mybir.AxisListType

P = 128
D = 1024
DC = D // P
NT = 5
NP = 4
CHUNK = 64
NB = 8
Q = 16
PAST = 512
H = 4
DH = 64
DV = 128
RANK = 16
EPS = 1e-6
LAM_INIT = 0.8 - 0.6 * 1.0
NG = 4
EPG = 8
NE = NG * EPG
FE = 256
CAP = 64
PAIRS = NE // 2
ROUNDS = NT * P // CAP
SLOTS = NE * CAP
GU_W = DC * 2 * FE
DN_W = 2 * D
EXP_W = GU_W + DN_W
CW = NT * 512
NEG = -1e30
C_G, C_GV, C_GR, C_K, C_Q, C_V = range(6)


def build(nc, x, cache_kt, cache_v, state, w_main, w_ga, w_a2b, w_out, cols, k_gain, lam, w_r, b_r,
          w_gu, w_dn, y_out, k_out, v_out, sp_out, ss_out, hn_dram, ye_dram):
    ctx = ExitStack()
    with ctx:
        def sb(name, shape, dt=F32):
            return ctx.enter_context(nc.sbuf_tensor(name, shape, dt))

        def sem(name):
            return ctx.enter_context(nc.semaphore(name))

        bank = [ctx.enter_context(nc.psum_tensor(f"bank{i}", [P, 512], F32)) for i in range(8)]

        X = sb("X", [P, NT, D])
        Zpad = sb("Zpad", [P, EXP_W - 2 * CW + 6 * CW])
        hbuf = sb("hbuf", [P, DC * NT * P])
        W = sb("W", [P, 8192])
        G = sb("G", [P, 8192])
        R0 = sb("R0", [P, EXP_W])
        Z0 = EXP_W - 2 * CW

        def z(c, i, a=0, b=512):
            o = Z0 + c * CW + i * 512
            return Zpad[:, o + a:o + b]

        def zall(c):
            return Zpad[:, Z0 + c * CW:Z0 + (c + 1) * CW]

        ident = sb("ident", [P, P])
        tri64 = sb("tri64", [P, P])
        tri16 = sb("tri16", [P, P])
        strict = sb("strict", [P, P])
        ones = sb("ones", [P, P])
        iota128 = sb("iota128", [P, P])
        iota_i = sb("iota_i", [P, P], I32)
        desc_i = sb("desc_i", [P, EPG], I32)
        desc = sb("desc", [P, EPG])
        tok_i = sb("tok_i", [P, NT], I32)
        tok = sb("tok", [P, NT])
        bmask = sb("bmask", [P, NB])
        C0 = sb("C0", [P, H * Q])
        C1 = sb("C1", [P, H * Q])
        Cm = sb("Cm", [P, H * Q])
        Cb = sb("Cb", [P, 2, H * Q])
        mA = sb("mA", [P, P])
        mB = sb("mB", [P, CHUNK])
        epsc = sb("epsc", [P, 1])
        colt = sb("colt", [P, 2 * DC + 3])
        g1, g2 = colt[:, 0:DC], colt[:, DC:2 * DC]
        qg, ag, gg = colt[:, 16:17], colt[:, 17:18], colt[:, 18:19]
        ag8 = sb("ag8", [P, 1])
        kg = sb("kg", [P, DH])
        wga = sb("wga", [P, DC, RANK])
        zga = sb("zga", [P, NT, RANK])
        wr = sb("wr", [P, DC, NG + NE])
        br = sb("br", [P, NG + NE])
        ssx = sb("ssx", [P, NT])
        stdx = sb("stdx", [P, NT])
        rx = sb("rx", [P, NT])
        sskq = sb("sskq", [P, 2, NT, 8])
        rkq = sb("rkq", [P, 2, NT, 8])
        lsum = sb("lsum", [P, 2])
        lexp = sb("lexp", [P, 2])
        nlam = sb("nlam", [P, 1])
        em = sb("em", [P, 2, 16])
        gl = sb("gl", [P, 2, 16])
        sso = sb("sso", [P, NT, 8])
        ro = sb("ro", [P, NT, 8])
        junk = sb("junk", [P, DV])
        mx = sb("mx", [P, 2, 2])
        nm = sb("nm", [P, 2, 2])
        es = sb("es", [P, 2, 2])
        ri = sb("ri", [P, 2, 2])
        ss2 = sb("ss2", [P, NT])
        st2 = sb("st2", [P, NT])
        r2 = sb("r2", [P, NT])
        ovf = sb("ovf", [P, 1], I32)
        idx = sb("idx", [P, PAIRS + 1], I32)
        slot = sb("slot", [P, 2 * NT], I32)
        wk = sb("wk", [P, 2, NT])
        cur = sb("cur", [P, 1])

        hT = hbuf[:, :].rearrange("p (c i t) -> p c i t", c=DC, i=NT)
        qT = hbuf[:, 0:H * NT * P].rearrange("p (h t) -> p h t", h=H)
        kT = hbuf[:, H * NT * P:].rearrange("p (h t) -> p h t", h=H)
        mixT = hbuf[:, :].rearrange("p (c t) -> p c t", c=DC)
        xn = [Zpad[:, Z0 + C_Q * CW + k * D:Z0 + C_Q * CW + (k + 1) * D] for k in range(2)]
        xjunk = Zpad[:, Z0 + C_V * CW:Z0 + C_V * CW + D]
        win = [W[:, k * 4096:(k + 1) * 4096].rearrange("p (c n) -> p c n", c=DC) for k in range(2)]
        kqsq = [G[:, k * 512:(k + 1) * 512] for k in range(2)]
        la = R0[:, 0:1280].rearrange("p (i n) -> p i n", i=NT)
        gz = R0[:, 1280:2560]
        gt = R0[:, 2560:3840]
        gaT = R0[:, 3840:4480]
        wa2 = R0[:, 4480:4736]
        lamv = R0[:, 4736:4992].rearrange("p (a n) -> p a n", a=4)
        lamp = R0[:, 4992:5120].rearrange("p (a n) -> p a n", a=2)
        bT = W[:, 0:1280].rearrange("p (h t) -> p h t", h=2)
        Ep = W[:, 1280:2560].rearrange("p (h t) -> p h t", h=2)
        Em = W[:, 2560:3840].rearrange("p (h t) -> p h t", h=2)
        qt = W[:, 3840:5120].rearrange("p (h t) -> p h t", h=2)
        kt = W[:, 5120:6400].rearrange("p (h t) -> p h t", h=2)
        ktok = W[:, 6400:7680].rearrange("p (i n) -> p i n", i=NT)
        St = G[:, 0:2048].rearrange("p (c h v) -> p c h v", c=8, h=2)
        S0 = G[:, 2048:4096].rearrange("p (b h v) -> p b h v", b=NB, h=2)
        Ss = G[:, 4096:6144].rearrange("p (b h v) -> p b h v", b=NB, h=2)
        kz = G[:, 6144:8192].rearrange("p (b n) -> p b n", b=NB)
        AT = R0[:, 0:2560].rearrange("p (i h e t) -> p i h e t", i=NT, h=2, e=2)
        qz = R0[:, 2560:4608].rearrange("p (h b t) -> p h b t", h=2, b=NB)
        tmpU = R0[:, 4608:4864].rearrange("p (h v) -> p h v", h=2)
        S = R0[:, 4864:5120].rearrange("p (h v) -> p h v", h=2)
        tmpS = R0[:, 5120:5632].rearrange("p (b h v) -> p b h v", b=2, h=2)
        E = [[G[:, (2 * k + m) * 512:(2 * k + m + 1) * 512] for m in range(2)] for k in range(2)]
        PT = [G[:, 2048 + k * 512:2560 + k * 512] for k in range(2)]
        DG = [[G[:, 3072 + (2 * k + m) * 128:3200 + (2 * k + m) * 128] for m in range(2)] for k in range(2)]
        enew = G[:, 3584:4608].rearrange("p (b t) -> p b t", b=NB)
        qbd = G[:, 4608:5632].rearrange("p (b h m q) -> p b h m q", b=NB, h=H, m=2)
        OT = G[:, 5632:6144]
        Kc = [W[:, k * 4096:k * 4096 + 2048].rearrange("p (h t) -> p h t", h=H) for k in range(2)]
        Vc = [W[:, k * 4096 + 2048:k * 4096 + 4096].rearrange("p (j n) -> p j n", j=4) for k in range(2)]
        wo = W[:, :].rearrange("p (c n) -> p c n", c=DC)
        hn = [G[:, 6144 + k * D:6144 + (k + 1) * D] for k in range(2)]
        GR0 = Z0 + C_GR * CW
        h2T = [Zpad[:, GR0 + k * D:GR0 + (k + 1) * D].rearrange("p (c t) -> p c t", c=DC) for k in range(2)]

        at = [GR0 + 2048]

        def tmp(n):
            at[0] += n
            assert at[0] <= GR0 + CW
            return Zpad[:, at[0] - n:at[0]]

        NL = NG + NE
        Lg = tmp(NT * NL).rearrange("p (i n) -> p i n", i=NT)
        at[0] = GR0
        gmax = tmp(NT)
        ge = tmp(NT * NG).rearrange("p (i g) -> p i g", i=NT)
        gs = tmp(NT)
        goh = tmp(NT * NG).rearrange("p (i g) -> p i g", i=NT)
        gm2 = tmp(NT)
        egs = tmp(NT * NE).rearrange("p (i g e) -> p i g e", i=NT, g=NG)
        esel = [tmp(NT * EPG).rearrange("p (i e) -> p i e", i=NT) for _ in range(2)]
        oh = [tmp(NT * EPG).rearrange("p (i e) -> p i e", i=NT) for _ in range(2)]
        mk = tmp(2 * NT).rearrange("p (k i) -> p k i", k=2)
        mk2 = tmp(NT)
        dm = tmp(NT)
        den = tmp(NT)
        M = [tmp(NT * NE).rearrange("p (i g e) -> p i g e", i=NT, g=NG) for _ in range(2)]
        Ms = tmp(NT * NE).rearrange("p (i g e) -> p i g e", i=NT, g=NG)
        rk = tmp(2 * NT).rearrange("p (k i) -> p k i", k=2)
        ek = tmp(2 * NT).rearrange("p (k i) -> p k i", k=2)
        pk = tmp(2 * NT).rearrange("p (k i) -> p k i", k=2)
        rn = tmp(2 * NT).rearrange("p (k i) -> p k i", k=2)
        loc = tmp(2 * NT).rearrange("p (k i) -> p k i", k=2)
        qk = tmp(2 * NT).rearrange("p (k i) -> p k i", k=2)
        sl = tmp(2 * NT).rearrange("p (k i) -> p k i", k=2)
        cmpr = tmp(2 * NT * 9).rearrange("p (k i j) -> p k i j", k=2, i=NT)
        mprod = tmp(NT * NE).rearrange("p (i n) -> p i n", i=NT)
        Mp = tmp(2 * NT * PAIRS).rearrange("p (k i n) -> p k i n", k=2, i=NT)
        rmask = tmp(2 * NT).rearrange("p (k i) -> p k i", k=2)
        wkr = tmp(2 * NT).rearrange("p (k i) -> p k i", k=2)
        cnt = tmp(1)
        ovf_f = tmp(1)
        assert at[0] <= GR0 + 2048
        at[0] = GR0 + 2048 + NT * NL
        Rt = tmp(2 * NT * (PAIRS + 1)).rearrange("p (k i n) -> p k i n", k=2, i=NT)
        OH0 = Z0 + C_V * CW + 1024
        OH = Zpad[:, OH0:OH0 + 1280].rearrange("p (n s) -> p n s", n=2 * NT)

        ebuf = [R0[:, :], Zpad[:, 0:EXP_W], Zpad[:, Z0 + C_K * CW:Z0 + C_K * CW + EXP_W], G[:, 0:EXP_W]]
        egu = [e[:, 0:GU_W].rearrange("p (c n) -> p c n", c=DC) for e in ebuf]
        edn = [e[:, GU_W:EXP_W].rearrange("p (f n) -> p f n", f=2) for e in ebuf]
        NXS = 2
        xs = [W[:, k * D:(k + 1) * D] for k in range(NXS)]
        xsT = [W[:, (3 + k) * D:(4 + k) * D].rearrange("p (c s) -> p c s", c=DC) for k in range(2)]
        ysb = [W[:, (5 + k) * D:(6 + k) * D] for k in range(2)]
        sil = [W[:, 7 * D + k * 128:7 * D + (k + 1) * 128] for k in range(4)]
        hTs = [W[:, 7 * D + 512 + k * 128:7 * D + 640 + k * 128].rearrange("p (f s) -> p f s", f=2)
               for k in range(4)]
        NYG = 6
        yg = [R0[:, k * D:(k + 1) * D] for k in range(NYG)]

        ld_x = [sem(f"ld_x{i}") for i in range(NT)]
        ld_cols = sem("ld_cols")
        ld_small = sem("ld_small")
        ld_win = [sem(f"ld_win{k}") for k in range(2)]
        ld_state = sem("ld_state")
        ld_k = [sem(f"ld_k{k}") for k in range(2)]
        ld_v = [sem(f"ld_v{k}") for k in range(2)]
        ld_wo = sem("ld_wo")
        ld_gu = [sem(f"ld_gu{k}") for k in range(4)]
        ld_dn = [sem(f"ld_dn{k}") for k in range(4)]
        pool_step = sem("pool_step")
        pool_seen = sem("pool_seen")
        sp_seen = sem("sp_seen")
        consts = sem("consts")
        dve_step = sem("dve_step")
        act_step = sem("act_step")
        ssq1 = sem("ssq1")
        std1 = sem("std1")
        rstd1 = sem("rstd1")
        xn_ready = sem("xn_ready")
        xT_done = sem("xT_done")
        hT_ready = sem("hT_ready")
        ga_done = sem("ga_done")
        zga_ready = sem("zga_ready")
        gaT_done = sem("gaT_done")
        gaT_ready = sem("gaT_ready")
        pre_done = sem("pre_done")
        gabs_ready = sem("gabs_ready")
        gln_ready = sem("gln_ready")
        la_ready = sem("la_ready")
        lam_mid = sem("lam_mid")
        lam_exp = sem("lam_exp")
        lam_ready = sem("lam_ready")
        proj_done = sem("proj_done")
        z_free = sem("z_free")
        kqss_ready = sem("kqss_ready")
        kqstd = sem("kqstd")
        k_ready = sem("k_ready")
        q_ready = sem("q_ready")
        b_done = sem("b_done")
        b_ready = sem("b_ready")
        dec_in = sem("dec_in")
        dec_ready = sem("dec_ready")
        at_zero = sem("at_zero")
        qkT_done = sem("qkT_done")
        qkT_ready = sem("qkT_ready")
        gT_done = sem("gT_done")
        gqk_ready = sem("gqk_ready")
        qz_ready = sem("qz_ready")
        ktok_done = sem("ktok_done")
        ktok_ready = sem("ktok_ready")
        kz_ready = sem("kz_ready")
        sc_done = sem("sc_done")
        AT_ready = sem("AT_ready")
        U_done = sem("U_done")
        U_used = sem("U_used")
        St_ready = sem("St_ready")
        Ss_ready = sem("Ss_ready")
        go_done = sem("go_done")
        go_sq = sem("go_sq")
        go_ready = sem("go_ready")
        silu_ready = sem("silu_ready")
        sp_ready = sem("sp_ready")
        ss_ready = sem("ss_ready")
        st_states = sem("st_states")
        st_kv = sem("st_kv")
        att_zero = sem("att_zero")
        s_done = sem("s_done")
        nm_ready = sem("nm_ready")
        e_ready = sem("e_ready")
        dg_ready = sem("dg_ready")
        pt_done = sem("pt_done")
        pt_ready = sem("pt_ready")
        o_done = sem("o_done")
        o_sq = sem("o_sq")
        ao_ready = sem("ao_ready")
        qbd_ready = sem("qbd_ready")
        d_s_done = sem("d_s_done")
        d_nm_ready = sem("d_nm_ready")
        d_e_ready = sem("d_e_ready")
        cb_ready = sem("cb_ready")
        d_pt_done = sem("d_pt_done")
        d_pt_ready = sem("d_pt_ready")
        d_pv_done = sem("d_pv_done")
        ot_ready = sem("ot_ready")
        ostd = sem("ostd")
        mix_ready = sem("mix_ready")
        mT_done = sem("mT_done")
        mT_a = sem("mT_a")
        mT_g = sem("mT_g")
        out_done = sem("out_done")
        x2_ready = sem("x2_ready")
        ssq2 = sem("ssq2")
        std2 = sem("std2")
        rstd2 = sem("rstd2")
        hn_ready = sem("hn_ready")
        st_hn = [sem(f"st_hn{k}") for k in range(2)]
        h2_done = sem("h2_done")
        h2_ready = sem("h2_ready")
        lg_done = sem("lg_done")
        gexp_in = sem("gexp_in")
        gexp_out = sem("gexp_out")
        m_ready = sem("m_ready")
        rank_done = sem("rank_done")
        tab_step = sem("tab_step")
        tab_in = sem("tab_in")
        tab_done = sem("tab_done")
        idx_ready = sem("idx_ready")
        ovf_ready = sem("ovf_ready")
        gath = [sem(f"gath{k}") for k in range(NXS)]
        xsT_done = sem("xsT_done")
        xsT_ready = sem("xsT_ready")
        gu_done = sem("gu_done")
        sil_ready = sem("sil_ready")
        h_ready = sem("h_ready")
        dn_done = sem("dn_done")
        ysb_ready = sem("ysb_ready")
        st_y = [sem(f"st_y{k}") for k in range(2)]
        ygath = [sem(f"ygath{k}") for k in range(NYG)]
        ysum = sem("ysum")
        st_out = sem("st_out")

        block = ctx.enter_context(nc.Block())

        def gu_rows(e):
            return w_gu[bass.ds(e * P, P), :].rearrange("p (c n) -> p c n", c=DC)

        def dn_rows(e):
            return w_dn[bass.ds(e * P, P), :].rearrange("p (f n) -> p f n", f=2)

        @block.sync
        def _(sp):
            for i in range(2):
                sp.dma_start(X[:, i, :], x[i]).then_inc(ld_x[i], 16)
            sp.dma_start(colt[:, :], cols).then_inc(ld_cols, 16)
            for i in range(2, NT):
                sp.dma_start(X[:, i, :], x[i]).then_inc(ld_x[i], 16)
            sp.dma_start(wga[:, :, :], w_ga).then_inc(ld_small, 16)
            sp.dma_start(wa2[0:RANK + 1, :], w_a2b).then_inc(ld_small, 16)
            sp.dma_start(lamv, lam.partition_broadcast(P)).then_inc(ld_small, 16)
            sp.dma_start(kg[:, :], k_gain.partition_broadcast(P)).then_inc(ld_small, 16)
            sp.dma_start(br[:, :], b_r.partition_broadcast(P)).then_inc(ld_small, 16)
            sp.dma_start(wr[:, :, :], w_r).then_inc(ld_small, 16)
            for c in range(6):
                if c >= 2:
                    sp.wait_ge(proj_done, NT * (c - 1))
                sp.dma_start(win[c % 2], w_main[c]).then_inc(ld_win[c % 2], 16)
            sp.dma_start(S0, state).then_inc(ld_state, 16)
            sp.wait_ge(go_done, NT)
            sp.wait_ge(ss_ready, 1)
            for b in range(NB):
                if b >= 2:
                    sp.wait_ge(d_s_done, b - 1)
                sp.dma_start(Kc[b % 2], cache_kt[b]).then_inc(ld_k[b % 2], 16)
                if b >= 2:
                    sp.wait_ge(d_pv_done, b - 1)
                sp.dma_start(Vc[b % 2], cache_v[b]).then_inc(ld_v[b % 2], 16)
                if b == 1:
                    sp.wait_ge(st_states, 2 * 16)
                    for e in range(2):
                        sp.dma_start(egu[e], gu_rows(e)).then_inc(ld_gu[e], 16)
                        sp.dma_start(edn[e], dn_rows(e)).then_inc(ld_dn[e], 16)
            sp.wait_ge(d_pv_done, NB)
            sp.dma_start(wo, w_out).then_inc(ld_wo, 16)
            sp.wait_ge(mT_done, 2 * NT)
            sp.wait_ge(st_kv, 2 * NT * 16)
            for e in (2, 3):
                sp.dma_start(egu[e], gu_rows(e)).then_inc(ld_gu[e], 16)
                sp.dma_start(edn[e], dn_rows(e)).then_inc(ld_dn[e], 16)

            def experts(g0, g):
                for k in range(4):
                    sp.wait_ge(dn_done, (g0 + g) * 4 + k + 1 - 4)
                    sp.dma_start(egu[k], gu_rows(g * 4 + k)).then_inc(ld_gu[k], 16)
                    sp.dma_start(edn[k], dn_rows(g * 4 + k)).then_inc(ld_dn[k], 16)

            with sp.Fori(1, NE // 4) as g:
                experts(0, g)
            sp.wait_ge(ovf_ready, 1)
            with sp.If(sp.value_load(ovf[0:1, 0:1]) > 0):
                with sp.Fori(1, ROUNDS) as r:
                    sp.wait_ge(ysum, r * 2 * NT)
                    sp.sem_inc(sp_seen, 1)
                    with sp.Fori(0, NE // 4) as g:
                        experts(r * 8, g)
                sp.wait_ge(ysum, ROUNDS * 2 * NT)
            for i in range(NT):
                sp.wait_ge(ysum, 2 * (i + 1))
                sp.dma_start(y_out[i], X[:, i, :]).then_inc(st_out, 16)
            sp.wait_ge(st_out, NT * 16)
            sp.wait_ge(st_kv, 2 * NT * 16)
            sp.wait_ge(st_states, 2 * 16)

        @block.gpsimd
        def _(pool):
            n = [0]

            def step(ins):
                n[0] += 1
                ins.then_inc(pool_step, 1)
                pool.wait_ge(pool_step, n[0])

            pool.memset(epsc[:, :], EPS)
            pool.memset(ones[:, :], 1.0)
            pool.memset(gaT[0:RANK + 1, :], 1.0)
            pool.memset(C0[:, :], 0.0)
            pool.memset(C1[:, :], 0.0)
            pool.memset(mA[:, :], 0.0)
            pool.memset(mB[:, :], NEG)
            pool.memset(strict[:, :], 1.0)
            pool.memset(bmask[:, :], 1.0)
            pool.memset(tri64[:, :], 1.0 / 16)
            step(pool.memset(ident[:, :], 0.0))
            step(pool.affine_select(out=ident[:, :], in_=ident[:, :], compare_op=ALU.not_equal, fill=1.0,
                                    base=0, pattern=[[-1, P]], channel_multiplier=1))
            step(pool.affine_select(out=tri64[:, :], in_=tri64[:, :], compare_op=ALU.is_ge, fill=0.0,
                                    base=0, pattern=[[1, P]], channel_multiplier=-1))
            t16 = tri16[:, :].rearrange("p (b t) -> p b t", b=NB)
            step(pool.affine_select(out=t16, in_=tri64[:, :].rearrange("p (b t) -> p b t", b=NB),
                                    compare_op=ALU.is_ge, fill=0.0,
                                    base=0, pattern=[[-Q, NB], [0, Q]], channel_multiplier=1))
            step(pool.memset(tri64[0:CHUNK, CHUNK:P], 0.0))
            step(pool.affine_select(out=strict[:, :], in_=strict[:, :], compare_op=ALU.is_gt, fill=0.0,
                                    base=0, pattern=[[1, P]], channel_multiplier=-1))
            step(pool.affine_select(out=bmask[:, :], in_=bmask[:, :], compare_op=ALU.is_ge, fill=0.0,
                                    base=0, pattern=[[-Q, NB]], channel_multiplier=1))
            step(pool.affine_select(out=bmask[:, :], in_=bmask[:, :], compare_op=ALU.is_ge, fill=0.0,
                                    base=Q - 1, pattern=[[Q, NB]], channel_multiplier=-1))
            for m, c in ((0, C0), (1, C1)):
                cv = c[:, :].rearrange("p (h q) -> p h q", h=H)
                step(pool.affine_select(out=cv, in_=cv, compare_op=ALU.not_equal, fill=1.0,
                                        base=-Q * m, pattern=[[-2 * Q, H], [-1, Q]], channel_multiplier=1))
            pool.memset(mA[0:1, 0:CHUNK], 1.0)
            step(pool.memset(mA[CHUNK:CHUNK + 1, 0:CHUNK], 1.0))
            pool.iota(iota_i[:, :], pattern=[[1, P]], base=0, channel_multiplier=0)
            step(pool.iota(tok_i[:, :], pattern=[[P, NT]], base=0, channel_multiplier=1))
            step(pool.iota(desc_i[:, :], pattern=[[-1, EPG]], base=EPG, channel_multiplier=0))
            pool.tensor_copy(iota128[:, :], iota_i[:, :])
            pool.tensor_copy(desc[:, :], desc_i[:, :])
            pool.memset(cur[:, :], 0.0)
            pool.tensor_copy(tok[:, :], tok_i[:, :]).then_inc(consts, 1)
            for i in range(NT):
                pool.wait_ge(k_ready, i + 1)
                pool.dma_start(k_out[i], z(C_K, i)).then_inc(st_kv, 16)
            for i in range(NT):
                pool.wait_ge(z_free, 5 + 25 + i + 1)
                pool.dma_start(v_out[i], z(C_V, i)).then_inc(st_kv, 16)
            pool.wait_ge(b_done, 1)
            pool.memset(R0[:, 0:2560], 0.0).then_inc(at_zero, 1)
            pool.memset(R0[:, 2560:4608], 0.0).then_inc(at_zero, 1)
            pool.wait_ge(sp_ready, 1)
            pool.dma_start(sp_out, S).then_inc(st_states, 16)
            pool.wait_ge(ss_ready, 1)
            pool.dma_start(ss_out, S0).then_inc(st_states, 16)
            pool.wait_ge(go_done, NT)
            pool.wait_ge(st_states, 32)
            pool.memset(G[:, 3584:4608], 0.0).then_inc(att_zero, 1)
            pool.memset(G[:, 4608:5632], 0.0).then_inc(att_zero, 1)
            for i in range(NT):
                pool.wait_ge(hn_ready, i + 1)
                pool.dma_start(hn_dram[i * P:(i + 1) * P, :], hn[i % 2]).then_inc(st_hn[i % 2], 16)
            pool.wait_ge(st_hn[0], 3 * 16)
            pool.wait_ge(st_hn[1], 2 * 16)

            def gathers(r):
                pool.wait_ge(idx_ready, r + 1)
                if not isinstance(r, int):
                    pool.sem_inc(pool_seen, 1)
                for p in range(PAIRS + 1):
                    k = p % NXS
                    if p >= NXS:
                        pool.wait_ge(xsT_done, r * 2 * (PAIRS + 1) + 2 * (p - NXS + 1))
                        if not isinstance(r, int):
                            pool.sem_inc(pool_seen, 1)
                    pool.indirect_dma_start(
                        out=xs[k], out_offset=None, in_=hn_dram,
                        in_offset=bass.IndirectOffsetOnAxis(ap=idx[:, p:p + 1], axis=0),
                    ).then_inc(gath[k], 16)

            def y_gathers(r):
                for k in range(2):
                    pool.wait_ge(st_y[k], (r + 1) * (PAIRS // 2 * 16))
                pool.wait_ge(dn_done, (r + 1) * NE)
                if not isinstance(r, int):
                    pool.sem_inc(pool_seen, 1)
                for m in range(2 * NT):
                    i, k = m // 2, m % 2
                    if m >= NYG:
                        pool.wait_ge(ysum, r * 2 * NT + m - NYG + 1)
                        if not isinstance(r, int):
                            pool.sem_inc(pool_seen, 1)
                    pool.indirect_dma_start(
                        out=yg[m % NYG], out_offset=None, in_=ye_dram,
                        in_offset=bass.IndirectOffsetOnAxis(ap=slot[:, k * NT + i:k * NT + i + 1], axis=0),
                    ).then_inc(ygath[m % NYG], 16)

            gathers(0)
            y_gathers(0)
            pool.wait_ge(ovf_ready, 1)
            with pool.If(pool.value_load(ovf[0:1, 0:1]) > 0):
                with pool.Fori(1, ROUNDS) as r:
                    pool.wait_ge(xsT_done, r * 2 * (PAIRS + 1))
                    gathers(r)
                    y_gathers(r)

        @block.scalar
        def _(act):
            n = [0]

            def step(ins):
                n[0] += 1
                ins.then_inc(act_step, 1)
                act.wait_ge(act_step, n[0])

            act.wait_ge(consts, 1)
            act.wait_ge(ld_cols, 16)

            def root(i):
                act.wait_ge(ssq1, i + 1)
                act.activation(stdx[:, i:i + 1], ssx[:, i:i + 1], ACT.Sqrt, bias=epsc[:, 0:1],
                               scale=1.0 / D).then_inc(std1, 1)

            root(0)
            for i in range(NT):
                if i + 1 < NT:
                    root(i + 1)
                act.wait_ge(rstd1, i + 1)
                if i >= 2:
                    act.wait_ge(xT_done, 2 * (i - 1))
                act.activation(xn[i % 2], X[:, i, :], ACT.Copy, scale=rx[:, i:i + 1]).then_inc(xn_ready, 1)
            act.wait_ge(lam_mid, 1)
            act.activation(lexp[:, :], lsum[:, :], ACT.Exp).then_inc(lam_exp, 1)
            act.wait_ge(gabs_ready, 1)
            step(act.activation(gt, gt, ACT.Exp))
            act.activation(gt, gt, ACT.Ln, bias=1.0).then_inc(gln_ready, 1)

            for i in range(NT):
                act.nop().then_inc(z_free, 1)
            def evac(c, n_before, i):
                act.wait_ge(proj_done, n_before + i + 1)
                o = c * CW + (Z0 + i * 512)
                act.activation(Zpad[:, bass.ds(o, 512)], bank[i][:, :], ACT.Copy).then_inc(z_free, 1)

            with act.Fori(0, 2) as g:
                for par in range(2):
                    for i in range(NT):
                        evac(2 * g + par, 10 * g + 5 * par, i)
            for i in range(NT):
                evac(4, 20, i)
            evac(5, 25, 0)
            act.wait_ge(kqss_ready, 1)
            act.activation(rkq[:, :, :, :], sskq[:, :, :, :], ACT.Sqrt, bias=epsc[:, 0:1],
                           scale=1.0 / DH).then_inc(kqstd, 1)
            for i in range(1, NT):
                evac(5, 25, i)
            act.wait_ge(b_done, 1)
            for k in range(3):
                w = 2 if k < 2 else 1
                act.activation(bT[:, :, 256 * k:256 * k + 128 * w].rearrange("p h (i t) -> p i h t", i=w),
                               bank[5 + k][:, 0:256 * w].rearrange("p (i h t) -> p i h t", i=w, h=2),
                               ACT.Copy).then_inc(b_ready, 1)
            act.wait_ge(b_ready, 3)
            act.activation(em[:, :, 0:8], bT[:, :, 0:512].rearrange("p h (c t) -> p h c t", c=8)[:, :, :, 31],
                           ACT.Exp).then_inc(dec_ready, 1)
            act.activation(em[:, :, 8:16], bT[:, :, 512:640].rearrange("p h (c t) -> p h c t", c=8)[:, :, :, 7],
                           ACT.Exp).then_inc(dec_ready, 1)
            act.wait_ge(dec_in, 2)
            act.activation(Ep, kt, ACT.Exp).then_inc(dec_ready, 1)
            act.activation(Em, kt, ACT.Exp, scale=-1.0).then_inc(dec_ready, 1)
            for m in range(2 * NT):
                act.wait_ge(qkT_done, m + 1)
                i = m % NT
                src = bank[m % 4][:, :].rearrange("p (h t) -> p h t", h=H)
                if m < NT:
                    act.activation(kT[:, :, i * P:(i + 1) * P], src, ACT.Copy).then_inc(qkT_ready, 1)
                else:
                    act.activation(qT[:, :, i * P:(i + 1) * P], src, ACT.Copy, scale=qg).then_inc(qkT_ready, 1)
            for i in range(NT):
                act.wait_ge(ktok_done, i + 1)
                act.activation(ktok[:, i, :], bank[6 + i % 2][:, 0:256], ACT.Copy).then_inc(ktok_ready, 1)
            act.wait_ge(z_free, 7 * NT)
            act.activation(zall(C_GR), zall(C_GR), ACT.Silu).then_inc(silu_ready, 1)
            for i in range(NT):
                act.wait_ge(go_done, i + 1)
                for h in range(H):
                    step(act.activation(junk[:, :], bank[2 * (i % 2) + h % 2][:, (h // 2) * P:(h // 2 + 1) * P],
                                        ACT.Square, accum_out=sso[:, i, H + h:H + h + 1]))
                act.nop().then_inc(go_sq, 1)
            items = [(i, h) for i in range(NP) for h in range(H)]
            NI = len(items)
            act.wait_ge(att_zero, 2)

            def exps(m):
                i, h = items[m]
                L = (i + 1) * P
                act.wait_ge(nm_ready, m + 1)
                if m >= 2:
                    act.wait_ge(pt_done, m - 1)
                for mm in range(2):
                    act.activation(E[m % 2][mm][:, 0:L], bank[2 * (m % 2) + mm][:, 0:L], ACT.Exp,
                                   bias=nm[:, m % 2, mm:mm + 1], scale=DH ** -0.5,
                                   accum_out=es[:, m % 2, mm:mm + 1]).then_inc(e_ready, 1)

            def pts(m):
                i, h = items[m]
                L = (i + 1) * P
                act.wait_ge(pt_done, m + 1)
                if m >= 2:
                    act.wait_ge(o_done, m - 1)
                act.activation(PT[m % 2][:, 0:L], bank[4 + m % 2][:, 0:L], ACT.Copy).then_inc(pt_ready, 1)

            def osq(i, src, done, value):
                act.wait_ge(done, value)
                for h in range(H):
                    step(act.activation(junk[:, :], src[:, h * P:(h + 1) * P], ACT.Square,
                                        accum_out=sso[:, i, h:h + 1]))
                act.nop().then_inc(o_sq, 1)

            for m in range(NI + 2):
                if m < NI:
                    exps(m)
                if 1 <= m <= NI:
                    pts(m - 1)
                if m >= 2 and (m - 2) % H == H - 1:
                    i = (m - 2) // H
                    osq(i, bank[6 + i % 2], o_done, m - 1)

            def d_exps(b):
                act.wait_ge(d_nm_ready, b + 1)
                if b >= 2:
                    act.wait_ge(d_pt_done, b - 1)
                act.activation(E[b % 2][0], bank[2 * (b % 2)][:, :], ACT.Exp, bias=nm[:, b % 2, 0:1],
                               scale=DH ** -0.5, accum_out=es[:, b % 2, 0:1]).then_inc(d_e_ready, 1)
                act.activation(enew[:, b, b * Q:(b + 1) * Q], bank[2 * (b % 2) + 1][:, 0:Q], ACT.Exp,
                               bias=nm[:, b % 2, 0:1], scale=DH ** -0.5,
                               accum_out=es[:, b % 2, 1:2]).then_inc(d_e_ready, 1)

            def d_pts(b):
                act.wait_ge(d_pt_done, b + 1)
                if b >= 2:
                    act.wait_ge(d_pv_done, b - 1)
                act.activation(PT[b % 2][:, 0:5 * H * Q], bank[4 + b % 2][:, 0:5 * H * Q],
                               ACT.Copy).then_inc(d_pt_ready, 1)

            for b in range(NB + 1):
                if b < NB:
                    d_exps(b)
                if b >= 1:
                    d_pts(b - 1)
            act.wait_ge(d_pv_done, NB)
            act.activation(OT, bank[6][:, :], ACT.Copy).then_inc(ot_ready, 1)
            osq(NP, bank[7], o_done, NI + 1)
            act.wait_ge(o_sq, NT)
            act.activation(ro[:, :, :], sso[:, :, :], ACT.Sqrt, bias=epsc[:, 0:1], scale=1.0 / DV).then_inc(ostd, 1)
            for i in range(NT):
                act.wait_ge(mT_done, 2 * i + 2)
                act.activation(mixT[:, H:2 * H, i * P:(i + 1) * P],
                               bank[2 * (i % 2) + 1][:, :].rearrange("p (c t) -> p c t", c=H),
                               ACT.Copy, scale=gg).then_inc(mT_g, 1)
            for i in range(NT):
                act.wait_ge(ssq2, i + 1)
                act.activation(st2[:, i:i + 1], ss2[:, i:i + 1], ACT.Sqrt, bias=epsc[:, 0:1],
                               scale=1.0 / D).then_inc(std2, 1)
                act.wait_ge(rstd2, i + 1)
                if i >= 2:
                    act.wait_ge(st_hn[i % 2], 16 * (i // 2))
                    act.wait_ge(h2_done, 2 * (i - 1))
                act.activation(hn[i % 2], X[:, i, :], ACT.Copy, scale=r2[:, i:i + 1]).then_inc(hn_ready, 1)
            act.wait_ge(gexp_in, 1)
            act.activation(ge, ge, ACT.Exp).then_inc(gexp_out, 1)
            act.wait_ge(gexp_in, 2)
            act.activation(dm, dm, ACT.Exp).then_inc(gexp_out, 1)

            def silu(r, g, k):
                e = g * 4 + k + r * NE
                act.wait_ge(gu_done, e + 1)
                act.activation(sil[k], bank[2 + k % 2][:, 0:128], ACT.Silu).then_inc(sil_ready, 1)

            def rows(r, g, q, first):
                act.wait_ge(dn_done, r * NE + g * 4 + 2 * q + 2)
                if not first:
                    act.wait_ge(st_y[q], (r * 8 + g) * 16)
                for hf in range(2):
                    act.activation(ysb[q][:, hf * 512:(hf + 1) * 512], bank[4 + 2 * q + hf][:, :],
                                   ACT.Copy).then_inc(ysb_ready, 1)
                act.wait_ge(ysb_ready, r * 2 * PAIRS + g * 4 + 2 * q + 2)
                act.dma_start(ye_dram[bass.ds(g * (4 * CAP) + q * P, P), :], ysb[q]).then_inc(st_y[q], 16)

            def group(r, g, first=False):
                silu(r, g, 0)
                silu(r, g, 1)
                silu(r, g, 2)
                rows(r, g, 0, first)
                silu(r, g, 3)
                rows(r, g, 1, first)

            group(0, 0, first=True)
            with act.Fori(1, NE // 4) as g:
                group(0, g)
            act.wait_ge(ovf_ready, 1)
            with act.If(act.value_load(ovf[0:1, 0:1]) > 0):
                with act.Fori(1, ROUNDS) as r:
                    act.wait_ge(ysum, r * 2 * NT)
                    with act.Fori(0, NE // 4) as g:
                        group(r, g)

        @block.vector
        def _(dve):
            n = [0]

            def step(ins):
                n[0] += 1
                ins.then_inc(dve_step, 1)
                dve.wait_ge(dve_step, n[0])

            def bc(ap, shape):
                return ap.unsqueeze(len(ap.shape)).broadcast_to(shape)

            def squares(i):
                dve.wait_ge(ld_x[i], 16)
                if i:
                    dve.wait_ge(ssq1, i)
                dve.tensor_tensor_reduce(out=xjunk, in0=X[:, i, :], in1=X[:, i, :], scale=1.0, scalar=0.0,
                                         op0=ALU.mult, op1=ALU.add, accum_out=ssx[:, i:i + 1]).then_inc(ssq1, 1)

            def hT_out(i):
                for q in range(2):
                    dve.wait_ge(xT_done, 2 * i + q + 1)
                    ins = dve.tensor_tensor(hT[:, 4 * q:4 * q + 4, i, :],
                                            bank[2 * (i % 2) + q][:, :].rearrange("p (c t) -> p c t", c=4),
                                            bc(g1[:, 4 * q:4 * q + 4], [P, 4, P]), ALU.mult)
                    ins.then_inc(hT_ready, 1)

            squares(0)
            dve.wait_ge(ld_cols, 16)
            for i in range(NT):
                if i + 1 < NT:
                    squares(i + 1)
                dve.wait_ge(std1, i + 1)
                dve.reciprocal(rx[:, i:i + 1], stdx[:, i:i + 1]).then_inc(rstd1, 1)
                if i >= 1:
                    hT_out(i - 1)
            hT_out(NT - 1)
            dve.wait_ge(ga_done, 1)
            dve.tensor_copy(zga[:, :, :], bank[5][:, 0:NT * RANK].rearrange("p (i r) -> p i r", i=NT)).then_inc(zga_ready, 1)
            dve.wait_ge(gaT_done, 1)
            dve.wait_ge(consts, 1)
            dve.tensor_copy(gaT[0:RANK, 0:512], bank[6][0:RANK, :]).then_inc(gaT_ready, 1)
            dve.tensor_copy(gaT[0:RANK, 512:640], bank[7][0:RANK, 0:128]).then_inc(gaT_ready, 1)
            dve.wait_ge(ld_small, 6 * 16)
            step(dve.tensor_tensor(lamp, lamv[:, 0:4:2, :], lamv[:, 1:4:2, :], ALU.mult))
            dve.tensor_reduce(lsum[:, :], lamp, AX.X, ALU.add).then_inc(lam_mid, 1)
            dve.wait_ge(pre_done, 1)
            dve.tensor_copy(gz[:, 0:512], bank[5][:, :])
            dve.tensor_copy(gz[:, 512:1024], bank[6][:, :])
            step(dve.tensor_copy(gz[:, 1024:1280], bank[7][:, 0:256]))
            dve.scalar_tensor_tensor(out=gt, in0=gz, scalar=-1.0, in1=gz, op0=ALU.mult, op1=ALU.min).then_inc(gabs_ready, 1)
            dve.wait_ge(gln_ready, 1)
            dve.scalar_tensor_tensor(out=la.rearrange("p i n -> p (i n)"), in0=gz, scalar=0.0, in1=gt,
                                     op0=ALU.min, op1=ALU.subtract).then_inc(la_ready, 1)
            dve.wait_ge(lam_exp, 1)
            step(dve.scalar_tensor_tensor(out=nlam[:, :], in0=lexp[:, 1:2], scalar=-LAM_INIT, in1=lexp[:, 0:1],
                                          op0=ALU.add, op1=ALU.subtract))
            dve.scalar_tensor_tensor(out=Cm[:, :], in0=C1[:, :], scalar=nlam[:, 0:1], in1=C0[:, :],
                                     op0=ALU.mult, op1=ALU.add)
            step(dve.tensor_scalar(ag8[:, :], ag, 1.0 - LAM_INIT, None, ALU.mult))
            for c, kq in ((C_K, 0), (C_Q, 1)):
                for i in range(NT):
                    dve.wait_ge(z_free, 5 + 5 * c + i + 1)
                    step(dve.tensor_tensor(kqsq[i % 2], z(c, i), z(c, i), ALU.mult))
                    step(dve.tensor_reduce(sskq[:, kq, i, :], kqsq[i % 2].rearrange("p (g d) -> p g d", g=8),
                                           AX.X, ALU.add))
            dve.nop().then_inc(kqss_ready, 1)
            dve.wait_ge(kqstd, 1)
            step(dve.reciprocal(rkq[:, :, :, :], rkq[:, :, :, :]))
            for i in range(NT):
                kv = z(C_K, i).rearrange("p (g d) -> p g d", g=8)
                step(dve.tensor_tensor(kv, kv, bc(rkq[:, 0, i, :], [P, 8, DH]), ALU.mult))
                dve.tensor_tensor(kv, kv, kg[:, :].unsqueeze(1).broadcast_to([P, 8, DH]), ALU.mult).then_inc(k_ready, 1)
            for i in range(NT):
                qv = z(C_Q, i).rearrange("p (g d) -> p g d", g=8)
                dve.tensor_tensor(qv, qv, bc(rkq[:, 1, i, :], [P, 8, DH]), ALU.mult).then_inc(q_ready, 1)
            dve.wait_ge(b_ready, 3)
            for a, L, mid in ((0, CHUNK, CHUNK // 2 - 1), (512, Q, Q // 2 - 1)):
                bv = bT[:, :, a:a + 8 * L].rearrange("p h (c t) -> p h c t", c=8)
                dv = kt[:, :, a:a + 8 * L].rearrange("p h (c t) -> p h c t", c=8)
                for hp in range(2):
                    ins = dve.tensor_tensor(dv[:, hp], bv[:, hp], bv[:, hp, :, mid:mid + 1].broadcast_to([P, 8, L]),
                                            ALU.subtract)
                ins.then_inc(dec_in, 1)
            dve.wait_ge(dec_ready, 4)
            elp = Ep[:, :, 0:512].rearrange("p h (c t) -> p h c t", c=8)[:, :, :, CHUNK - 1]
            els = Ep[:, :, 512:640].rearrange("p h (c t) -> p h c t", c=8)[:, :, :, Q - 1]
            dve.tensor_tensor(gl[:, :, 0:8], em[:, :, 0:8], elp, ALU.mult)
            step(dve.tensor_tensor(gl[:, :, 8:16], em[:, :, 8:16], els, ALU.mult))
            for i in range(NT):
                dve.wait_ge(gT_done, i + 1)
                ts = slice(i * P, (i + 1) * P)
                b4 = bank[4 + i % 2][:, :].rearrange("p (a h t) -> p a h t", a=2, h=2)
                dve.scalar_tensor_tensor(out=qt[:, :, ts], in0=b4[:, 0], scalar=DH ** -0.5, in1=Ep[:, :, ts],
                                         op0=ALU.mult, op1=ALU.mult).then_inc(gqk_ready, 1)
                dve.tensor_tensor(kt[:, :, ts], b4[:, 1], Em[:, :, ts], ALU.mult).then_inc(gqk_ready, 1)
            dve.wait_ge(gqk_ready, 2 * NT)
            dve.wait_ge(at_zero, 2)
            for hp in range(2):
                dve.tensor_copy(bass.AP(qz.tensor, qz[:, hp, 0, 0:Q].offset, [qz.ap[0], [P + Q, NB], [1, Q]]),
                                qt[:, hp, 512:640].rearrange("p (b t) -> p b t", b=NB)).then_inc(qz_ready, 1)
            dve.wait_ge(ld_state, 16)
            for hp in range(2):
                dve.tensor_tensor(Ss[:, :, hp, :], S0[:, :, hp, :], bc(em[:, hp, 8:16], [P, NB, DV]), ALU.mult).then_inc(Ss_ready, 1)
            dve.wait_ge(ktok_ready, NT)
            for b in range(NB):
                dve.tensor_scalar(kz[:, b, :], ktok[:, NP, :], bmask[:, b:b + 1], None, ALU.mult).then_inc(kz_ready, 1)

            def masked(i):
                tri = tri64 if i < NP else tri16
                for h2 in range(2):
                    dve.wait_ge(sc_done, 2 * i + h2 + 1)
                    for hp in range(2):
                        ins = dve.copy_predicated(AT[:, i, hp, h2, :], tri[:, :].bitcast(U32),
                                                  bank[2 * (i % 2) + h2][:, hp * P:(hp + 1) * P])
                    ins.then_inc(AT_ready, 1)

            def states(i):
                dve.wait_ge(U_done, i + 1)
                for j in range(2):
                    c = 2 * i + j
                    if c >= 1:
                        for hp in range(2):
                            ins = dve.tensor_scalar(St[:, c, hp, :], S[:, hp, :], em[:, hp, c:c + 1], None, ALU.mult)
                    else:
                        ins = dve.nop()
                    ins.then_inc(St_ready, 1)
                    el = Ep[:, :, c * CHUNK + CHUNK - 1:c * CHUNK + CHUNK]
                    for hp in range(2):
                        u = bank[4 + 2 * (i % 2) + j][:, hp * P:(hp + 1) * P]
                        if c == 0:
                            step(dve.tensor_scalar(S[:, hp, :], u, el[:, hp, :], None, ALU.mult))
                        else:
                            step(dve.tensor_scalar(tmpU[:, hp, :], u, el[:, hp, :], None, ALU.mult))
                            step(dve.scalar_tensor_tensor(out=S[:, hp, :], in0=S[:, hp, :], scalar=gl[:, hp, c:c + 1],
                                                          in1=tmpU[:, hp, :], op0=ALU.mult, op1=ALU.add))
                dve.nop().then_inc(U_used, 1)

            def go_out(i):
                dve.wait_ge(go_sq, i + 1)
                dve.wait_ge(silu_ready, 1)
                gv = z(C_GR, i).rearrange("p (h e v) -> p h e v", h=2, e=2)
                for h2 in range(2):
                    ins = dve.tensor_tensor(gv[:, :, h2, :], gv[:, :, h2, :],
                                            bank[2 * (i % 2) + h2][:, 0:256].rearrange("p (h v) -> p h v", h=2), ALU.mult)
                    ins.then_inc(go_ready, 1)

            for i in range(NT):
                masked(i)
                if i < NP:
                    states(i)
                else:
                    dve.nop().then_inc(sp_ready, 1)
                    for hp in range(2):
                        dve.wait_ge(Ss_ready, 2)
                        step(dve.tensor_tensor(S0[:, :, hp, :], S0[:, :, hp, :], bc(gl[:, hp, 8:16], [P, NB, DV]), ALU.mult))
                    for b2 in range(4):
                        dve.wait_ge(U_done, NP + b2 + 1)
                        for hp in range(2):
                            u = bank[4 + b2][:, :].rearrange("p (b h v) -> p b h v", b=2, h=2)[:, :, hp, :]
                            els2 = els[:, hp, 2 * b2:2 * b2 + 2]
                            step(dve.tensor_tensor(tmpS[:, :, hp, :], u, bc(els2, [P, 2, DV]), ALU.mult))
                            step(dve.tensor_tensor(S0[:, 2 * b2:2 * b2 + 2, hp, :], S0[:, 2 * b2:2 * b2 + 2, hp, :],
                                                   tmpS[:, :, hp, :], ALU.add))
                    dve.nop().then_inc(ss_ready, 1)
                go_out(i)
            items = [(i, h) for i in range(NP) for h in range(H)]
            NI = len(items)
            dve.wait_ge(att_zero, 2)

            def maxes(m):
                i, h = items[m]
                L = (i + 1) * P
                dve.wait_ge(s_done, m + 1)
                if m >= 2:
                    dve.wait_ge(e_ready, 2 * (m - 1))
                for mm in range(2):
                    ins = dve.tensor_reduce(mx[:, m % 2, mm:mm + 1], bank[2 * (m % 2) + mm][:, 0:L], AX.X, ALU.max)
                step(ins)
                dve.tensor_scalar(nm[:, m % 2, :], mx[:, m % 2, :], -DH ** -0.5, None, ALU.mult).then_inc(nm_ready, 1)

            def diags(m):
                dve.wait_ge(e_ready, 2 * m + 2)
                if m >= 2:
                    dve.wait_ge(pt_done, m - 1)
                step(dve.reciprocal(ri[:, m % 2, :], es[:, m % 2, :]))
                dve.tensor_scalar(DG[m % 2][0], ident[:, :], ri[:, m % 2, 0:1], None, ALU.mult)
                dve.tensor_scalar(DG[m % 2][1], ident[:, :], ri[:, m % 2, 1:2], nlam[:, 0:1],
                                  ALU.mult, ALU.mult).then_inc(dg_ready, 1)

            def ao_out(i, src):
                dve.wait_ge(o_sq, i + 1)
                dve.tensor_copy(z(C_Q, i), src[:, :]).then_inc(ao_ready, 1)

            for m in range(NI + 2):
                if m < NI:
                    maxes(m)
                if 1 <= m <= NI:
                    diags(m - 1)
                if m >= 2 and (m - 2) % H == H - 1:
                    i = (m - 2) // H
                    ao_out(i, bank[6 + i % 2])
            dve.wait_ge(qkT_ready, 2 * NT)
            for mm in range(2):
                for h in range(H):
                    src = qT[64 * mm:64 * mm + 64, h, 512:640].rearrange("p (b q) -> p b q", b=NB)
                    ins = dve.tensor_copy(qbd[64 * mm:64 * mm + 64, :, h, mm, :], src)
            ins.then_inc(qbd_ready, 1)

            def d_max(b):
                dve.wait_ge(d_s_done, b + 1)
                if b >= 2:
                    dve.wait_ge(d_e_ready, 2 * (b - 1))
                dve.tensor_reduce(mx[:, b % 2, 0:1], bank[2 * (b % 2)][:, :], AX.X, ALU.max)
                step(dve.tensor_reduce(mx[:, b % 2, 1:2], bank[2 * (b % 2) + 1][:, 0:Q], AX.X, ALU.max))
                dve.tensor_scalar(nm[:, b % 2, 0:1], mx[:, b % 2, 0:1], mx[:, b % 2, 1:2], -DH ** -0.5,
                                  ALU.max, ALU.mult).then_inc(d_nm_ready, 1)

            def d_comb(b):
                dve.wait_ge(d_e_ready, 2 * b + 2)
                if b >= 2:
                    dve.wait_ge(d_pt_done, b - 1)
                step(dve.tensor_tensor(ri[:, b % 2, 0:1], es[:, b % 2, 0:1], es[:, b % 2, 1:2], ALU.add))
                step(dve.reciprocal(ri[:, b % 2, 1:2], ri[:, b % 2, 0:1]))
                dve.tensor_scalar(Cb[:, b % 2, :], Cm[:, :], ri[:, b % 2, 1:2], None, ALU.mult).then_inc(cb_ready, 1)

            for b in range(NB + 1):
                if b < NB:
                    d_max(b)
                if b >= 1:
                    d_comb(b - 1)
            ao_out(NP, bank[7])
            dve.wait_ge(ostd, 1)
            dve.wait_ge(go_ready, 2 * NT)
            dve.wait_ge(ao_ready, NT)
            step(dve.reciprocal(ro[:, :, :], ro[:, :, :]))
            for i in range(NT):
                for c, a in ((C_Q, 0), (C_GR, H)):
                    v = z(c, i).rearrange("p (h v) -> p h v", h=H)
                    dve.tensor_tensor(v, v, bc(ro[:, i, a:a + H], [P, H, DV]), ALU.mult).then_inc(mix_ready, 1)
                if i >= 1:
                    dve.wait_ge(mT_done, 2 * i - 1)
                    dve.tensor_scalar(mixT[:, 0:H, (i - 1) * P:i * P],
                                      bank[2 * ((i - 1) % 2)][:, :].rearrange("p (c t) -> p c t", c=H),
                                      ag8[:, 0:1], None, ALU.mult).then_inc(mT_a, 1)
            dve.wait_ge(mT_done, 2 * NT - 1)
            dve.tensor_scalar(mixT[:, 0:H, NP * P:NT * P],
                              bank[0][:, :].rearrange("p (c t) -> p c t", c=H),
                              ag8[:, 0:1], None, ALU.mult).then_inc(mT_a, 1)

            def h2_out(i):
                for q in range(2):
                    dve.wait_ge(h2_done, 2 * i + q + 1)
                    if i >= 2:
                        dve.wait_ge(lg_done, i - 1)
                    dve.tensor_tensor(h2T[i % 2][:, 4 * q:4 * q + 4, :],
                                      bank[q][:, :].rearrange("p (c t) -> p c t", c=4),
                                      bc(g2[:, 4 * q:4 * q + 4], [P, 4, P]), ALU.mult).then_inc(h2_ready, 1)

            for i in range(NT):
                dve.wait_ge(out_done, i + 1)
                for hf in range(2):
                    ins = dve.tensor_tensor(X[:, i, hf * 512:(hf + 1) * 512], X[:, i, hf * 512:(hf + 1) * 512],
                                            bank[4 + 2 * (i % 2) + hf][:, :], ALU.add)
                    ins.then_inc(x2_ready, 1)
                dve.wait_ge(x2_ready, 2 * i + 2)
                if i >= 2:
                    dve.wait_ge(st_hn[i % 2], 16 * (i // 2))
                    dve.wait_ge(h2_done, 2 * (i - 1))
                dve.tensor_tensor_reduce(out=hn[i % 2], in0=X[:, i, :], in1=X[:, i, :], scale=1.0, scalar=0.0,
                                         op0=ALU.mult, op1=ALU.add, accum_out=ss2[:, i:i + 1]).then_inc(ssq2, 1)
                dve.wait_ge(std2, i + 1)
                dve.reciprocal(r2[:, i:i + 1], st2[:, i:i + 1]).then_inc(rstd2, 1)
                if i >= 1:
                    h2_out(i - 1)
            h2_out(NT - 1)
            dve.wait_ge(lg_done, NT)
            step(dve.tensor_tensor(Lg, bank[3][:, 0:NT * NL].rearrange("p (i n) -> p i n", i=NT),
                                   br[:, :].unsqueeze(1).broadcast_to([P, NT, NL]), ALU.add))
            gl4 = Lg[:, :, 0:NG]
            ev = Lg[:, :, NG:NL].rearrange("p i (g e) -> p i g e", g=NG)

            def first_max(val, mxout, ohout, m2, w):
                step(dve.tensor_reduce(mxout, val, AX.X, ALU.max))
                step(dve.tensor_tensor(ohout, val, bc(mxout, [P, NT, w]), ALU.is_equal))
                step(dve.tensor_tensor(ohout, ohout, desc[:, 0:w].unsqueeze(1).broadcast_to([P, NT, w]), ALU.mult))
                step(dve.tensor_reduce(m2, ohout, AX.X, ALU.max))
                step(dve.tensor_tensor(ohout, ohout, bc(m2, [P, NT, w]), ALU.is_equal))

            first_max(gl4, gmax, goh, gm2, NG)
            dve.tensor_tensor(ge, gl4, bc(gmax, [P, NT, NG]), ALU.subtract).then_inc(gexp_in, 1)
            for i in range(NT):
                ins = dve.tensor_tensor(egs[:, i], ev[:, i], bc(goh[:, i], [P, NG, EPG]), ALU.mult)
            step(ins)
            step(dve.tensor_reduce(esel[0], egs.rearrange("p i g e -> p i e g"), AX.X, ALU.add))
            first_max(esel[0], mk[:, 0], oh[0], mk2, EPG)
            step(dve.scalar_tensor_tensor(out=esel[1], in0=oh[0], scalar=NEG, in1=esel[0], op0=ALU.mult, op1=ALU.add))
            first_max(esel[1], mk[:, 1], oh[1], mk2, EPG)
            dve.tensor_tensor(dm, mk[:, 1], mk[:, 0], ALU.subtract).then_inc(gexp_in, 1)
            for k in range(2):
                for i in range(NT):
                    ins = dve.tensor_tensor(M[k][:, i], bc(goh[:, i], [P, NG, EPG]),
                                            oh[k][:, i].unsqueeze(1).broadcast_to([P, NG, EPG]), ALU.mult)
            step(ins)
            dve.tensor_tensor(Ms, M[0], M[1], ALU.add).then_inc(m_ready, 1)
            dve.wait_ge(gexp_out, 2)
            step(dve.tensor_reduce(gs, ge, AX.X, ALU.add))
            step(dve.scalar_tensor_tensor(out=den, in0=dm, scalar=1.0, in1=gs, op0=ALU.add, op1=ALU.mult))
            step(dve.reciprocal(wk[:, 0, :], den))
            step(dve.tensor_tensor(wk[:, 1, :], wk[:, 0, :], dm, ALU.mult))
            for k in range(2):
                mf = M[k].rearrange("p i g e -> p i (g e)")
                step(dve.tensor_tensor(mprod, mf, iota128[:, 0:NE].unsqueeze(1).broadcast_to([P, NT, NE]), ALU.mult))
                dve.tensor_reduce(ek[:, k], mprod, AX.X, ALU.add)
                dve.tensor_reduce(pk[:, k], mf.rearrange("p i (n e) -> p i n e", e=2)[:, :, :, 1], AX.X, ALU.add)
                step(dve.tensor_reduce(Mp[:, k], mf.rearrange("p i (n e) -> p i n e", e=2), AX.X, ALU.add))
                dve.wait_ge(rank_done, 1)
                step(dve.tensor_tensor(mprod, mf, bank[0][:, 0:NT * NE].rearrange("p (i n) -> p i n", i=NT), ALU.mult))
                step(dve.tensor_reduce(rk[:, k], mprod, AX.X, ALU.add))
            step(dve.tensor_reduce(cnt, bank[0][:, NT * NE:(NT + 1) * NE], AX.X, ALU.max))
            step(dve.tensor_scalar(ovf_f, cnt, float(CAP), None, ALU.is_gt))
            dve.tensor_copy(ovf[:, :], ovf_f).then_inc(ovf_ready, 1)
            for k in range(2):
                for j in range(1, ROUNDS):
                    ins = dve.tensor_scalar(cmpr[:, k, :, j - 1], rk[:, k], float(CAP * j), None, ALU.is_ge)
            step(ins)
            step(dve.tensor_reduce(rn, cmpr, AX.X, ALU.add))
            step(dve.scalar_tensor_tensor(out=loc, in0=rn, scalar=-float(CAP), in1=rk, op0=ALU.mult, op1=ALU.add))
            dve.scalar_tensor_tensor(out=qk, in0=pk, scalar=float(CAP), in1=loc, op0=ALU.mult, op1=ALU.add)
            step(dve.scalar_tensor_tensor(out=sl, in0=ek, scalar=float(CAP), in1=loc, op0=ALU.mult, op1=ALU.add))
            for k in range(2):
                for i in range(NT):
                    dve.tensor_scalar(OH[:, k * NT + i, :], iota128[:, :], qk[:, k, i:i + 1], None, ALU.is_equal)
                step(dve.tensor_tensor(Mp[:, k], Mp[:, k], bc(tok[:, :], [P, NT, PAIRS]), ALU.mult))
            step(dve.memset(Rt, 0.0))
            TS = 3

            def tables(r, later):
                def tstep(k, ins):
                    ins.then_inc(tab_step, 1)
                    dve.wait_ge(tab_step, r * TS + k)
                tstep(1, dve.tensor_scalar(rmask, rn, cur[:, 0:1], None, ALU.is_equal))
                tstep(2, dve.tensor_scalar(cur[:, :], cur[:, :], 1.0, None, ALU.add))
                for k in range(2):
                    ins = dve.tensor_tensor(Rt[:, k, :, 0:PAIRS], Mp[:, k], bc(rmask[:, k], [P, NT, PAIRS]), ALU.mult)
                dve.tensor_tensor(wkr, wk[:, :, :], rmask, ALU.mult)
                dve.tensor_tensor(slot[:, :].rearrange("p (k i) -> p k i", k=2), sl, rmask, ALU.mult)
                tstep(3, ins)
                dve.nop().then_inc(tab_in, 1)
                dve.wait_ge(tab_done, r + 1)
                dve.tensor_copy(idx[:, :], bank[0][:, 0:PAIRS + 1]).then_inc(idx_ready, 1)

            def xsT_out(r, p, q):
                for hf in range(2):
                    dve.wait_ge(xsT_done, r * 2 * (PAIRS + 1) + 2 * p + hf + 1)
                    dve.tensor_tensor(xsT[q][:, 4 * hf:4 * hf + 4, :],
                                      bank[hf][:, :].rearrange("p (c s) -> p c s", c=4),
                                      bc(g2[:, 4 * hf:4 * hf + 4], [P, 4, P]), ALU.mult).then_inc(xsT_ready, 1)

            def gated(r, g, k):
                e = r * NE + g * 4 + k
                dve.wait_ge(sil_ready, e + 1)
                dve.tensor_tensor(hTs[k].rearrange("p f s -> p (f s)"), sil[k], bank[2 + k % 2][:, 128:256],
                                  ALU.mult).then_inc(h_ready, 1)

            def group(r, g):
                gated(r, g, 0)
                gated(r, g, 1)
                xsT_out(r, 2 * g + 1, 1)
                gated(r, g, 2)
                gated(r, g, 3)
                xsT_out(r, 2 * g + 2, 0)

            def moe(r, later):
                tables(r, later)
                xsT_out(r, 0, 0)
                with dve.Fori(0, NE // 4) as g:
                    group(r, g)
                for m in range(2 * NT):
                    i, k = m // 2, m % 2
                    fills = (2 * NT - m % NYG + NYG - 1) // NYG
                    dve.wait_ge(ygath[m % NYG], (r * fills + m // NYG + 1) * 16)
                    dve.wait_ge(ysum, r * 2 * NT + m)
                    dve.scalar_tensor_tensor(out=X[:, i, :], in0=yg[m % NYG], scalar=wkr[:, k, i:i + 1],
                                             in1=X[:, i, :], op0=ALU.mult, op1=ALU.add).then_inc(ysum, 1)
                dve.wait_ge(ysum, (r + 1) * 2 * NT)

            moe(0, False)
            dve.wait_ge(ovf_ready, 1)
            with dve.If(dve.value_load(ovf[0:1, 0:1]) > 0):
                with dve.Fori(1, ROUNDS) as r:
                    moe(r, True)

        @block.tensor
        def _(pe):
            pe.wait_ge(consts, 1)

            def ga(i):
                pe.wait_ge(hT_ready, 2 * i + 2)
                for c in range(DC):
                    ins = pe.matmul(bank[5][:, i * RANK:(i + 1) * RANK], hT[:, c, i, :], wga[:, c, :],
                                    start=(c == 0), stop=(c == DC - 1))
                return ins

            for i in range(NT):
                pe.wait_ge(xn_ready, i + 1)
                if i >= 2:
                    pe.wait_ge(hT_ready, 2 * (i - 1))
                for q in range(2):
                    for c in range(4):
                        ins = pe.transpose(bank[2 * (i % 2) + q][:, c * P:(c + 1) * P],
                                           xn[i % 2][:, (4 * q + c) * P:(4 * q + c + 1) * P], ident[:, :])
                    ins.then_inc(xT_done, 1)
                if i == 0:
                    pe.wait_ge(ld_small, 6 * 16)
                if i >= 1:
                    ga(i - 1)
            ga(NT - 1).then_inc(ga_done, 1)
            pe.wait_ge(zga_ready, 1)
            for i in range(NT):
                dst = bank[6][0:RANK, i * P:(i + 1) * P] if i < 4 else bank[7][0:RANK, 0:P]
                ins = pe.transpose(dst, zga[:, i, :], ident[:, :])
            ins.then_inc(gaT_done, 1)
            pe.wait_ge(gaT_ready, 2)
            for i in range(NT):
                ins = pe.matmul(bank[5 + i // 2][:, (i % 2) * 256:(i % 2) * 256 + 256],
                                gaT[0:RANK + 1, i * P:(i + 1) * P], wa2[0:RANK + 1, :], start=True, stop=True)
            ins.then_inc(pre_done, 1)

            with pe.Fori(0, 3) as g:
                for par in range(2):
                    pe.wait_ge(ld_win[par], (g + 1) * 16)
                    for i in range(NT):
                        pe.wait_ge(z_free, 10 * g + 5 * par + i + 1)
                        for c in range(DC):
                            ins = pe.matmul(bank[i][:, :], hT[:, c, i, :], win[par][:, c, :],
                                            start=(c == 0), stop=(c == DC - 1))
                        ins.then_inc(proj_done, 1)

            pe.wait_ge(la_ready, 1)
            for i in range(NT):
                for hp in range(2):
                    o = (i % 2) * 256 + hp * P
                    ins = pe.matmul(bank[5 + i // 2][:, o:o + P], la[:, i, hp * P:(hp + 1) * P],
                                    (tri64 if i < NP else tri16)[:, :], start=True, stop=True)
            ins.then_inc(b_done, 1)
            for m in range(2 * NT):
                i = m % NT
                if m < NT:
                    pe.wait_ge(k_ready, i + 1)
                else:
                    pe.wait_ge(q_ready, i + 1)
                if m < 4:
                    pe.wait_ge(z_free, 5 + 25 + m + 1)
                else:
                    pe.wait_ge(qkT_ready, m - 3)
                for h in range(H):
                    ins = pe.transpose(bank[m % 4][:, h * P:(h + 1) * P],
                                       z(C_K if m < NT else C_Q, i, h * P, (h + 1) * P), ident[:, :])
                ins.then_inc(qkT_done, 1)

            def g_tr(i):
                if i == 0:
                    pe.wait_ge(z_free, 5 + 30)
                    pe.wait_ge(b_ready, 3)
                if i >= 2:
                    pe.wait_ge(gqk_ready, 2 * (i - 1))
                for t in range(4):
                    ins = pe.transpose(bank[4 + i % 2][:, t * P:(t + 1) * P], z(C_G, i, t * P, (t + 1) * P), ident[:, :])
                ins.then_inc(gT_done, 1)

            def ktok_tr(i):
                pe.wait_ge(gqk_ready, 2 * i + 2)
                if i >= 2:
                    pe.wait_ge(ktok_ready, i - 1)
                for hp in range(2):
                    ins = pe.transpose(bank[6 + i % 2][:, hp * P:(hp + 1) * P], kt[:, hp, i * P:(i + 1) * P], ident[:, :])
                ins.then_inc(ktok_done, 1)

            g_tr(0)
            for i in range(NT):
                if i + 1 < NT:
                    g_tr(i + 1)
                ktok_tr(i)

            def scores(i):
                if i < 2:
                    pe.wait_ge(qkT_ready, 2 * NT)
                else:
                    pe.wait_ge(go_sq, i - 1)
                    pe.wait_ge(go_ready, 2 * (i - 1))
                for h2 in range(2):
                    rows = slice(64 * h2, 64 * h2 + 64)
                    for hp in range(2):
                        ins = pe.matmul(bank[2 * (i % 2) + h2][:, hp * P:(hp + 1) * P], kt[rows, hp, i * P:(i + 1) * P],
                                        qt[rows, hp, i * P:(i + 1) * P], start=True, stop=True)
                    ins.then_inc(sc_done, 1)

            def updates(i):
                pe.wait_ge(ktok_ready, NT)
                if i >= 2:
                    pe.wait_ge(U_used, i - 1)
                for j in range(2):
                    rows = slice(64 * j, 64 * j + 64)
                    for hp in range(2):
                        for h2 in range(2):
                            o = hp * P + 64 * h2
                            ins = pe.matmul(bank[4 + 2 * (i % 2) + j][64 * h2:64 * h2 + 64, hp * P:(hp + 1) * P],
                                            ktok[rows, i, o:o + 64],
                                            z(C_GV, i)[rows, (2 * hp + h2) * P:(2 * hp + h2 + 1) * P],
                                            start=True, stop=True)
                ins.then_inc(U_done, 1)

            def s_updates(b2):
                pe.wait_ge(kz_ready, NB)
                if b2 == 0:
                    pe.wait_ge(U_used, NP)
                for b in (2 * b2, 2 * b2 + 1):
                    for hp in range(2):
                        for h2 in range(2):
                            o = hp * P + 64 * h2
                            c = (b % 2) * 256 + hp * P
                            ins = pe.matmul(bank[4 + b2][64 * h2:64 * h2 + 64, c:c + P], kz[:, b, o:o + 64],
                                            z(C_GV, NP, (2 * hp + h2) * P, (2 * hp + h2 + 1) * P), start=True, stop=True)
                ins.then_inc(U_done, 1)

            def outputs(i):
                pe.wait_ge(AT_ready, 2 * i + 2)
                if i < NP:
                    pe.wait_ge(St_ready, 2 * i + 2)
                else:
                    pe.wait_ge(Ss_ready, 2)
                    pe.wait_ge(qz_ready, 2)
                for h2 in range(2):
                    rows = slice(64 * h2, 64 * h2 + 64)
                    for hp in range(2):
                        o = bank[2 * (i % 2) + h2]
                        v = slice(hp * P, (hp + 1) * P)
                        h = 2 * hp + h2
                        pe.matmul(o[:, v], AT[:, i, hp, h2, :], z(C_GV, i, h * P, (h + 1) * P), start=True, stop=False,
                                  skip_group_check=True)
                        if i < NP:
                            for j in range(2):
                                if 2 * i + j:
                                    t = i * P + j * CHUNK
                                    ins = pe.matmul(o[64 * j:64 * j + 64, v], qt[rows, hp, t:t + CHUNK],
                                                    St[rows, 2 * i + j, hp, :], start=False, stop=True,
                                                    skip_group_check=True)
                        else:
                            for b in range(NB):
                                ins = pe.matmul(o[:, v], qz[rows, hp, b, :], Ss[rows, b, hp, :], start=False,
                                                stop=(b == NB - 1), skip_group_check=True)
                ins.then_inc(go_done, 1)

            for i in range(NT):
                scores(i)
                if i < NP:
                    updates(i)
                else:
                    for b2 in range(4):
                        s_updates(b2)
                outputs(i)

            items = [(i, h) for i in range(NP) for h in range(H)]
            NI = len(items)

            def att_scores(m):
                i, h = items[m]
                L = (i + 1) * P
                if m < 2:
                    pe.wait_ge(go_sq, NT)
                    pe.wait_ge(go_ready, 2 * NT)
                else:
                    pe.wait_ge(e_ready, 2 * (m - 1))
                for mm in range(2):
                    rows = slice(64 * mm, 64 * mm + 64)
                    o = bank[2 * (m % 2) + mm]
                    pe.matmul(o[:, 0:L], qT[rows, h, i * P:(i + 1) * P], kT[rows, h, 0:L], start=True, stop=False,
                              skip_group_check=True)
                    ins = pe.matmul(o[:, L - CHUNK:L], mA[rows, :], mB[rows, :], start=False, stop=True,
                                    skip_group_check=True)
                ins.then_inc(s_done, 1)

            def att_pt(m):
                i, h = items[m]
                pe.wait_ge(dg_ready, m + 1)
                if m >= 2:
                    pe.wait_ge(pt_ready, m - 1)
                else:
                    pe.wait_ge(ss_ready, 1)
                for j in range(i + 1):
                    for mm in range(2):
                        ins = pe.matmul(bank[4 + m % 2][:, j * P:(j + 1) * P], E[m % 2][mm][:, j * P:(j + 1) * P],
                                        DG[m % 2][mm], start=(mm == 0), stop=(mm == 1))
                ins.then_inc(pt_done, 1)

            def att_pv(m):
                i, h = items[m]
                pe.wait_ge(pt_ready, m + 1)
                if h == 0 and i >= 2:
                    pe.wait_ge(o_sq, i - 1)
                    pe.wait_ge(ao_ready, i - 1)
                for j in range(i + 1):
                    ins = pe.matmul(bank[6 + i % 2][:, h * P:(h + 1) * P], PT[m % 2][:, j * P:(j + 1) * P],
                                    z(C_V, j, h * P, (h + 1) * P), start=(j == 0), stop=(j == i))
                ins.then_inc(o_done, 1)

            for m in range(NI + 2):
                if m < NI:
                    att_scores(m)
                if 1 <= m <= NI:
                    att_pt(m - 1)
                if m >= 2:
                    att_pv(m - 2)

            def d_scores(b):
                pe.wait_ge(ld_k[b % 2], 16 * (b // 2 + 1))
                if b < 2:
                    pe.wait_ge(e_ready, 2 * NI)
                    pe.wait_ge(qbd_ready, 1)
                else:
                    pe.wait_ge(d_e_ready, 2 * (b - 1))
                for h in range(H):
                    w = qbd[:, b, h, :, :].rearrange("p m q -> p (m q)")
                    pe.matmul(bank[2 * (b % 2)][32 * h:32 * h + 32, :], w, Kc[b % 2][:, h, :], start=True, stop=True,
                              tile_position=(0, 32 * h))
                    ins = pe.matmul(bank[2 * (b % 2) + 1][32 * h:32 * h + 32, 0:Q], w,
                                    kT[:, h, 512 + b * Q:512 + (b + 1) * Q], start=True, stop=True,
                                    tile_position=(0, 32 * h))
                ins.then_inc(d_s_done, 1)

            def d_pt(b):
                pe.wait_ge(cb_ready, b + 1)
                if b >= 2:
                    pe.wait_ge(d_pt_ready, b - 1)
                else:
                    pe.wait_ge(pt_ready, NI)
                for j in range(5):
                    lhs = E[b % 2][0][:, j * P:(j + 1) * P] if j < 4 else enew[:, b, :]
                    ins = pe.matmul(bank[4 + b % 2][:, j * 64:(j + 1) * 64], lhs, Cb[:, b % 2, :], start=True, stop=True)
                ins.then_inc(d_pt_done, 1)

            def d_pv(b):
                pe.wait_ge(d_pt_ready, b + 1)
                pe.wait_ge(ld_v[b % 2], 16 * (b // 2 + 1))
                if b == 0:
                    pe.wait_ge(o_sq, NP)
                    pe.wait_ge(ao_ready, NP)
                for h in range(H):
                    for j in range(5):
                        lhs = Vc[b % 2][:, j, h * P:(h + 1) * P] if j < 4 else z(C_V, NP, h * P, (h + 1) * P)
                        o = j * 64 + h * Q
                        ins = pe.matmul(bank[6][:, h * P + b * Q:h * P + (b + 1) * Q], lhs, PT[b % 2][:, o:o + Q],
                                        start=(j == 0), stop=(j == 4))
                ins.then_inc(d_pv_done, 1)

            for b in range(NB + 2):
                if b < NB:
                    d_scores(b)
                if 1 <= b <= NB:
                    d_pt(b - 1)
                if b >= 2:
                    d_pv(b - 2)
            pe.wait_ge(ot_ready, 1)
            for h in range(H):
                ins = pe.transpose(bank[7][:, h * P:(h + 1) * P], OT[:, h * P:(h + 1) * P], ident[:, :])
            ins.then_inc(o_done, 1)

            for i in range(NT):
                for q, c in ((0, C_Q), (1, C_GR)):
                    pe.wait_ge(mix_ready, 2 * i + q + 1)
                    if i >= 2:
                        pe.wait_ge(mT_a, i - 1)
                        pe.wait_ge(mT_g, i - 1)
                    for h in range(H):
                        ins = pe.transpose(bank[2 * (i % 2) + q][:, h * P:(h + 1) * P], z(c, i, h * P, (h + 1) * P),
                                           ident[:, :])
                    ins.then_inc(mT_done, 1)
            pe.wait_ge(ld_wo, 16)

            def out_proj(i):
                pe.wait_ge(mT_a, i + 1)
                pe.wait_ge(mT_g, i + 1)
                if i >= 2:
                    pe.wait_ge(x2_ready, 2 * (i - 1))
                for hf in range(2):
                    for c in range(DC):
                        ins = pe.matmul(bank[4 + 2 * (i % 2) + hf][:, :], mixT[:, c, i * P:(i + 1) * P],
                                        wo[:, c, hf * 512:(hf + 1) * 512], start=(c == 0), stop=(c == DC - 1))
                ins.then_inc(out_done, 1)

            def h2_tr(i):
                pe.wait_ge(hn_ready, i + 1)
                if i == 0:
                    pe.wait_ge(mT_a, NT)
                    pe.wait_ge(mT_g, NT)
                for q in range(2):
                    if i >= 1:
                        pe.wait_ge(h2_ready, 2 * (i - 1) + q + 1)
                    for c in range(4):
                        ins = pe.transpose(bank[q][:, c * P:(c + 1) * P], hn[i % 2][:, (4 * q + c) * P:(4 * q + c + 1) * P],
                                           ident[:, :])
                    ins.then_inc(h2_done, 1)

            def router(i):
                pe.wait_ge(h2_ready, 2 * i + 2)
                for c in range(DC):
                    ins = pe.matmul(bank[3][:, i * NL:(i + 1) * NL], h2T[i % 2][:, c, :], wr[:, c, :],
                                    start=(c == 0), stop=(c == DC - 1))
                ins.then_inc(lg_done, 1)

            out_proj(0)
            for i in range(NT):
                if i + 1 < NT:
                    out_proj(i + 1)
                h2_tr(i)
                if i >= 1:
                    router(i - 1)
            router(NT - 1)
            pe.wait_ge(m_ready, 1)
            for i in range(NT):
                for j in range(i + 1):
                    pe.matmul(bank[0][:, i * NE:(i + 1) * NE], ones[:, :] if j < i else strict[:, :],
                              Ms[:, j].rearrange("p g e -> p (g e)"), start=(j == 0), stop=(j == i))
            for j in range(NT):
                ins = pe.matmul(bank[0][:, NT * NE:(NT + 1) * NE], ones[:, :], Ms[:, j].rearrange("p g e -> p (g e)"),
                                start=(j == 0), stop=(j == NT - 1))
            ins.then_inc(rank_done, 1)

            def tables(r):
                pe.wait_ge(tab_in, r + 1)
                for m in range(2 * NT):
                    ins = pe.matmul(bank[0][:, 0:PAIRS + 1], OH[:, m, :], Rt[:, m // NT, m % NT, :], start=(m == 0),
                                    stop=(m == 2 * NT - 1))
                ins.then_inc(tab_done, 1)

            def xs_tr(r, p, q, half_p):
                pe.wait_ge(gath[q], (r * (PAIRS // 2 + 1 - q) + half_p + 1) * 16)
                for hf in range(2):
                    if not (isinstance(p, int) and isinstance(r, int) and p == 0 and r == 0):
                        pe.wait_ge(xsT_ready, (r * (PAIRS + 1) + p) * 2 + hf - 1)
                    for c in range(4):
                        ins = pe.transpose(bank[hf][:, c * P:(c + 1) * P],
                                           xs[q][:, (4 * hf + c) * P:(4 * hf + c + 1) * P], ident[:, :])
                    ins.then_inc(xsT_done, 1)

            def gate_up(r, g, k):
                q, j = k // 2, k % 2
                pe.wait_ge(ld_gu[k], (r * 8 + g + 1) * 16)
                if j == 0:
                    pe.wait_ge(xsT_ready, (r * (PAIRS + 1) + 2 * g + q + 1) * 2)
                for t in range(4):
                    for c in range(DC):
                        ins = pe.matmul(bank[2 + k % 2][:, t * CAP:(t + 1) * CAP], egu[k][:, c, t * P:(t + 1) * P],
                                        xsT[q][:, c, j * CAP:(j + 1) * CAP], start=(c == 0), stop=(c == DC - 1))
                ins.then_inc(gu_done, 1)

            def down_proj(r, g, k, first):
                q, j = k // 2, k % 2
                pe.wait_ge(h_ready, r * NE + g * 4 + k + 1)
                pe.wait_ge(ld_dn[k], (r * 8 + g + 1) * 16)
                if j == 0 and not first:
                    pe.wait_ge(ysb_ready, r * 2 * PAIRS + g * 4 + 2 * q - 2)
                for hf in range(2):
                    for f in range(2):
                        ins = pe.matmul(bank[4 + 2 * q + hf][CAP * j:CAP * j + CAP, :], hTs[k][:, f, :],
                                        edn[k][:, f, hf * 512:(hf + 1) * 512], start=(f == 0), stop=(f == 1),
                                        tile_position=(0, CAP * j))
                ins.then_inc(dn_done, 1)

            def group(r, g, first=False):
                gate_up(r, g, 0)
                gate_up(r, g, 1)
                xs_tr(r, 2 * g + 1, 1, g)
                down_proj(r, g, 0, first)
                gate_up(r, g, 2)
                down_proj(r, g, 1, first)
                gate_up(r, g, 3)
                xs_tr(r, 2 * g + 2, 0, g + 1)
                down_proj(r, g, 2, first)
                down_proj(r, g, 3, first)

            tables(0)
            xs_tr(0, 0, 0, 0)
            group(0, 0, first=True)
            with pe.Fori(1, NE // 4) as g:
                group(0, g)
            pe.wait_ge(ovf_ready, 1)
            with pe.If(pe.value_load(ovf[0:1, 0:1]) > 0):
                with pe.Fori(1, ROUNDS) as r:
                    tables(r)
                    xs_tr(r, 0, 0, 0)
                    with pe.Fori(0, NE // 4) as g:
                        group(r, g)


_OUTS = [("y_out", (NT, P, D)), ("k_out", (NT, P, 512)), ("v_out", (NT, P, 512)),
         ("sp_out", (P, 2, DV)), ("ss_out", (P, NB, 2, DV))]


def kernel(x_prompt, x_sample, cache_k, cache_v, state_gla, norm1_gain, w_in, a_q_gain, a_k_gain,
           lambda_q1, lambda_k1, lambda_q2, lambda_k2, a_out_gain, w_a2, b_a, g_out_gain, w_out,
           norm2_gain, w_group, b_group, w_erouter, b_erouter, w_gate, w_up, w_down):
    import numpy as np
    import concourse.bacc as bacc
    from concourse.bass_utils import run_bass_kernel_spmd

    def rows(w):
        return w.reshape(-1, P, w.shape[-1]).transpose(1, 0, 2)

    wi = np.asarray(w_in)[0]
    cuts = np.cumsum([512, 512, 512, 256, 256, 512, RANK])
    aq, ak, av, gq, gk, gv, ga, gr = np.split(wi, cuts, axis=1)
    chunks = [np.concatenate([gq, gk], 1), gv, gr, ak, aq, av]
    x = np.concatenate([np.asarray(x_prompt).reshape(-1, D), np.asarray(x_sample).reshape(-1, D)]).reshape(NT, P, D)
    gains = [np.asarray(norm1_gain)[0].reshape(DC, P).T, np.asarray(norm2_gain)[0].reshape(DC, P).T,
             np.concatenate([np.asarray(a_q_gain)[0]] * 2)[:, None],
             np.asarray(a_out_gain)[0][:, None], np.asarray(g_out_gain)[0][:, None]]
    wg, wu, wd = np.asarray(w_gate)[0], np.asarray(w_up)[0], np.asarray(w_down)[0]
    gu = np.concatenate([wg, wu], 2).reshape(NE, DC, P, 2 * FE).transpose(0, 2, 1, 3)
    ins = {
        "x": x,
        "cache_kt": np.asarray(cache_k)[0].transpose(0, 3, 4, 2, 1).reshape(NB, P, H, PAST),
        "cache_v": np.asarray(cache_v)[0].reshape(NB, 4, P, 512).transpose(0, 2, 1, 3),
        "state": np.asarray(state_gla)[0].reshape(NB, 2, P, DV).transpose(2, 0, 1, 3),
        "w_main": np.stack([rows(c) for c in chunks]),
        "w_ga": rows(ga),
        "w_a2b": np.concatenate([np.asarray(w_a2)[0], np.asarray(b_a)], 0),
        "w_out": rows(np.asarray(w_out)[0]),
        "cols": np.concatenate(gains, 1),
        "k_gain": np.asarray(a_k_gain)[0],
        "lam": np.stack([np.asarray(v)[0] for v in (lambda_q1, lambda_k1, lambda_q2, lambda_k2)]),
        "w_r": rows(np.concatenate([np.asarray(w_group)[0], np.asarray(w_erouter)[0]], 1)),
        "b_r": np.concatenate([np.asarray(b_group)[0], np.asarray(b_erouter)[0]]),
        "w_gu": gu.reshape(NE * P, GU_W),
        "w_dn": wd.reshape(NE, 2, P, D).transpose(0, 2, 1, 3).reshape(NE * P, DN_W),
    }
    ck = np.asarray(cache_k)[0]
    ins["cache_kt"] = ck.transpose(0, 3, 4, 2, 1).reshape(NB, P, H, PAST)
    nc = bacc.Bacc("TRN2", target_bir_lowering=False, num_devices=1)
    arrays, args = {}, []
    for name, a in ins.items():
        a = np.ascontiguousarray(a)
        arrays[f"in_{name}"] = a
        args.append(nc.dram_tensor(f"in_{name}", a.shape, F32, kind="ExternalInput").ap())
    for name, shape in _OUTS:
        args.append(nc.dram_tensor(name, shape, F32, kind="ExternalOutput").ap())
    args.append(nc.dram_tensor("hn_dram", (NT * P, D), F32, kind="Internal").ap())
    args.append(nc.dram_tensor("ye_dram", (SLOTS, D), F32, kind="Internal").ap())
    build(nc, *args)
    r = run_bass_kernel_spmd(nc, [arrays], core_ids=[0]).results[0]
    y, k, v, s1, s2 = (r[name] for name, _ in _OUTS)
    y, k, v = y.reshape(NT * P, D), k.reshape(NT * P, 512), v.reshape(NT * P, 512)
    n = NP * P
    return (y[:n].reshape(1, n, D), y[n:].reshape(NB, Q, D),
            k[:n].reshape(1, 1, n, H, 2, DH), v[:n].reshape(1, 1, n, H, DV),
            s1.reshape(2, DH, 2, DV).transpose(2, 0, 1, 3).reshape(1, 1, H, DH, DV),
            k[n:].reshape(1, NB, Q, H, 2, DH), v[n:].reshape(1, NB, Q, H, DV),
            s2.reshape(2, DH, NB, 2, DV).transpose(2, 3, 0, 1, 4).reshape(1, NB, H, DH, DV))
```

```python
from contextlib import ExitStack

import concourse.bass as bass
from concourse import mybir

F32 = mybir.dt.float32
F32R = mybir.dt.float32r
I32 = mybir.dt.int32
U32 = mybir.dt.uint32
ALU = mybir.AluOpType
ACT = mybir.ActivationFunctionType
AX = mybir.AxisListType

P = 128
D = 1024
DC = D // P
NT = 5
NP = 4
CHUNK = 64
NB = 8
Q = 16
PAST = 512
H = 4
DH = 64
DV = 128
RANK = 16
EPS = 1e-6
LAM_INIT = 0.8 - 0.6 * 1.0
NG = 4
EPG = 8
NE = NG * EPG
FE = 256
CAP = 64
PAIRS = NE // 2
ROUNDS = NT * P // CAP
SLOTS = NE * CAP
GU_W = DC * 2 * FE
DN_W = 2 * D
EXP_W = GU_W + DN_W
CW = NT * 512
NEG = -1e30
C_G, C_GV, C_GR, C_K, C_Q, C_V = range(6)


def build(nc, x, cache_kt, cache_v, state, w_main, w_ga, w_a2b, w_out, cols, k_gain, lam, w_r, b_r,
          w_gu, w_dn, y_out, k_out, v_out, sp_out, ss_out, hn_dram, ye_dram):
    ctx = ExitStack()
    with ctx:
        def sb(name, shape, dt=F32):
            return ctx.enter_context(nc.sbuf_tensor(name, shape, dt))

        def sem(name):
            return ctx.enter_context(nc.semaphore(name))

        bank = [ctx.enter_context(nc.psum_tensor(f"bank{i}", [P, 512], F32)) for i in range(8)]

        X = sb("X", [P, NT, D])
        Zpad = sb("Zpad", [P, EXP_W - 2 * CW + 6 * CW])
        def overlay(name, words):
            with nc.sbuf_tensor(f"{name}_r", [P, words], F32R) as r:
                pass
            return r, sb(name, [P, words])

        hbuf_r, hbuf = overlay("hbuf", DC * NT * P)
        W_r, W = overlay("W", 8192)
        G_r, G = overlay("G", 8192)
        R0 = sb("R0", [P, EXP_W])
        Z0 = EXP_W - 2 * CW

        def z(c, i, a=0, b=512):
            o = Z0 + c * CW + i * 512
            return Zpad[:, o + a:o + b]

        def zall(c):
            return Zpad[:, Z0 + c * CW:Z0 + (c + 1) * CW]

        ident = sb("ident", [P, P])
        tri64 = sb("tri64", [P, P])
        tri16 = sb("tri16", [P, P])
        strict = sb("strict", [P, P])
        ones = sb("ones", [P, P])
        iota128 = sb("iota128", [P, P])
        iota_i = sb("iota_i", [P, P], I32)
        desc_i = sb("desc_i", [P, EPG], I32)
        desc = sb("desc", [P, EPG])
        thr = sb("thr", [P, ROUNDS - 1])
        tok_i = sb("tok_i", [P, NT], I32)
        tok = sb("tok", [P, NT])
        bmask = sb("bmask", [P, NB])
        C0 = sb("C0", [P, H * Q])
        C1 = sb("C1", [P, H * Q])
        Cm = sb("Cm", [P, H * Q])
        Cb = sb("Cb", [P, 2, P])
        mA = sb("mA", [P, P])
        mB = sb("mB", [P, CHUNK])
        epsc = sb("epsc", [P, 1])
        colt = sb("colt", [P, 2 * DC + 3])
        g1, g2 = colt[:, 0:DC], colt[:, DC:2 * DC]
        qg, ag, gg = colt[:, 16:17], colt[:, 17:18], colt[:, 18:19]
        ag8 = sb("ag8", [P, 1])
        kg = sb("kg", [P, DH])
        wga = sb("wga", [P, DC, RANK])
        zga = sb("zga", [P, NT, RANK])
        wr = sb("wr", [P, DC, NG + NE])
        br = sb("br", [P, NG + NE])
        ssx = sb("ssx", [P, NT])
        stdx = sb("stdx", [P, NT])
        rx = sb("rx", [P, NT])
        sskq = sb("sskq", [P, 2, NT, 8])
        rkq = sb("rkq", [P, 2, NT, 8])
        lsum = sb("lsum", [P, 2])
        lexp = sb("lexp", [P, 2])
        nlam = sb("nlam", [P, 1])
        em = sb("em", [P, 2, 16])
        gl = sb("gl", [P, 2, 16])
        sso = sb("sso", [P, NT, 8])
        ro = sb("ro", [P, NT, 8])
        junk = sb("junk", [P, DV])
        mx = sb("mx", [P, 2, 2])
        nm = sb("nm", [P, 2, 2])
        es = sb("es", [P, 2, 2])
        ri = sb("ri", [P, 2, 2])
        ss2 = sb("ss2", [P, NT])
        st2 = sb("st2", [P, NT])
        r2 = sb("r2", [P, NT])
        ovf = sb("ovf", [P, 1], I32)
        idx = sb("idx", [P, PAIRS + 1], I32)
        tk = sb("tk", [P, 2, 2, NT])
        dst = sb("dst", [P, PAIRS + 1], I32)
        wk = sb("wk", [P, 2, NT])
        cur = sb("cur", [P, 1])

        hT = G[:, 1024:1024 + DC * NT * P].rearrange("p (c i t) -> p c i t", c=DC, i=NT)
        hL = G_r[:, 1024:1024 + DC * NT * P].rearrange("p (c i t) -> p c i t", c=DC, i=NT)
        hH = hbuf_r[:, :].rearrange("p (c i t) -> p c i t", c=DC, i=NT)
        qT = hbuf[:, 0:H * NT * P].rearrange("p (h t) -> p h t", h=H)
        kT = hbuf[:, H * NT * P:].rearrange("p (h t) -> p h t", h=H)
        mixT = hbuf[:, :].rearrange("p (c t) -> p c t", c=DC)
        xn = [Zpad[:, Z0 + C_Q * CW + k * D:Z0 + C_Q * CW + (k + 1) * D] for k in range(2)]
        xjunk = Zpad[:, Z0 + C_V * CW:Z0 + C_V * CW + D]
        HW = DC // 2 * 512
        wH = [W_r[:, k * HW:(k + 1) * HW] for k in range(2)]
        win = [W[:, (2 + k) * HW:(3 + k) * HW] for k in range(2)]
        wL = [W_r[:, (2 + k) * HW:(3 + k) * HW] for k in range(2)]
        kqsq = [G[:, k * 512:(k + 1) * 512] for k in range(2)]
        la = R0[:, 0:1280].rearrange("p (i n) -> p i n", i=NT)
        gz = R0[:, 1280:2560]
        gt = R0[:, 2560:3840]
        gaT = R0[:, 3840:4480]
        wa2 = R0[:, 4480:4736]
        lamv = R0[:, 4736:4992].rearrange("p (a n) -> p a n", a=4)
        lamp = R0[:, 4992:5120].rearrange("p (a n) -> p a n", a=2)
        bT = W[:, 0:1280].rearrange("p (h t) -> p h t", h=2)
        Ep = W[:, 1280:2560].rearrange("p (h t) -> p h t", h=2)
        Em = W[:, 2560:3840].rearrange("p (h t) -> p h t", h=2)
        qt = W[:, 3840:5120].rearrange("p (h t) -> p h t", h=2)
        kt = W[:, 5120:6400].rearrange("p (h t) -> p h t", h=2)
        ktok = W[:, 6400:7680].rearrange("p (i n) -> p i n", i=NT)
        St = G[:, 0:2048].rearrange("p (c h v) -> p c h v", c=8, h=2)
        S0 = G[:, 2048:4096].rearrange("p (b h v) -> p b h v", b=NB, h=2)
        Ss = G[:, 4096:6144].rearrange("p (b h v) -> p b h v", b=NB, h=2)
        kz = G[:, 6144:8192].rearrange("p (b n) -> p b n", b=NB)
        AT = R0[:, 0:2560].rearrange("p (i h e t) -> p i h e t", i=NT, h=2, e=2)
        qz = R0[:, 2560:4608].rearrange("p (h b t) -> p h b t", h=2, b=NB)
        tmpU = R0[:, 4608:4864].rearrange("p (h v) -> p h v", h=2)
        S = R0[:, 4864:5120].rearrange("p (h v) -> p h v", h=2)
        tmpS = R0[:, 5120:5632].rearrange("p (b h v) -> p b h v", b=2, h=2)
        NER = 3
        E = [[G[:, (2 * k + m) * 512:(2 * k + m + 1) * 512] for m in range(2)] for k in range(NER)]
        PT = [G[:, 3072 + k * 640:3712 + k * 640] for k in range(2)]
        enew = G[:, 4352:5376].rearrange("p (b t) -> p b t", b=NB)
        qbd = G[:, 5376:6400].rearrange("p (b h m q) -> p b h m q", b=NB, h=H, m=2)
        NKV = 5
        Kc = [r.rearrange("p (h t) -> p h t", h=H) for r in
              (W[:, 0:2048], W[:, 4096:6144], R0[:, 0:2048], Zpad[:, 0:2048], R0[:, 4096:6144])]
        Vc = [r.rearrange("p (j n) -> p j n", j=4) for r in
              (W[:, 2048:4096], W[:, 6144:8192], R0[:, 2048:4096], Zpad[:, 2048:4096], Zpad[:, 4096:6144])]
        wo = W[:, :].rearrange("p (c n) -> p c n", c=DC)
        hn = [G[:, 6144 + k * D:6144 + (k + 1) * D] for k in range(2)]
        GR0 = Z0 + C_GR * CW
        h2T = [Zpad[:, GR0 + k * D:GR0 + (k + 1) * D].rearrange("p (c t) -> p c t", c=DC) for k in range(2)]

        at = [GR0 + 2048]

        def tmp(n):
            at[0] += n
            assert at[0] <= GR0 + CW
            return Zpad[:, at[0] - n:at[0]]

        NL = NG + NE
        Lg = tmp(NT * NL).rearrange("p (i n) -> p i n", i=NT)
        at[0] = GR0
        gmax = tmp(NT)
        ge = tmp(NT * NG).rearrange("p (i g) -> p i g", i=NT)
        gs = tmp(NT)
        goh = tmp(NT * NG).rearrange("p (i g) -> p i g", i=NT)
        gm2 = tmp(NT)
        egs = tmp(NT * NE).rearrange("p (i g e) -> p i g e", i=NT, g=NG)
        esel = [tmp(NT * EPG).rearrange("p (i e) -> p i e", i=NT) for _ in range(2)]
        oh = [tmp(NT * EPG).rearrange("p (i e) -> p i e", i=NT) for _ in range(2)]
        mk = tmp(2 * NT).rearrange("p (k i) -> p k i", k=2)
        mk2 = tmp(NT)
        dm = tmp(NT)
        den = tmp(NT)
        M = tmp(2 * NT * NE).rearrange("p (k i g e) -> p k i g e", k=2, i=NT, g=NG)
        Ms = tmp((NT + 1) * NE)
        rk = tmp(2 * NT).rearrange("p (k i) -> p k i", k=2)
        pk = tmp(2 * NT).rearrange("p (k i) -> p k i", k=2)
        rn = tmp(2 * NT).rearrange("p (k i) -> p k i", k=2)
        loc = tmp(2 * NT).rearrange("p (k i) -> p k i", k=2)
        qk = tmp(2 * NT).rearrange("p (k i) -> p k i", k=2)
        cmpr = tmp(2 * NT * (ROUNDS - 1)).rearrange("p (m j) -> p m j", m=2 * NT)
        mprod = tmp(2 * NT * NE).rearrange("p (k n) -> p k n", k=2)
        Mp = tmp(4 * NT * PAIRS).rearrange("p (a k i n) -> p a k i n", a=2, k=2, i=NT)
        rmask = tmp(2 * NT).rearrange("p (k i) -> p k i", k=2)
        none = tmp(2 * (PAIRS + 1))
        cnt = tmp(1)
        ovf_f = tmp(1)
        assert at[0] <= GR0 + 2048
        OH0 = Z0 + C_V * CW + 1024
        Rt = hbuf[:, 0:4 * NT * (PAIRS + 1)].rearrange("p (k i a n) -> p k i a n", k=2, i=NT, a=2)
        OH = Zpad[:, OH0:OH0 + 1280].rearrange("p (n s) -> p n s", n=2 * NT)

        ebuf = [R0[:, :], Zpad[:, 0:EXP_W], Zpad[:, Z0 + C_K * CW:Z0 + C_K * CW + EXP_W], G[:, 0:EXP_W]]
        egu = [e[:, 0:GU_W].rearrange("p (c n) -> p c n", c=DC) for e in ebuf]
        edn = [e[:, GU_W:EXP_W].rearrange("p (f n) -> p f n", f=2) for e in ebuf]
        NXS = 2
        xs = [W[:, k * D:(k + 1) * D] for k in range(NXS)]
        xsT = [W[:, (2 + k) * D:(3 + k) * D].rearrange("p (c s) -> p c s", c=DC) for k in range(2)]
        ysb = [W[:, (4 + k) * D:(5 + k) * D] for k in range(2)]
        sil = [W[:, (6 + k) * D:(6 + k) * D + FE] for k in range(2)]
        hs = [W[:, (6 + k) * D + 256:(6 + k) * D + 256 + FE] for k in range(2)]
        hTs = [W[:, (6 + k) * D + 512:(6 + k) * D + 768].rearrange("p (f s) -> p f s", f=2) for k in range(2)]
        NYG = 3
        yg = [R0[:, k * 2 * D:(k + 1) * 2 * D] for k in range(NYG)]

        ld_x = [sem(f"ld_x{i}") for i in range(NT)]
        ld_cols = sem("ld_cols")
        ld_small = sem("ld_small")
        ld_win = [sem(f"ld_win{k}") for k in range(2)]
        ld_state = sem("ld_state")
        ld_k = [sem(f"ld_k{k}") for k in range(NKV)]
        ld_v = [sem(f"ld_v{k}") for k in range(NKV)]
        ld_wo = sem("ld_wo")
        ld_gu = [sem(f"ld_gu{k}") for k in range(4)]
        ld_dn = [sem(f"ld_dn{k}") for k in range(4)]
        pool_step = sem("pool_step")
        pool_seen = sem("pool_seen")
        sp_seen = sem("sp_seen")
        consts = sem("consts")
        dve_step = sem("dve_step")
        act_step = sem("act_step")
        ssq1 = sem("ssq1")
        std1 = sem("std1")
        rstd1 = sem("rstd1")
        xn_ready = sem("xn_ready")
        xT_done = sem("xT_done")
        hT_ready = sem("hT_ready")
        ga_done = sem("ga_done")
        zga_ready = sem("zga_ready")
        gaT_done = sem("gaT_done")
        gaT_ready = sem("gaT_ready")
        pre_done = sem("pre_done")
        gabs_ready = sem("gabs_ready")
        gln_ready = sem("gln_ready")
        la_ready = sem("la_ready")
        lam_mid = sem("lam_mid")
        lam_exp = sem("lam_exp")
        lam_ready = sem("lam_ready")
        hH_ready = sem("hH_ready")
        hL_ready = sem("hL_ready")
        wH_ready = sem("wH_ready")
        wL_ready = sem("wL_ready")
        half_done = sem("half_done")
        proj_done = sem("proj_done")
        z_free = sem("z_free")
        kqss_ready = sem("kqss_ready")
        kqstd = sem("kqstd")
        k_ready = sem("k_ready")
        q_ready = sem("q_ready")
        b_done = sem("b_done")
        b_ready = sem("b_ready")
        dec_in = sem("dec_in")
        dec_ready = sem("dec_ready")
        at_zero = sem("at_zero")
        qkT_done = sem("qkT_done")
        qkT_ready = sem("qkT_ready")
        gT_done = sem("gT_done")
        gqk_ready = sem("gqk_ready")
        qz_ready = sem("qz_ready")
        ktok_done = sem("ktok_done")
        ktok_ready = sem("ktok_ready")
        kz_ready = sem("kz_ready")
        sc_done = sem("sc_done")
        AT_ready = sem("AT_ready")
        U_done = sem("U_done")
        U_used = sem("U_used")
        St_ready = sem("St_ready")
        Ss_ready = sem("Ss_ready")
        go_done = sem("go_done")
        go_sq = sem("go_sq")
        go_ready = sem("go_ready")
        silu_ready = sem("silu_ready")
        sp_ready = sem("sp_ready")
        ss_ready = sem("ss_ready")
        st_states = sem("st_states")
        st_kv = sem("st_kv")
        att_zero = sem("att_zero")
        s_done = sem("s_done")
        nm_ready = sem("nm_ready")
        e_ready = sem("e_ready")
        p_ready = sem("p_ready")
        pt_done = sem("pt_done")
        pt_ready = sem("pt_ready")
        o_done = sem("o_done")
        o_sq = sem("o_sq")
        ao_ready = sem("ao_ready")
        qbd_ready = sem("qbd_ready")
        d_s_done = sem("d_s_done")
        d_nm_ready = sem("d_nm_ready")
        d_e_ready = sem("d_e_ready")
        cb_ready = sem("cb_ready")
        d_pt_done = sem("d_pt_done")
        d_pt_ready = sem("d_pt_ready")
        d_pv_done = sem("d_pv_done")
        ostd = sem("ostd")
        mix_ready = sem("mix_ready")
        mT_done = sem("mT_done")
        mT_a = sem("mT_a")
        mT_g = sem("mT_g")
        out_done = sem("out_done")
        x2_ready = sem("x2_ready")
        ssq2 = sem("ssq2")
        std2 = sem("std2")
        rstd2 = sem("rstd2")
        hn_ready = sem("hn_ready")
        st_hn = [sem(f"st_hn{k}") for k in range(2)]
        h2_done = sem("h2_done")
        h2_ready = sem("h2_ready")
        lg_done = sem("lg_done")
        gexp_in = sem("gexp_in")
        gexp_out = sem("gexp_out")
        m_ready = sem("m_ready")
        rank_done = sem("rank_done")
        tab_step = sem("tab_step")
        tab_in = sem("tab_in")
        tab_done = sem("tab_done")
        idx_ready = sem("idx_ready")
        ovf_ready = sem("ovf_ready")
        gath = [sem(f"gath{k}") for k in range(NXS)]
        xsT_done = sem("xsT_done")
        xsT_ready = sem("xsT_ready")
        gu_done = sem("gu_done")
        sil_ready = sem("sil_ready")
        h_ready = sem("h_ready")
        hT_done = sem("hT_done")
        xs_zero = sem("xs_zero")
        hTs_ready = sem("hTs_ready")
        dn_done = sem("dn_done")
        ysb_ready = sem("ysb_ready")
        st_y = [sem(f"st_y{k}") for k in range(2)]
        ygath = [sem(f"ygath{k}") for k in range(NYG)]
        ysum = sem("ysum")
        st_out = sem("st_out")

        block = ctx.enter_context(nc.Block())

        def gu_rows(e):
            return w_gu[bass.ds(e * P, P), :].rearrange("p (c n) -> p c n", c=DC)

        def dn_rows(e):
            return w_dn[bass.ds(e * P, P), :].rearrange("p (f n) -> p f n", f=2)

        @block.sync
        def _(sp):
            for i in range(2):
                sp.dma_start(X[:, i, :], x[i]).then_inc(ld_x[i], 16)
            sp.dma_start(colt[:, :], cols).then_inc(ld_cols, 16)
            for i in range(2, NT):
                sp.dma_start(X[:, i, :], x[i]).then_inc(ld_x[i], 16)
            sp.dma_start(wga[:, :, :], w_ga).then_inc(ld_small, 16)
            sp.dma_start(wa2[0:RANK + 1, :], w_a2b).then_inc(ld_small, 16)
            sp.dma_start(lamv, lam.partition_broadcast(P)).then_inc(ld_small, 16)
            sp.dma_start(kg[:, :], k_gain.partition_broadcast(P)).then_inc(ld_small, 16)
            sp.dma_start(br[:, :], b_r.partition_broadcast(P)).then_inc(ld_small, 16)
            sp.dma_start(wr[:, :, :], w_r).then_inc(ld_small, 16)
            def w_half(c, k):
                sp.dma_start(win[k], w_main[bass.ds(c * P, P), k * HW:(k + 1) * HW]).then_inc(ld_win[k], 16)

            for k in range(2):
                w_half(0, k)
            with sp.Fori(1, 6) as c:
                sp.wait_ge(half_done, c)
                w_half(c, 0)
                sp.wait_ge(proj_done, NT * c)
                w_half(c, 1)
            sp.wait_ge(proj_done, NT * 6)
            sp.dma_start(S0, state).then_inc(ld_state, 16)
            sp.wait_ge(go_done, NT)
            sp.wait_ge(ss_ready, 1)
            for b in range(NB):
                if b == 2:
                    sp.wait_ge(st_states, 2 * 16)
                if b >= NKV:
                    sp.wait_ge(d_s_done, b - NKV + 1)
                sp.dma_start(Kc[b % NKV], cache_kt[b]).then_inc(ld_k[b % NKV], 16)
                if b >= NKV:
                    sp.wait_ge(d_pv_done, b - NKV + 1)
                sp.dma_start(Vc[b % NKV], cache_v[b]).then_inc(ld_v[b % NKV], 16)
            for k in range(2):
                sp.wait_ge(d_s_done, NKV + k + 1)
                sp.dma_start(wo[:, 4 * k:4 * k + 2, :], w_out[:, 4 * k:4 * k + 2, :]).then_inc(ld_wo, 16)
            for k in range(2):
                sp.wait_ge(d_pv_done, NKV + k + 1)
                sp.dma_start(wo[:, 4 * k + 2:4 * k + 4, :], w_out[:, 4 * k + 2:4 * k + 4, :]).then_inc(ld_wo, 16)
            sp.wait_ge(d_s_done, NB)
            sp.wait_ge(d_pv_done, NB)
            for e in range(2):
                sp.dma_start(egu[e], gu_rows(e)).then_inc(ld_gu[e], 16)
                sp.dma_start(edn[e], dn_rows(e)).then_inc(ld_dn[e], 16)
            sp.wait_ge(mT_done, 2 * NT)
            sp.wait_ge(st_kv, 2 * NT * 16)
            for e in (2, 3):
                sp.dma_start(egu[e], gu_rows(e)).then_inc(ld_gu[e], 16)
                sp.dma_start(edn[e], dn_rows(e)).then_inc(ld_dn[e], 16)

            def experts(g0, g):
                for k in range(4):
                    if k % 2 == 0:
                        sp.wait_ge(gu_done, (g0 + g) * 2 + k // 2 - 1)
                    sp.dma_start(egu[k], gu_rows(g * 4 + k)).then_inc(ld_gu[k], 16)
                for k in range(4):
                    if k % 2 == 0:
                        sp.wait_ge(dn_done, (g0 + g) * 2 + k // 2 - 1)
                    sp.dma_start(edn[k], dn_rows(g * 4 + k)).then_inc(ld_dn[k], 16)

            with sp.Fori(1, NE // 4) as g:
                experts(0, g)
            sp.wait_ge(ovf_ready, 1)
            with sp.If(sp.value_load(ovf[0:1, 0:1]) > 0):
                with sp.Fori(1, ROUNDS) as r:
                    with sp.Fori(0, NE // 4) as g:
                        experts(r * 8, g)
                for k in range(2):
                    sp.wait_ge(st_y[k], ROUNDS * (PAIRS // 2) * 16)
            for k in range(2):
                sp.wait_ge(st_y[k], PAIRS // 2 * 16)
            sp.wait_ge(dn_done, PAIRS)
            for i in range(NT):
                if i >= NYG:
                    sp.wait_ge(ysum, 2 * (i - NYG + 1))
                sp.dma_start(yg[i % NYG], ye_dram[2 * P * i:2 * P * (i + 1), :].rearrange("(p k) d -> p (k d)", k=2)
                             ).then_inc(ygath[i % NYG], 16)
            sp.wait_ge(st_kv, 2 * NT * 16)
            sp.wait_ge(st_states, 2 * 16)

        @block.gpsimd
        def _(pool):
            n = [0]

            def step(ins):
                n[0] += 1
                ins.then_inc(pool_step, 1)
                pool.wait_ge(pool_step, n[0])

            pool.memset(epsc[:, :], EPS)
            pool.memset(ones[:, :], 1.0)
            pool.memset(gaT[0:RANK + 1, :], 1.0)
            pool.memset(C0[:, :], 0.0)
            pool.memset(C1[:, :], 0.0)
            pool.memset(mA[:, :], 0.0)
            pool.memset(mB[:, :], NEG)
            pool.memset(strict[:, :], 1.0)
            pool.memset(bmask[:, :], 1.0)
            pool.memset(tri64[:, :], 1.0 / 16)
            step(pool.memset(ident[:, :], 0.0))
            step(pool.affine_select(out=ident[:, :], in_=ident[:, :], compare_op=ALU.not_equal, fill=1.0,
                                    base=0, pattern=[[-1, P]], channel_multiplier=1))
            step(pool.affine_select(out=tri64[:, :], in_=tri64[:, :], compare_op=ALU.is_ge, fill=0.0,
                                    base=0, pattern=[[1, P]], channel_multiplier=-1))
            t16 = tri16[:, :].rearrange("p (b t) -> p b t", b=NB)
            step(pool.affine_select(out=t16, in_=tri64[:, :].rearrange("p (b t) -> p b t", b=NB),
                                    compare_op=ALU.is_ge, fill=0.0,
                                    base=0, pattern=[[-Q, NB], [0, Q]], channel_multiplier=1))
            step(pool.memset(tri64[0:CHUNK, CHUNK:P], 0.0))
            step(pool.affine_select(out=strict[:, :], in_=strict[:, :], compare_op=ALU.is_gt, fill=0.0,
                                    base=0, pattern=[[1, P]], channel_multiplier=-1))
            step(pool.affine_select(out=bmask[:, :], in_=bmask[:, :], compare_op=ALU.is_ge, fill=0.0,
                                    base=0, pattern=[[-Q, NB]], channel_multiplier=1))
            step(pool.affine_select(out=bmask[:, :], in_=bmask[:, :], compare_op=ALU.is_ge, fill=0.0,
                                    base=Q - 1, pattern=[[Q, NB]], channel_multiplier=-1))
            for m, c in ((0, C0), (1, C1)):
                cv = c[:, :].rearrange("p (h q) -> p h q", h=H)
                step(pool.affine_select(out=cv, in_=cv, compare_op=ALU.not_equal, fill=1.0,
                                        base=-Q * m, pattern=[[-2 * Q, H], [-1, Q]], channel_multiplier=1))
            pool.memset(mA[0:1, 0:CHUNK], 1.0)
            step(pool.memset(mA[CHUNK:CHUNK + 1, 0:CHUNK], 1.0))
            pool.iota(iota_i[:, :], pattern=[[1, P]], base=0, channel_multiplier=0)
            step(pool.iota(tok_i[:, :], pattern=[[P, NT]], base=0, channel_multiplier=1))
            step(pool.iota(desc_i[:, :], pattern=[[-1, EPG]], base=EPG, channel_multiplier=0))
            pool.tensor_copy(iota128[:, :], iota_i[:, :])
            pool.tensor_copy(desc[:, :], desc_i[:, :])
            pool.memset(cur[:, :], 0.0)
            step(pool.tensor_copy(tok[:, :], tok_i[:, :]))
            step(pool.tensor_scalar(thr[:, :], iota128[:, 1:ROUNDS], float(CAP), None, ALU.mult))
            for k in range(2):
                pool.tensor_scalar(tk[:, 0, k, :], tok[:, :], 1.0, None, ALU.add)
                step(pool.tensor_scalar(tk[:, 1, k, :], tok[:, :], 2.0, float(k + 1), ALU.mult, ALU.add))
            pool.nop().then_inc(consts, 1)
            for i in range(NT):
                pool.wait_ge(k_ready, i + 1)
                pool.dma_start(k_out[i], z(C_K, i)).then_inc(st_kv, 16)
            for i in range(NT):
                pool.wait_ge(z_free, 5 + 25 + i + 1)
                pool.dma_start(v_out[i], z(C_V, i)).then_inc(st_kv, 16)
            pool.wait_ge(b_done, 1)
            pool.memset(R0[:, 0:2560], 0.0).then_inc(at_zero, 1)
            pool.memset(R0[:, 2560:4608], 0.0).then_inc(at_zero, 1)
            pool.wait_ge(sp_ready, 1)
            pool.dma_start(sp_out, S).then_inc(st_states, 16)
            pool.wait_ge(ss_ready, 1)
            pool.dma_start(ss_out, S0).then_inc(st_states, 16)
            pool.wait_ge(go_done, NT)
            pool.wait_ge(st_states, 32)
            pool.memset(G[:, 4352:6400], 0.0).then_inc(att_zero, 1)
            pool.memset(Cb[:, :, :], 0.0).then_inc(att_zero, 1)
            for i in range(NT):
                pool.wait_ge(hn_ready, i + 1)
                pool.dma_start(hn_dram[i * P:(i + 1) * P, :], hn[i % 2]).then_inc(st_hn[i % 2], 16)
            pool.wait_ge(out_done, 2 * NT)
            pool.memset(W[:, 0:NXS * D], 0.0).then_inc(xs_zero, 1)
            pool.wait_ge(xs_zero, 1)
            pool.wait_ge(st_hn[0], 3 * 16)
            pool.wait_ge(st_hn[1], 2 * 16)

            def pairs(r):
                def seen():
                    if not isinstance(r, int):
                        pool.sem_inc(pool_seen, 1)

                def scatter(p):
                    pool.wait_ge(ysb_ready, r * 2 * PAIRS + 2 * (p + 1))
                    seen()
                    pool.indirect_dma_start(
                        out=ye_dram, out_offset=bass.IndirectOffsetOnAxis(ap=dst[:, p:p + 1], axis=0),
                        in_=ysb[p % 2], in_offset=None, bounds_check=2 * NT * P - 1, oob_is_err=False,
                    ).then_inc(st_y[p % 2], 16)

                pool.wait_ge(idx_ready, r + 1)
                seen()
                for p in range(PAIRS + 1):
                    if p >= NXS:
                        pool.wait_ge(xsT_done, r * 2 * (PAIRS + 1) + 2 * (p - NXS + 1))
                        seen()
                    pool.indirect_dma_start(
                        out=xs[p % NXS], out_offset=None, in_=hn_dram,
                        in_offset=bass.IndirectOffsetOnAxis(ap=idx[:, p:p + 1], axis=0),
                        bounds_check=NT * P - 1, oob_is_err=False,
                    ).then_inc(gath[p % NXS], 16)
                    if p >= 3:
                        scatter(p - 3)
                for p in range(PAIRS - 2, PAIRS):
                    scatter(p)

            pairs(0)
            pool.wait_ge(ovf_ready, 1)
            with pool.If(pool.value_load(ovf[0:1, 0:1]) > 0):
                with pool.Fori(1, ROUNDS) as r:
                    pool.wait_ge(xsT_done, r * 2 * (PAIRS + 1))
                    pairs(r)

        @block.scalar
        def _(act):
            n = [0]

            def step(ins):
                n[0] += 1
                ins.then_inc(act_step, 1)
                act.wait_ge(act_step, n[0])

            act.wait_ge(consts, 1)
            act.wait_ge(ld_cols, 16)

            def root(i):
                act.wait_ge(ssq1, i + 1)
                act.activation(stdx[:, i:i + 1], ssx[:, i:i + 1], ACT.Sqrt, bias=epsc[:, 0:1],
                               scale=1.0 / D).then_inc(std1, 1)

            def h_high(i):
                act.wait_ge(hT_ready, 2 * i + 2)
                act.activation(hH[:, :, i, :], hT[:, :, i, :], ACT.Copy).then_inc(hH_ready, 1)

            def w_high(c, k):
                act.wait_ge(ld_win[k], (c + 1) * 16)
                act.activation(wH[k], win[k], ACT.Copy).then_inc(wH_ready, 1)

            root(0)
            for i in range(NT):
                if i + 1 < NT:
                    root(i + 1)
                act.wait_ge(rstd1, i + 1)
                if i >= 2:
                    act.wait_ge(xT_done, 2 * (i - 1))
                act.activation(xn[i % 2], X[:, i, :], ACT.Copy, scale=rx[:, i:i + 1]).then_inc(xn_ready, 1)
                if i >= 1:
                    h_high(i - 1)
            w_high(0, 0)
            h_high(NT - 1)
            w_high(0, 1)
            act.wait_ge(lam_mid, 1)
            act.activation(lexp[:, :], lsum[:, :], ACT.Exp).then_inc(lam_exp, 1)
            act.wait_ge(gabs_ready, 1)
            step(act.activation(gt, gt, ACT.Exp))
            act.activation(gt, gt, ACT.Ln, bias=1.0).then_inc(gln_ready, 1)

            for i in range(NT):
                act.nop().then_inc(z_free, 1)
            def evac(c, n_before, i):
                act.wait_ge(proj_done, n_before + i + 1)
                o = c * CW + (Z0 + i * 512)
                act.activation(Zpad[:, bass.ds(o, 512)], bank[i][:, :], ACT.Copy).then_inc(z_free, 1)

            def chunk(c):
                for i in range(2):
                    evac(c, NT * c, i)
                w_high(c + 1, 0)
                for i in range(2, NT):
                    evac(c, NT * c, i)
                w_high(c + 1, 1)

            with act.Fori(0, 4) as c:
                chunk(c)
            chunk(4)
            evac(5, 25, 0)
            act.wait_ge(kqss_ready, 1)
            act.activation(rkq[:, :, :, :], sskq[:, :, :, :], ACT.Sqrt, bias=epsc[:, 0:1],
                           scale=1.0 / DH).then_inc(kqstd, 1)
            for i in range(1, NT):
                evac(5, 25, i)
            act.wait_ge(b_done, 1)
            for k in range(3):
                w = 2 if k < 2 else 1
                act.activation(bT[:, :, 256 * k:256 * k + 128 * w].rearrange("p h (i t) -> p i h t", i=w),
                               bank[5 + k][:, 0:256 * w].rearrange("p (i h t) -> p i h t", i=w, h=2),
                               ACT.Copy).then_inc(b_ready, 1)
            act.wait_ge(b_ready, 3)
            act.activation(em[:, :, 0:8], bT[:, :, 0:512].rearrange("p h (c t) -> p h c t", c=8)[:, :, :, 31],
                           ACT.Exp).then_inc(dec_ready, 1)
            act.activation(em[:, :, 8:16], bT[:, :, 512:640].rearrange("p h (c t) -> p h c t", c=8)[:, :, :, 7],
                           ACT.Exp).then_inc(dec_ready, 1)
            act.wait_ge(dec_in, 2)
            act.activation(Ep, kt, ACT.Exp).then_inc(dec_ready, 1)
            act.activation(Em, kt, ACT.Exp, scale=-1.0).then_inc(dec_ready, 1)
            for m in range(2 * NT):
                act.wait_ge(qkT_done, m + 1)
                i = m % NT
                src = bank[m % 4][:, :].rearrange("p (h t) -> p h t", h=H)
                if m < NT:
                    act.activation(kT[:, :, i * P:(i + 1) * P], src, ACT.Copy).then_inc(qkT_ready, 1)
                else:
                    act.activation(qT[:, :, i * P:(i + 1) * P], src, ACT.Copy, scale=qg).then_inc(qkT_ready, 1)
            for i in range(NT):
                act.wait_ge(ktok_done, i + 1)
                act.activation(ktok[:, i, :], bank[6 + i % 2][:, 0:256], ACT.Copy).then_inc(ktok_ready, 1)
            act.wait_ge(z_free, 7 * NT)
            act.activation(zall(C_GR), zall(C_GR), ACT.Silu).then_inc(silu_ready, 1)
            for i in range(NT):
                act.wait_ge(go_done, i + 1)
                for h in range(H):
                    step(act.activation(junk[:, :], bank[2 * (i % 2) + h % 2][:, (h // 2) * P:(h // 2 + 1) * P],
                                        ACT.Square, accum_out=sso[:, i, H + h:H + h + 1]))
                act.nop().then_inc(go_sq, 1)
            items = [(i, h) for i in range(NP) for h in range(H)]
            NI = len(items)
            act.wait_ge(att_zero, 2)

            def exps(m):
                i, h = items[m]
                L = (i + 1) * P
                act.wait_ge(nm_ready, m + 1)
                if m >= NER:
                    act.wait_ge(pt_done, m - NER + 1)
                if m >= 2:
                    act.wait_ge(p_ready, m - 1)
                for mm in range(2):
                    act.activation(E[m % NER][mm][:, 0:L], bank[2 * (m % 2) + mm][:, 0:L], ACT.Exp,
                                   bias=nm[:, m % 2, mm:mm + 1], scale=DH ** -0.5,
                                   accum_out=es[:, m % 2, mm:mm + 1]).then_inc(e_ready, 1)

            def pts(m):
                i, h = items[m]
                L = (i + 1) * P
                act.wait_ge(pt_done, m + 1)
                if m >= 2:
                    act.wait_ge(o_done, m - 1)
                act.activation(PT[m % 2][:, 0:L], bank[4 + m % 2][:, 0:L], ACT.Copy).then_inc(pt_ready, 1)

            def osq(i, src, done, value):
                act.wait_ge(done, value)
                for h in range(H):
                    step(act.activation(junk[:, :], src[:, h * P:(h + 1) * P], ACT.Square,
                                        accum_out=sso[:, i, h:h + 1]))
                act.nop().then_inc(o_sq, 1)

            for m in range(NI + 3):
                if m < NI:
                    exps(m)
                if 2 <= m < NI + 2:
                    pts(m - 2)
                if m >= 3 and (m - 3) % H == H - 1:
                    i = (m - 3) // H
                    osq(i, bank[6 + i % 2], o_done, m - 2)

            def d_exps(b):
                act.wait_ge(d_nm_ready, b + 1)
                if b < NER:
                    act.wait_ge(pt_done, NI)
                else:
                    act.wait_ge(d_pt_done, b - NER + 1)
                if b < 2:
                    act.wait_ge(p_ready, NI)
                else:
                    act.wait_ge(cb_ready, b - 1)
                act.activation(E[b % NER][0], bank[2 * (b % 2)][:, :], ACT.Exp, bias=nm[:, b % 2, 0:1],
                               scale=DH ** -0.5, accum_out=es[:, b % 2, 0:1]).then_inc(d_e_ready, 1)
                act.activation(enew[:, b, b * Q:(b + 1) * Q], bank[2 * (b % 2) + 1][:, 0:Q], ACT.Exp,
                               bias=nm[:, b % 2, 0:1], scale=DH ** -0.5,
                               accum_out=es[:, b % 2, 1:2]).then_inc(d_e_ready, 1)

            def d_pts(b):
                act.wait_ge(d_pt_done, b + 1)
                if b >= 2:
                    act.wait_ge(d_pv_done, b - 1)
                act.activation(PT[b % 2][:, 0:512], bank[4 + b % 2][:, :], ACT.Copy).then_inc(d_pt_ready, 1)
                act.activation(PT[b % 2][:, 512:640], bank[7][:, 0:P], ACT.Copy).then_inc(d_pt_ready, 1)

            for b in range(NB + 2):
                if b < NB:
                    d_exps(b)
                if b >= 2:
                    d_pts(b - 2)
            osq(NP, bank[6], d_pv_done, NB)
            act.wait_ge(o_sq, NT)
            act.activation(ro[:, :, :], sso[:, :, :], ACT.Sqrt, bias=epsc[:, 0:1], scale=1.0 / DV).then_inc(ostd, 1)
            for i in range(NT):
                act.wait_ge(mT_done, 2 * i + 2)
                act.activation(mixT[:, H:2 * H, i * P:(i + 1) * P],
                               bank[2 * (i % 2) + 1][:, :].rearrange("p (c t) -> p c t", c=H),
                               ACT.Copy, scale=gg).then_inc(mT_g, 1)
            for i in range(NT):
                act.wait_ge(ssq2, i + 1)
                act.activation(st2[:, i:i + 1], ss2[:, i:i + 1], ACT.Sqrt, bias=epsc[:, 0:1],
                               scale=1.0 / D).then_inc(std2, 1)
                act.wait_ge(rstd2, i + 1)
                if i >= 2:
                    act.wait_ge(st_hn[i % 2], 16 * (i // 2))
                    act.wait_ge(h2_done, 2 * (i - 1))
                act.activation(hn[i % 2], X[:, i, :], ACT.Copy, scale=r2[:, i:i + 1]).then_inc(hn_ready, 1)
            act.wait_ge(gexp_in, 1)
            act.activation(ge, ge, ACT.Exp).then_inc(gexp_out, 1)
            act.wait_ge(gexp_in, 2)
            act.activation(dm, dm, ACT.Exp).then_inc(gexp_out, 1)

            def silu(r, g, q):
                act.wait_ge(gu_done, (r * 8 + g) * 2 + q + 1)
                act.activation(sil[q], bank[2 + q][:, 0:FE], ACT.Silu).then_inc(sil_ready, 1)

            def hidden(r, g, q):
                act.wait_ge(hT_done, (r * 8 + g) * 2 + q + 1)
                act.activation(hTs[q].rearrange("p f s -> p (f s)"), bank[2 + q][:, 0:FE], ACT.Copy).then_inc(hTs_ready, 1)

            def rows(r, g, q, first):
                act.wait_ge(dn_done, (r * 8 + g) * 2 + q + 1)
                if not first:
                    act.wait_ge(st_y[q], (r * 8 + g) * 16)
                for hf in range(2):
                    act.activation(ysb[q][:, hf * 512:(hf + 1) * 512], bank[4 + 2 * q + hf][:, :],
                                   ACT.Copy).then_inc(ysb_ready, 1)

            def group(r, g, first=False):
                for q in range(2):
                    silu(r, g, q)
                    hidden(r, g, q)
                for q in range(2):
                    rows(r, g, q, first)

            group(0, 0, first=True)
            with act.Fori(1, NE // 4) as g:
                group(0, g)
            act.wait_ge(ovf_ready, 1)
            with act.If(act.value_load(ovf[0:1, 0:1]) > 0):
                with act.Fori(1, ROUNDS) as r:
                    with act.Fori(0, NE // 4) as g:
                        group(r, g)
            for i in range(NT):
                act.wait_ge(ysum, 2 * (i + 1))
                act.dma_start(y_out[i], X[:, i, :]).then_inc(st_out, 16)
            act.wait_ge(st_out, NT * 16)

        @block.vector
        def _(dve):
            n = [0]

            def step(ins):
                n[0] += 1
                ins.then_inc(dve_step, 1)
                dve.wait_ge(dve_step, n[0])

            def bc(ap, shape):
                return ap.unsqueeze(len(ap.shape)).broadcast_to(shape)

            def squares(i):
                dve.wait_ge(ld_x[i], 16)
                if i:
                    dve.wait_ge(ssq1, i)
                dve.tensor_tensor_reduce(out=xjunk, in0=X[:, i, :], in1=X[:, i, :], scale=1.0, scalar=0.0,
                                         op0=ALU.mult, op1=ALU.add, accum_out=ssx[:, i:i + 1]).then_inc(ssq1, 1)

            def hT_out(i):
                for q in range(2):
                    dve.wait_ge(xT_done, 2 * i + q + 1)
                    ins = dve.tensor_tensor(hT[:, 4 * q:4 * q + 4, i, :],
                                            bank[2 * (i % 2) + q][:, :].rearrange("p (c t) -> p c t", c=4),
                                            bc(g1[:, 4 * q:4 * q + 4], [P, 4, P]), ALU.mult)
                    ins.then_inc(hT_ready, 1)

            def h_low(i):
                dve.wait_ge(hH_ready, i + 1)
                dve.wait_ge(ga_done, i + 1)
                dve.tensor_tensor(hL[:, :, i, :], hT[:, :, i, :], hH[:, :, i, :].bitcast(F32),
                                  ALU.subtract).then_inc(hL_ready, 1)

            def w_low(c, k):
                dve.wait_ge(wH_ready, 2 * c + k + 1)
                dve.tensor_tensor(wL[k], win[k], wH[k].bitcast(F32), ALU.subtract).then_inc(wL_ready, 1)

            squares(0)
            dve.wait_ge(ld_cols, 16)
            for i in range(NT):
                if i + 1 < NT:
                    squares(i + 1)
                dve.wait_ge(std1, i + 1)
                dve.reciprocal(rx[:, i:i + 1], stdx[:, i:i + 1]).then_inc(rstd1, 1)
                if i >= 1:
                    hT_out(i - 1)
                if i >= 2:
                    h_low(i - 2)
            hT_out(NT - 1)
            h_low(NT - 2)
            w_low(0, 0)
            h_low(NT - 1)
            dve.wait_ge(ga_done, NT)
            dve.tensor_copy(zga[:, :, :], bank[5][:, 0:NT * RANK].rearrange("p (i r) -> p i r", i=NT)).then_inc(zga_ready, 1)
            dve.wait_ge(gaT_done, 1)
            dve.wait_ge(consts, 1)
            dve.tensor_copy(gaT[0:RANK, 0:512], bank[6][0:RANK, :]).then_inc(gaT_ready, 1)
            dve.tensor_copy(gaT[0:RANK, 512:640], bank[7][0:RANK, 0:128]).then_inc(gaT_ready, 1)
            w_low(0, 1)
            dve.wait_ge(ld_small, 6 * 16)
            step(dve.tensor_tensor(lamp, lamv[:, 0:4:2, :], lamv[:, 1:4:2, :], ALU.mult))
            dve.tensor_reduce(lsum[:, :], lamp, AX.X, ALU.add).then_inc(lam_mid, 1)
            dve.wait_ge(pre_done, 1)
            dve.tensor_copy(gz[:, 0:512], bank[5][:, :])
            dve.tensor_copy(gz[:, 512:1024], bank[6][:, :])
            step(dve.tensor_copy(gz[:, 1024:1280], bank[7][:, 0:256]))
            dve.scalar_tensor_tensor(out=gt, in0=gz, scalar=-1.0, in1=gz, op0=ALU.mult, op1=ALU.min).then_inc(gabs_ready, 1)
            dve.wait_ge(gln_ready, 1)
            dve.scalar_tensor_tensor(out=la.rearrange("p i n -> p (i n)"), in0=gz, scalar=0.0, in1=gt,
                                     op0=ALU.min, op1=ALU.subtract).then_inc(la_ready, 1)
            dve.wait_ge(lam_exp, 1)
            step(dve.scalar_tensor_tensor(out=nlam[:, :], in0=lexp[:, 1:2], scalar=-LAM_INIT, in1=lexp[:, 0:1],
                                          op0=ALU.add, op1=ALU.subtract))
            dve.scalar_tensor_tensor(out=Cm[:, :], in0=C1[:, :], scalar=nlam[:, 0:1], in1=C0[:, :],
                                     op0=ALU.mult, op1=ALU.add)
            step(dve.tensor_scalar(ag8[:, :], ag, 1.0 - LAM_INIT, None, ALU.mult))
            with dve.Fori(1, C_K + 1) as c:
                for k in range(2):
                    w_low(c, k)
            for c, kq in ((C_K, 0), (C_Q, 1)):
                w_low(c + 1, 0)
                for i in range(NT):
                    dve.wait_ge(z_free, 5 + 5 * c + i + 1)
                    step(dve.tensor_tensor(kqsq[i % 2], z(c, i), z(c, i), ALU.mult))
                    step(dve.tensor_reduce(sskq[:, kq, i, :], kqsq[i % 2].rearrange("p (g d) -> p g d", g=8),
                                           AX.X, ALU.add))
                w_low(c + 1, 1)
            dve.nop().then_inc(kqss_ready, 1)
            dve.wait_ge(kqstd, 1)
            step(dve.reciprocal(rkq[:, :, :, :], rkq[:, :, :, :]))
            for i in range(NT):
                kv = z(C_K, i).rearrange("p (g d) -> p g d", g=8)
                step(dve.tensor_tensor(kv, kv, bc(rkq[:, 0, i, :], [P, 8, DH]), ALU.mult))
                dve.tensor_tensor(kv, kv, kg[:, :].unsqueeze(1).broadcast_to([P, 8, DH]), ALU.mult).then_inc(k_ready, 1)
            for i in range(NT):
                qv = z(C_Q, i).rearrange("p (g d) -> p g d", g=8)
                dve.tensor_tensor(qv, qv, bc(rkq[:, 1, i, :], [P, 8, DH]), ALU.mult).then_inc(q_ready, 1)
            dve.wait_ge(b_ready, 3)
            for a, L, mid in ((0, CHUNK, CHUNK // 2 - 1), (512, Q, Q // 2 - 1)):
                bv = bT[:, :, a:a + 8 * L].rearrange("p h (c t) -> p h c t", c=8)
                dv = kt[:, :, a:a + 8 * L].rearrange("p h (c t) -> p h c t", c=8)
                for hp in range(2):
                    ins = dve.tensor_tensor(dv[:, hp], bv[:, hp], bv[:, hp, :, mid:mid + 1].broadcast_to([P, 8, L]),
                                            ALU.subtract)
                ins.then_inc(dec_in, 1)
            dve.wait_ge(dec_ready, 4)
            elp = Ep[:, :, 0:512].rearrange("p h (c t) -> p h c t", c=8)[:, :, :, CHUNK - 1]
            els = Ep[:, :, 512:640].rearrange("p h (c t) -> p h c t", c=8)[:, :, :, Q - 1]
            dve.tensor_tensor(gl[:, :, 0:8], em[:, :, 0:8], elp, ALU.mult)
            step(dve.tensor_tensor(gl[:, :, 8:16], em[:, :, 8:16], els, ALU.mult))
            for i in range(NT):
                dve.wait_ge(gT_done, i + 1)
                ts = slice(i * P, (i + 1) * P)
                b4 = bank[4 + i % 2][:, :].rearrange("p (a h t) -> p a h t", a=2, h=2)
                dve.scalar_tensor_tensor(out=qt[:, :, ts], in0=b4[:, 0], scalar=DH ** -0.5, in1=Ep[:, :, ts],
                                         op0=ALU.mult, op1=ALU.mult).then_inc(gqk_ready, 1)
                dve.tensor_tensor(kt[:, :, ts], b4[:, 1], Em[:, :, ts], ALU.mult).then_inc(gqk_ready, 1)
            dve.wait_ge(gqk_ready, 2 * NT)
            dve.wait_ge(at_zero, 2)
            for hp in range(2):
                dve.tensor_copy(bass.AP(qz.tensor, qz[:, hp, 0, 0:Q].offset, [qz.ap[0], [P + Q, NB], [1, Q]]),
                                qt[:, hp, 512:640].rearrange("p (b t) -> p b t", b=NB)).then_inc(qz_ready, 1)
            dve.wait_ge(ld_state, 16)
            for hp in range(2):
                dve.tensor_tensor(Ss[:, :, hp, :], S0[:, :, hp, :], bc(em[:, hp, 8:16], [P, NB, DV]), ALU.mult).then_inc(Ss_ready, 1)
            dve.wait_ge(ktok_ready, NT)
            for b in range(NB):
                dve.tensor_scalar(kz[:, b, :], ktok[:, NP, :], bmask[:, b:b + 1], None, ALU.mult).then_inc(kz_ready, 1)

            def masked(i):
                tri = tri64 if i < NP else tri16
                for h2 in range(2):
                    dve.wait_ge(sc_done, 2 * i + h2 + 1)
                    for hp in range(2):
                        ins = dve.copy_predicated(AT[:, i, hp, h2, :], tri[:, :].bitcast(U32),
                                                  bank[2 * (i % 2) + h2][:, hp * P:(hp + 1) * P])
                    ins.then_inc(AT_ready, 1)

            def states(i):
                dve.wait_ge(U_done, i + 1)
                for j in range(2):
                    c = 2 * i + j
                    if c >= 1:
                        for hp in range(2):
                            ins = dve.tensor_scalar(St[:, c, hp, :], S[:, hp, :], em[:, hp, c:c + 1], None, ALU.mult)
                    else:
                        ins = dve.nop()
                    ins.then_inc(St_ready, 1)
                    el = Ep[:, :, c * CHUNK + CHUNK - 1:c * CHUNK + CHUNK]
                    for hp in range(2):
                        u = bank[4 + 2 * (i % 2) + j][:, hp * P:(hp + 1) * P]
                        if c == 0:
                            step(dve.tensor_scalar(S[:, hp, :], u, el[:, hp, :], None, ALU.mult))
                        else:
                            step(dve.tensor_scalar(tmpU[:, hp, :], u, el[:, hp, :], None, ALU.mult))
                            step(dve.scalar_tensor_tensor(out=S[:, hp, :], in0=S[:, hp, :], scalar=gl[:, hp, c:c + 1],
                                                          in1=tmpU[:, hp, :], op0=ALU.mult, op1=ALU.add))
                dve.nop().then_inc(U_used, 1)

            def go_out(i):
                dve.wait_ge(go_sq, i + 1)
                dve.wait_ge(silu_ready, 1)
                gv = z(C_GR, i).rearrange("p (h e v) -> p h e v", h=2, e=2)
                for h2 in range(2):
                    ins = dve.tensor_tensor(gv[:, :, h2, :], gv[:, :, h2, :],
                                            bank[2 * (i % 2) + h2][:, 0:256].rearrange("p (h v) -> p h v", h=2), ALU.mult)
                    ins.then_inc(go_ready, 1)

            for i in range(NT):
                masked(i)
                if i < NP:
                    states(i)
                else:
                    dve.nop().then_inc(sp_ready, 1)
                    for hp in range(2):
                        dve.wait_ge(Ss_ready, 2)
                        step(dve.tensor_tensor(S0[:, :, hp, :], S0[:, :, hp, :], bc(gl[:, hp, 8:16], [P, NB, DV]), ALU.mult))
                    for b2 in range(4):
                        dve.wait_ge(U_done, NP + b2 + 1)
                        for hp in range(2):
                            u = bank[4 + b2][:, :].rearrange("p (b h v) -> p b h v", b=2, h=2)[:, :, hp, :]
                            els2 = els[:, hp, 2 * b2:2 * b2 + 2]
                            step(dve.tensor_tensor(tmpS[:, :, hp, :], u, bc(els2, [P, 2, DV]), ALU.mult))
                            step(dve.tensor_tensor(S0[:, 2 * b2:2 * b2 + 2, hp, :], S0[:, 2 * b2:2 * b2 + 2, hp, :],
                                                   tmpS[:, :, hp, :], ALU.add))
                    dve.nop().then_inc(ss_ready, 1)
                if i:
                    go_out(i - 1)
            go_out(NP)
            items = [(i, h) for i in range(NP) for h in range(H)]
            NI = len(items)
            dve.wait_ge(att_zero, 2)

            def maxes(m):
                i, h = items[m]
                L = (i + 1) * P
                dve.wait_ge(s_done, m + 1)
                if m >= 2:
                    dve.wait_ge(e_ready, 2 * (m - 1))
                for mm in range(2):
                    ins = dve.tensor_reduce(mx[:, m % 2, mm:mm + 1], bank[2 * (m % 2) + mm][:, 0:L], AX.X, ALU.max)
                step(ins)
                dve.tensor_scalar(nm[:, m % 2, :], mx[:, m % 2, :], -DH ** -0.5, None, ALU.mult).then_inc(nm_ready, 1)

            def combine(m):
                i, h = items[m]
                L = (i + 1) * P
                e0, e1 = E[m % NER][0][:, 0:L], E[m % NER][1][:, 0:L]
                dve.wait_ge(e_ready, 2 * m + 2)
                step(dve.reciprocal(ri[:, m % 2, :], es[:, m % 2, :]))
                step(dve.tensor_scalar(e1, e1, ri[:, m % 2, 1:2], nlam[:, 0:1], ALU.mult, ALU.mult))
                dve.scalar_tensor_tensor(out=e0, in0=e0, scalar=ri[:, m % 2, 0:1], in1=e1,
                                         op0=ALU.mult, op1=ALU.add).then_inc(p_ready, 1)

            def ao_out(i, src):
                dve.wait_ge(o_sq, i + 1)
                dve.tensor_copy(z(C_Q, i), src[:, :]).then_inc(ao_ready, 1)

            for m in range(NI + 3):
                if m < NI:
                    maxes(m)
                if 1 <= m <= NI:
                    combine(m - 1)
                if m >= 3 and (m - 3) % H == H - 1:
                    i = (m - 3) // H
                    ao_out(i, bank[6 + i % 2])
            dve.wait_ge(qkT_ready, 2 * NT)
            for mm in range(2):
                for h in range(H):
                    src = qT[64 * mm:64 * mm + 64, h, 512:640].rearrange("p (b q) -> p b q", b=NB)
                    ins = dve.tensor_copy(qbd[64 * mm:64 * mm + 64, :, h, mm, :], src)
            ins.then_inc(qbd_ready, 1)

            def d_max(b):
                dve.wait_ge(d_s_done, b + 1)
                if b >= 2:
                    dve.wait_ge(d_e_ready, 2 * (b - 1))
                dve.tensor_reduce(mx[:, b % 2, 0:1], bank[2 * (b % 2)][:, :], AX.X, ALU.max)
                step(dve.tensor_reduce(mx[:, b % 2, 1:2], bank[2 * (b % 2) + 1][:, 0:Q], AX.X, ALU.max))
                dve.tensor_scalar(nm[:, b % 2, 0:1], mx[:, b % 2, 0:1], mx[:, b % 2, 1:2], -DH ** -0.5,
                                  ALU.max, ALU.mult).then_inc(d_nm_ready, 1)

            def d_comb(b):
                dve.wait_ge(d_e_ready, 2 * b + 2)
                if b >= 2:
                    dve.wait_ge(d_pt_done, b - 1)
                step(dve.tensor_tensor(ri[:, b % 2, 0:1], es[:, b % 2, 0:1], es[:, b % 2, 1:2], ALU.add))
                step(dve.reciprocal(ri[:, b % 2, 1:2], ri[:, b % 2, 0:1]))
                cv = Cb[:, b % 2, :].rearrange("p (h e q) -> p h e q", h=H, e=2)[:, :, b % 2, :]
                dve.tensor_scalar(cv, Cm[:, :].rearrange("p (h q) -> p h q", h=H), ri[:, b % 2, 1:2], None,
                                  ALU.mult).then_inc(cb_ready, 1)

            for b in range(NB + 1):
                if b < NB:
                    d_max(b)
                if b >= 1:
                    d_comb(b - 1)
            ao_out(NP, bank[6])
            dve.wait_ge(ostd, 1)
            dve.wait_ge(go_ready, 2 * NT)
            dve.wait_ge(ao_ready, NT)
            step(dve.reciprocal(ro[:, :, :], ro[:, :, :]))
            for i in range(NT):
                for c, a in ((C_Q, 0), (C_GR, H)):
                    v = z(c, i).rearrange("p (h v) -> p h v", h=H)
                    dve.tensor_tensor(v, v, bc(ro[:, i, a:a + H], [P, H, DV]), ALU.mult).then_inc(mix_ready, 1)
                if i >= 1:
                    dve.wait_ge(mT_done, 2 * i - 1)
                    dve.tensor_scalar(mixT[:, 0:H, (i - 1) * P:i * P],
                                      bank[2 * ((i - 1) % 2)][:, :].rearrange("p (c t) -> p c t", c=H),
                                      ag8[:, 0:1], None, ALU.mult).then_inc(mT_a, 1)
            dve.wait_ge(mT_done, 2 * NT - 1)
            for b2 in range(NB // 2):
                ins = dve.tensor_scalar(mixT[:, 0:H, NP * P + 32 * b2:NP * P + 32 * b2 + 32],
                                        bank[0][:, b2 * P:(b2 + 1) * P].rearrange("p (h t) -> p h t", h=H),
                                        ag8[:, 0:1], None, ALU.mult)
            ins.then_inc(mT_a, 1)

            def h2_out(i):
                for q in range(2):
                    dve.wait_ge(h2_done, 2 * i + q + 1)
                    if i >= 2:
                        dve.wait_ge(lg_done, i - 1)
                    dve.tensor_tensor(h2T[i % 2][:, 4 * q:4 * q + 4, :],
                                      bank[q][:, :].rearrange("p (c t) -> p c t", c=4),
                                      bc(g2[:, 4 * q:4 * q + 4], [P, 4, P]), ALU.mult).then_inc(h2_ready, 1)

            for i in range(NT):
                for hf in range(2):
                    dve.wait_ge(out_done, 2 * i + hf + 1)
                    ins = dve.tensor_tensor(X[:, i, hf * 512:(hf + 1) * 512], X[:, i, hf * 512:(hf + 1) * 512],
                                            bank[4 + 2 * (i % 2) + hf][:, :], ALU.add)
                    ins.then_inc(x2_ready, 1)
                dve.wait_ge(x2_ready, 2 * i + 2)
                if i >= 2:
                    dve.wait_ge(st_hn[i % 2], 16 * (i // 2))
                    dve.wait_ge(h2_done, 2 * (i - 1))
                dve.tensor_tensor_reduce(out=hn[i % 2], in0=X[:, i, :], in1=X[:, i, :], scale=1.0, scalar=0.0,
                                         op0=ALU.mult, op1=ALU.add, accum_out=ss2[:, i:i + 1]).then_inc(ssq2, 1)
                dve.wait_ge(std2, i + 1)
                dve.reciprocal(r2[:, i:i + 1], st2[:, i:i + 1]).then_inc(rstd2, 1)
                h2_out(i)
            step(dve.memset(Rt, 0.0))
            dve.wait_ge(lg_done, NT)
            step(dve.memset(Ms[:, NT * NE:], 0.0))
            step(dve.tensor_tensor(Lg, bank[3][:, 0:NT * NL].rearrange("p (i n) -> p i n", i=NT),
                                   br[:, :].unsqueeze(1).broadcast_to([P, NT, NL]), ALU.add))
            gl4 = Lg[:, :, 0:NG]
            ev = Lg[:, :, NG:NL].rearrange("p i (g e) -> p i g e", g=NG)

            def first_max(val, mxout, ohout, m2, w):
                step(dve.tensor_reduce(mxout, val, AX.X, ALU.max))
                step(dve.tensor_tensor(ohout, val, bc(mxout, [P, NT, w]), ALU.is_equal))
                step(dve.tensor_tensor(ohout, ohout, desc[:, 0:w].unsqueeze(1).broadcast_to([P, NT, w]), ALU.mult))
                step(dve.tensor_reduce(m2, ohout, AX.X, ALU.max))
                step(dve.tensor_tensor(ohout, ohout, bc(m2, [P, NT, w]), ALU.is_equal))

            first_max(gl4, gmax, goh, gm2, NG)
            dve.tensor_tensor(ge, gl4, bc(gmax, [P, NT, NG]), ALU.subtract).then_inc(gexp_in, 1)
            step(dve.tensor_tensor(egs, ev, bc(goh, [P, NT, NG, EPG]), ALU.mult))
            step(dve.tensor_reduce(esel[0], egs.rearrange("p i g e -> p i e g"), AX.X, ALU.add))
            first_max(esel[0], mk[:, 0], oh[0], mk2, EPG)
            step(dve.scalar_tensor_tensor(out=esel[1], in0=oh[0], scalar=NEG, in1=esel[0], op0=ALU.mult, op1=ALU.add))
            first_max(esel[1], mk[:, 1], oh[1], mk2, EPG)
            dve.tensor_tensor(dm, mk[:, 1], mk[:, 0], ALU.subtract).then_inc(gexp_in, 1)
            for k in range(2):
                ins = dve.tensor_tensor(M[:, k], bc(goh, [P, NT, NG, EPG]),
                                        oh[k].unsqueeze(2).broadcast_to([P, NT, NG, EPG]), ALU.mult)
            step(ins)
            Mf = M.rearrange("p k i g e -> p k (i g e)")
            dve.tensor_tensor(Ms[:, 0:NT * NE], Mf[:, 0], Mf[:, 1], ALU.add).then_inc(m_ready, 1)
            dve.wait_ge(gexp_out, 2)
            step(dve.tensor_reduce(gs, ge, AX.X, ALU.add))
            step(dve.scalar_tensor_tensor(out=den, in0=dm, scalar=1.0, in1=gs, op0=ALU.add, op1=ALU.mult))
            step(dve.reciprocal(wk[:, 0, :], den))
            step(dve.tensor_tensor(wk[:, 1, :], wk[:, 0, :], dm, ALU.mult))
            for k in range(2):
                mf = M[:, k].rearrange("p i g (n e) -> p i (g n) e", e=2)
                dve.tensor_reduce(pk[:, k], mf[:, :, :, 1], AX.X, ALU.add)
                ins = dve.tensor_reduce(Mp[:, 1, k], mf, AX.X, ALU.add)
            step(ins)
            for k in range(2):
                ins = dve.tensor_tensor(Mp[:, 0, k], Mp[:, 1, k], bc(tk[:, 0, k, :], [P, NT, PAIRS]), ALU.mult)
            step(ins)
            for k in range(2):
                ins = dve.tensor_tensor(Mp[:, 1, k], Mp[:, 1, k], bc(tk[:, 1, k, :], [P, NT, PAIRS]), ALU.mult)
            step(ins)
            dve.wait_ge(rank_done, 1)
            step(dve.tensor_tensor(mprod, Mf, bank[0][:, 0:NT * NE].unsqueeze(1).broadcast_to([P, 2, NT * NE]),
                                   ALU.mult))
            step(dve.tensor_reduce(rk, mprod.rearrange("p k (i n) -> p k i n", i=NT), AX.X, ALU.add))
            dve.tensor_reduce(cnt, bank[0][:, NT * NE:(NT + 1) * NE], AX.X, ALU.max)
            step(dve.tensor_tensor(cmpr, bc(rk.rearrange("p k i -> p (k i)"), [P, 2 * NT, ROUNDS - 1]),
                                   thr[:, :].unsqueeze(1).broadcast_to([P, 2 * NT, ROUNDS - 1]), ALU.is_ge))
            step(dve.tensor_reduce(rn.rearrange("p k i -> p (k i)"), cmpr, AX.X, ALU.add))
            step(dve.scalar_tensor_tensor(out=loc, in0=rn, scalar=-float(CAP), in1=rk, op0=ALU.mult, op1=ALU.add))
            step(dve.scalar_tensor_tensor(out=qk, in0=pk, scalar=float(CAP), in1=loc, op0=ALU.mult, op1=ALU.add))
            step(dve.tensor_tensor(OH, iota128[:, :].unsqueeze(1).broadcast_to([P, 2 * NT, P]),
                                   bc(qk.rearrange("p k i -> p (k i)"), [P, 2 * NT, P]), ALU.is_equal))
            TS = 4

            def tables(r, later):
                def tstep(k, ins):
                    ins.then_inc(tab_step, 1)
                    dve.wait_ge(tab_step, r * TS + k)

                if later:
                    for q in range(2):
                        dve.wait_ge(st_y[q], r * (PAIRS // 2 * 16))
                tstep(1, dve.tensor_scalar(rmask, rn, cur[:, 0:1], None, ALU.is_equal))
                tstep(2, dve.tensor_scalar(cur[:, :], cur[:, :], 1.0, None, ALU.add))
                for a in range(2):
                    for k in range(2):
                        ins = dve.tensor_tensor(Rt[:, k, :, a, 0:PAIRS], Mp[:, a, k], bc(rmask[:, k], [P, NT, PAIRS]),
                                                ALU.mult)
                tstep(3, ins)
                dve.nop().then_inc(tab_in, 1)
                if not later:
                    step(dve.tensor_scalar(ovf_f, cnt, float(CAP), None, ALU.is_gt))
                    dve.tensor_copy(ovf[:, :], ovf_f).then_inc(ovf_ready, 1)
                dve.wait_ge(tab_done, r + 1)
                n1 = PAIRS + 1
                tstep(4, dve.tensor_scalar(none, bank[0][:, 0:2 * n1], 0.0, 4096.0, ALU.is_equal, ALU.mult))
                for t, a in ((dst, n1), (idx, 0)):
                    ins = dve.scalar_tensor_tensor(out=t[:, :], in0=bank[0][:, a:a + n1], scalar=-1.0,
                                                   in1=none[:, a:a + n1], op0=ALU.add, op1=ALU.add)
                ins.then_inc(idx_ready, 1)

            def xsT_out(r, p, q):
                for hf in range(2):
                    dve.wait_ge(xsT_done, r * 2 * (PAIRS + 1) + 2 * p + hf + 1)
                    dve.tensor_tensor(xsT[q][:, 4 * hf:4 * hf + 4, :],
                                      bank[hf][:, :].rearrange("p (c s) -> p c s", c=4),
                                      bc(g2[:, 4 * hf:4 * hf + 4], [P, 4, P]), ALU.mult).then_inc(xsT_ready, 1)

            def gated(r, g, q):
                dve.wait_ge(sil_ready, (r * 8 + g) * 2 + q + 1)
                dve.tensor_tensor(hs[q], sil[q], bank[2 + q][:, FE:2 * FE], ALU.mult).then_inc(h_ready, 1)

            def moe(r, later):
                tables(r, later)
                xsT_out(r, 0, 0)
                with dve.Fori(0, NE // 4) as g:
                    gated(r, g, 0)
                    xsT_out(r, 2 * g + 1, 1)
                    gated(r, g, 1)
                    xsT_out(r, 2 * g + 2, 0)

            moe(0, False)
            dve.wait_ge(ovf_ready, 1)
            with dve.If(dve.value_load(ovf[0:1, 0:1]) > 0):
                with dve.Fori(1, ROUNDS) as r:
                    moe(r, True)
            for i in range(NT):
                dve.wait_ge(ygath[i % NYG], (i // NYG + 1) * 16)
                for k in range(2):
                    if 2 * i + k:
                        dve.wait_ge(ysum, 2 * i + k)
                    dve.scalar_tensor_tensor(out=X[:, i, :], in0=yg[i % NYG][:, k * D:(k + 1) * D],
                                             scalar=wk[:, k, i:i + 1], in1=X[:, i, :], op0=ALU.mult,
                                             op1=ALU.add).then_inc(ysum, 1)

        @block.tensor
        def _(pe):
            pe.wait_ge(consts, 1)

            def ga(i):
                pe.wait_ge(hT_ready, 2 * i + 2)
                for c in range(DC):
                    ins = pe.matmul(bank[5][:, i * RANK:(i + 1) * RANK], hT[:, c, i, :], wga[:, c, :],
                                    start=(c == 0), stop=(c == DC - 1))
                return ins

            for i in range(NT):
                pe.wait_ge(xn_ready, i + 1)
                if i >= 2:
                    pe.wait_ge(hT_ready, 2 * (i - 1))
                for q in range(2):
                    for c in range(4):
                        ins = pe.transpose(bank[2 * (i % 2) + q][:, c * P:(c + 1) * P],
                                           xn[i % 2][:, (4 * q + c) * P:(4 * q + c + 1) * P], ident[:, :])
                    ins.then_inc(xT_done, 1)
                if i == 0:
                    pe.wait_ge(ld_small, 6 * 16)
                if i >= 1:
                    ga(i - 1).then_inc(ga_done, 1)
            ga(NT - 1).then_inc(ga_done, 1)
            pe.wait_ge(zga_ready, 1)
            for i in range(NT):
                dst = bank[6][0:RANK, i * P:(i + 1) * P] if i < 4 else bank[7][0:RANK, 0:P]
                ins = pe.transpose(dst, zga[:, i, :], ident[:, :])
            ins.then_inc(gaT_done, 1)
            pe.wait_ge(gaT_ready, 2)
            for i in range(NT):
                ins = pe.matmul(bank[5 + i // 2][:, (i % 2) * 256:(i % 2) * 256 + 256],
                                gaT[0:RANK + 1, i * P:(i + 1) * P], wa2[0:RANK + 1, :], start=True, stop=True)
            ins.then_inc(pre_done, 1)

            pe.wait_ge(hL_ready, NT)
            with pe.Fori(0, 6) as c:
                for k in range(2):
                    pe.wait_ge(wL_ready, 2 * c + k + 1)
                    for i in range(NT):
                        if k == 0:
                            pe.wait_ge(z_free, NT * c + i + 1)
                        for s in range(DC // 2):
                            cols = slice(s * 512, (s + 1) * 512)
                            d = k * DC // 2 + s
                            pe.matmul(bank[i][:, :], hH[:, d, i, :], wH[k][:, cols], start=(d == 0), stop=False)
                            pe.matmul(bank[i][:, :], hH[:, d, i, :], wL[k][:, cols], start=False, stop=False)
                            ins = pe.matmul(bank[i][:, :], hL[:, d, i, :], wH[k][:, cols], start=False,
                                            stop=(d == DC - 1))
                        if k == 1:
                            ins.then_inc(proj_done, 1)
                    if k == 0:
                        ins.then_inc(half_done, 1)

            pe.wait_ge(la_ready, 1)
            for i in range(NT):
                for hp in range(2):
                    o = (i % 2) * 256 + hp * P
                    ins = pe.matmul(bank[5 + i // 2][:, o:o + P], la[:, i, hp * P:(hp + 1) * P],
                                    (tri64 if i < NP else tri16)[:, :], start=True, stop=True)
            ins.then_inc(b_done, 1)
            for m in range(2 * NT):
                i = m % NT
                if m < NT:
                    pe.wait_ge(k_ready, i + 1)
                else:
                    pe.wait_ge(q_ready, i + 1)
                if m < 4:
                    pe.wait_ge(z_free, 5 + 25 + m + 1)
                else:
                    pe.wait_ge(qkT_ready, m - 3)
                for h in range(H):
                    ins = pe.transpose(bank[m % 4][:, h * P:(h + 1) * P],
                                       z(C_K if m < NT else C_Q, i, h * P, (h + 1) * P), ident[:, :])
                ins.then_inc(qkT_done, 1)

            def g_tr(i):
                if i == 0:
                    pe.wait_ge(z_free, 5 + 30)
                    pe.wait_ge(b_ready, 3)
                if i >= 2:
                    pe.wait_ge(gqk_ready, 2 * (i - 1))
                for t in range(4):
                    ins = pe.transpose(bank[4 + i % 2][:, t * P:(t + 1) * P], z(C_G, i, t * P, (t + 1) * P), ident[:, :])
                ins.then_inc(gT_done, 1)

            def ktok_tr(i):
                pe.wait_ge(gqk_ready, 2 * i + 2)
                if i >= 2:
                    pe.wait_ge(ktok_ready, i - 1)
                for hp in range(2):
                    ins = pe.transpose(bank[6 + i % 2][:, hp * P:(hp + 1) * P], kt[:, hp, i * P:(i + 1) * P], ident[:, :])
                ins.then_inc(ktok_done, 1)

            g_tr(0)
            for i in range(NT):
                if i + 1 < NT:
                    g_tr(i + 1)
                ktok_tr(i)

            def scores(i):
                if i < 2:
                    pe.wait_ge(qkT_ready, 2 * NT)
                else:
                    pe.wait_ge(go_sq, i - 1)
                    pe.wait_ge(go_ready, 2 * (i - 1))
                for h2 in range(2):
                    rows = slice(64 * h2, 64 * h2 + 64)
                    for hp in range(2):
                        ins = pe.matmul(bank[2 * (i % 2) + h2][:, hp * P:(hp + 1) * P], kt[rows, hp, i * P:(i + 1) * P],
                                        qt[rows, hp, i * P:(i + 1) * P], start=True, stop=True)
                    ins.then_inc(sc_done, 1)

            def updates(i):
                pe.wait_ge(ktok_ready, NT)
                if i >= 2:
                    pe.wait_ge(U_used, i - 1)
                for j in range(2):
                    rows = slice(64 * j, 64 * j + 64)
                    for hp in range(2):
                        for h2 in range(2):
                            o = hp * P + 64 * h2
                            ins = pe.matmul(bank[4 + 2 * (i % 2) + j][64 * h2:64 * h2 + 64, hp * P:(hp + 1) * P],
                                            ktok[rows, i, o:o + 64],
                                            z(C_GV, i)[rows, (2 * hp + h2) * P:(2 * hp + h2 + 1) * P],
                                            start=True, stop=True)
                ins.then_inc(U_done, 1)

            def s_updates(b2):
                pe.wait_ge(kz_ready, NB)
                if b2 == 0:
                    pe.wait_ge(U_used, NP)
                for b in (2 * b2, 2 * b2 + 1):
                    for hp in range(2):
                        for h2 in range(2):
                            o = hp * P + 64 * h2
                            c = (b % 2) * 256 + hp * P
                            ins = pe.matmul(bank[4 + b2][64 * h2:64 * h2 + 64, c:c + P], kz[:, b, o:o + 64],
                                            z(C_GV, NP, (2 * hp + h2) * P, (2 * hp + h2 + 1) * P), start=True, stop=True)
                ins.then_inc(U_done, 1)

            def outputs(i):
                pe.wait_ge(AT_ready, 2 * i + 2)
                if i < NP:
                    pe.wait_ge(St_ready, 2 * i + 2)
                else:
                    pe.wait_ge(Ss_ready, 2)
                    pe.wait_ge(qz_ready, 2)
                for h2 in range(2):
                    rows = slice(64 * h2, 64 * h2 + 64)
                    for hp in range(2):
                        o = bank[2 * (i % 2) + h2]
                        v = slice(hp * P, (hp + 1) * P)
                        h = 2 * hp + h2
                        pe.matmul(o[:, v], AT[:, i, hp, h2, :], z(C_GV, i, h * P, (h + 1) * P), start=True, stop=False,
                                  skip_group_check=True)
                        if i < NP:
                            for j in range(2):
                                if 2 * i + j:
                                    t = i * P + j * CHUNK
                                    ins = pe.matmul(o[64 * j:64 * j + 64, v], qt[rows, hp, t:t + CHUNK],
                                                    St[rows, 2 * i + j, hp, :], start=False, stop=True,
                                                    skip_group_check=True)
                        else:
                            for b in range(NB):
                                ins = pe.matmul(o[:, v], qz[rows, hp, b, :], Ss[rows, b, hp, :], start=False,
                                                stop=(b == NB - 1), skip_group_check=True)
                ins.then_inc(go_done, 1)

            for i in range(NT):
                scores(i)
                if i < NP:
                    updates(i)
                else:
                    for b2 in range(4):
                        s_updates(b2)
                if i:
                    outputs(i - 1)
            outputs(NP)

            items = [(i, h) for i in range(NP) for h in range(H)]
            NI = len(items)

            def att_scores(m):
                i, h = items[m]
                L = (i + 1) * P
                if m < 2:
                    pe.wait_ge(go_sq, NT)
                    pe.wait_ge(go_ready, 2 * NT)
                else:
                    pe.wait_ge(e_ready, 2 * (m - 1))
                for mm in range(2):
                    rows = slice(64 * mm, 64 * mm + 64)
                    o = bank[2 * (m % 2) + mm]
                    pe.matmul(o[:, 0:L], qT[rows, h, i * P:(i + 1) * P], kT[rows, h, 0:L], start=True, stop=False,
                              skip_group_check=True)
                    ins = pe.matmul(o[:, L - CHUNK:L], mA[rows, :], mB[rows, :], start=False, stop=True,
                                    skip_group_check=True)
                ins.then_inc(s_done, 1)

            def att_pt(m):
                i, h = items[m]
                pe.wait_ge(p_ready, m + 1)
                if m >= 2:
                    pe.wait_ge(pt_ready, m - 1)
                else:
                    pe.wait_ge(ss_ready, 1)
                for j in range(i + 1):
                    ins = pe.transpose(bank[4 + m % 2][:, j * P:(j + 1) * P], E[m % NER][0][:, j * P:(j + 1) * P],
                                       ident[:, :])
                ins.then_inc(pt_done, 1)

            def att_pv(m):
                i, h = items[m]
                pe.wait_ge(pt_ready, m + 1)
                if h == 0 and i >= 2:
                    pe.wait_ge(o_sq, i - 1)
                    pe.wait_ge(ao_ready, i - 1)
                for j in range(i + 1):
                    ins = pe.matmul(bank[6 + i % 2][:, h * P:(h + 1) * P], PT[m % 2][:, j * P:(j + 1) * P],
                                    z(C_V, j, h * P, (h + 1) * P), start=(j == 0), stop=(j == i))
                ins.then_inc(o_done, 1)

            for m in range(NI + 3):
                if m < NI:
                    att_scores(m)
                if 2 <= m < NI + 2:
                    att_pt(m - 2)
                if m >= 3:
                    att_pv(m - 3)

            def d_scores(b):
                pe.wait_ge(ld_k[b % NKV], 16 * (b // NKV + 1))
                if b < 2:
                    pe.wait_ge(e_ready, 2 * NI)
                    pe.wait_ge(qbd_ready, 1)
                else:
                    pe.wait_ge(d_e_ready, 2 * (b - 1))
                w = [qbd[:, b, h, :, :].rearrange("p m q -> p (m q)") for h in range(H)]
                for h in range(H):
                    pe.matmul(bank[2 * (b % 2)][32 * h:32 * h + 32, :], w[h], Kc[b % NKV][:, h, :], start=True, stop=True,
                              tile_position=(0, 32 * h))
                for h in range(H):
                    ins = pe.matmul(bank[2 * (b % 2) + 1][32 * h:32 * h + 32, 0:Q], w[h],
                                    kT[:, h, 512 + b * Q:512 + (b + 1) * Q], start=True, stop=True,
                                    tile_position=(0, 32 * h))
                ins.then_inc(d_s_done, 1)

            def d_pt(b):
                pe.wait_ge(cb_ready, b + 1)
                if b >= 2:
                    pe.wait_ge(d_pt_ready, 2 * (b - 1))
                else:
                    pe.wait_ge(pt_ready, NI)
                for j in range(4):
                    pe.matmul(bank[4 + b % 2][:, j * P:(j + 1) * P], E[b % NER][0][:, j * P:(j + 1) * P],
                              Cb[:, b % 2, :], start=True, stop=True)
                if b == 0:
                    pe.wait_ge(o_sq, NP)
                    pe.wait_ge(ao_ready, NP)
                else:
                    pe.wait_ge(d_pt_ready, 2 * b)
                pe.matmul(bank[7][:, 0:P], enew[:, b, :], Cb[:, b % 2, :], start=True, stop=True).then_inc(d_pt_done, 1)

            def d_pv(b):
                pe.wait_ge(d_pt_ready, 2 * b + 2)
                pe.wait_ge(ld_v[b % NKV], 16 * (b // NKV + 1))
                for j in range(5):
                    for h in range(H):
                        rhs = Vc[b % NKV][:, j, h * P:(h + 1) * P] if j < 4 else z(C_V, NP, h * P, (h + 1) * P)
                        o = j * P + 32 * h
                        ins = pe.matmul(bank[6][32 * h:32 * h + 32, (b // 2) * P:(b // 2 + 1) * P],
                                        PT[b % 2][:, o:o + 32], rhs, start=(b % 2 == 0 and j == 0),
                                        stop=(b % 2 == 1 and j == 4), tile_position=(0, 32 * h), skip_group_check=True)
                ins.then_inc(d_pv_done, 1)

            for b in range(NB + 3):
                if b < NB:
                    d_scores(b)
                if 2 <= b < NB + 2:
                    d_pt(b - 2)
                if b >= 3:
                    d_pv(b - 3)

            for i in range(NT):
                for q, c in ((0, C_Q), (1, C_GR)):
                    pe.wait_ge(mix_ready, 2 * i + q + 1)
                    if i >= 2:
                        pe.wait_ge(mT_a, i - 1)
                        pe.wait_ge(mT_g, i - 1)
                    for h in range(H):
                        ins = pe.transpose(bank[2 * (i % 2) + q][:, h * P:(h + 1) * P], z(c, i, h * P, (h + 1) * P),
                                           ident[:, :])
                    ins.then_inc(mT_done, 1)
            pe.wait_ge(ld_wo, 4 * 16)

            def out_proj(i, hf):
                if hf == 0:
                    pe.wait_ge(mT_a, i + 1)
                    pe.wait_ge(mT_g, i + 1)
                if i >= 2:
                    pe.wait_ge(x2_ready, 2 * (i - 2) + hf + 1)
                for c in range(DC):
                    ins = pe.matmul(bank[4 + 2 * (i % 2) + hf][:, :], mixT[:, c, i * P:(i + 1) * P],
                                    wo[:, c, hf * 512:(hf + 1) * 512], start=(c == 0), stop=(c == DC - 1))
                ins.then_inc(out_done, 1)

            def h2_tr(i):
                pe.wait_ge(hn_ready, i + 1)
                if i == 0:
                    pe.wait_ge(mT_a, NT)
                    pe.wait_ge(mT_g, NT)
                for q in range(2):
                    if i >= 1:
                        pe.wait_ge(h2_ready, 2 * (i - 1) + q + 1)
                    for c in range(4):
                        ins = pe.transpose(bank[q][:, c * P:(c + 1) * P], hn[i % 2][:, (4 * q + c) * P:(4 * q + c + 1) * P],
                                           ident[:, :])
                    ins.then_inc(h2_done, 1)

            def router(i):
                pe.wait_ge(h2_ready, 2 * i + 2)
                for c in range(DC):
                    ins = pe.matmul(bank[3][:, i * NL:(i + 1) * NL], h2T[i % 2][:, c, :], wr[:, c, :],
                                    start=(c == 0), stop=(c == DC - 1))
                ins.then_inc(lg_done, 1)

            for hf in range(2):
                out_proj(0, hf)
            for i in range(NT):
                if i + 1 < NT:
                    out_proj(i + 1, 0)
                h2_tr(i)
                if i + 1 < NT:
                    out_proj(i + 1, 1)
                router(i)
            pe.wait_ge(m_ready, 1)
            pe.matmul(bank[0][:, 0:(NT + 1) * NE], strict[:, :], Ms, start=True, stop=False, skip_group_check=True)
            for d in range(1, NT + 1):
                ins = pe.matmul(bank[0][:, d * NE:(NT + 1) * NE], ones[:, :], Ms[:, 0:(NT + 1 - d) * NE],
                                start=False, stop=(d == NT), skip_group_check=True)
            ins.then_inc(rank_done, 1)

            def tables(r):
                pe.wait_ge(tab_in, r + 1)
                for m in range(2 * NT):
                    ins = pe.matmul(bank[0][:, 0:2 * (PAIRS + 1)], OH[:, m, :],
                                    Rt[:, m // NT, m % NT].rearrange("p a n -> p (a n)"), start=(m == 0),
                                    stop=(m == 2 * NT - 1))
                ins.then_inc(tab_done, 1)

            def xs_tr(r, p, q, half_p):
                pe.wait_ge(gath[q], (r * (PAIRS // 2 + 1 - q) + half_p + 1) * 16)
                for hf in range(2):
                    if not (isinstance(p, int) and isinstance(r, int) and p == 0 and r == 0):
                        pe.wait_ge(xsT_ready, (r * (PAIRS + 1) + p) * 2 + hf - 1)
                    for c in range(4):
                        ins = pe.transpose(bank[hf][:, c * P:(c + 1) * P],
                                           xs[q][:, (4 * hf + c) * P:(4 * hf + c + 1) * P], ident[:, :])
                    ins.then_inc(xsT_done, 1)

            def gate_up(r, g, q):
                for j in range(2):
                    pe.wait_ge(ld_gu[2 * q + j], (r * 8 + g + 1) * 16)
                pe.wait_ge(xsT_ready, (r * (PAIRS + 1) + 2 * g + q + 1) * 2)
                for c in range(DC):
                    for j in range(2):
                        ins = pe.matmul(bank[2 + q][CAP * j:CAP * j + CAP, :], xsT[q][:, c, j * CAP:(j + 1) * CAP],
                                        egu[2 * q + j][:, c, :], start=(c == 0), stop=(c == DC - 1),
                                        tile_position=(0, CAP * j))
                ins.then_inc(gu_done, 1)

            def hidden_tr(r, g, q):
                pe.wait_ge(h_ready, (r * 8 + g) * 2 + q + 1)
                for f in range(2):
                    ins = pe.transpose(bank[2 + q][:, f * P:(f + 1) * P], hs[q][:, f * P:(f + 1) * P], ident[:, :])
                ins.then_inc(hT_done, 1)

            def down_proj(r, g, q, first):
                pe.wait_ge(hTs_ready, (r * 8 + g) * 2 + q + 1)
                for j in range(2):
                    pe.wait_ge(ld_dn[2 * q + j], (r * 8 + g + 1) * 16)
                if not first:
                    pe.wait_ge(ysb_ready, r * 2 * PAIRS + g * 4 + 2 * q - 2)
                for hf in range(2):
                    for f in range(2):
                        for j in range(2):
                            ins = pe.matmul(bank[4 + 2 * q + hf][CAP * j:CAP * j + CAP, :],
                                            hTs[q][:, f, j * CAP:(j + 1) * CAP],
                                            edn[2 * q + j][:, f, hf * 512:(hf + 1) * 512], start=(f == 0),
                                            stop=(f == 1), tile_position=(0, CAP * j))
                ins.then_inc(dn_done, 1)

            def group(r, g, first=False):
                gate_up(r, g, 0)
                xs_tr(r, 2 * g + 1, 1, g)
                hidden_tr(r, g, 0)
                gate_up(r, g, 1)
                down_proj(r, g, 0, first)
                xs_tr(r, 2 * g + 2, 0, g + 1)
                hidden_tr(r, g, 1)
                down_proj(r, g, 1, first)

            tables(0)
            xs_tr(0, 0, 0, 0)
            group(0, 0, first=True)
            with pe.Fori(1, NE // 4) as g:
                group(0, g)
            pe.wait_ge(ovf_ready, 1)
            with pe.If(pe.value_load(ovf[0:1, 0:1]) > 0):
                with pe.Fori(1, ROUNDS) as r:
                    tables(r)
                    xs_tr(r, 0, 0, 0)
                    with pe.Fori(0, NE // 4) as g:
                        group(r, g)


_OUTS = [("y_out", (NT, P, D)), ("k_out", (NT, P, 512)), ("v_out", (NT, P, 512)),
         ("sp_out", (P, 2, DV)), ("ss_out", (P, NB, 2, DV))]


def kernel(x_prompt, x_sample, cache_k, cache_v, state_gla, norm1_gain, w_in, a_q_gain, a_k_gain,
           lambda_q1, lambda_k1, lambda_q2, lambda_k2, a_out_gain, w_a2, b_a, g_out_gain, w_out,
           norm2_gain, w_group, b_group, w_erouter, b_erouter, w_gate, w_up, w_down):
    import numpy as np
    import concourse.bacc as bacc
    from concourse.bass_utils import run_bass_kernel_spmd

    def rows(w):
        return w.reshape(-1, P, w.shape[-1]).transpose(1, 0, 2)

    wi = np.asarray(w_in)[0]
    cuts = np.cumsum([512, 512, 512, 256, 256, 512, RANK])
    aq, ak, av, gq, gk, gv, ga, gr = np.split(wi, cuts, axis=1)
    chunks = [np.concatenate([gq, gk], 1), gv, gr, ak, aq, av]
    x = np.concatenate([np.asarray(x_prompt).reshape(-1, D), np.asarray(x_sample).reshape(-1, D)]).reshape(NT, P, D)
    gains = [np.asarray(norm1_gain)[0].reshape(DC, P).T, np.asarray(norm2_gain)[0].reshape(DC, P).T,
             np.concatenate([np.asarray(a_q_gain)[0]] * 2)[:, None],
             np.asarray(a_out_gain)[0][:, None], np.asarray(g_out_gain)[0][:, None]]
    wg, wu, wd = np.asarray(w_gate)[0], np.asarray(w_up)[0], np.asarray(w_down)[0]
    gu = np.concatenate([wg, wu], 2).reshape(NE, DC, P, 2 * FE).transpose(0, 2, 1, 3)
    ins = {
        "x": x,
        "cache_kt": np.asarray(cache_k)[0].transpose(0, 3, 4, 2, 1).reshape(NB, P, H, PAST),
        "cache_v": np.asarray(cache_v)[0].reshape(NB, 4, P, 512).transpose(0, 2, 1, 3),
        "state": np.asarray(state_gla)[0].reshape(NB, 2, P, DV).transpose(2, 0, 1, 3),
        "w_main": np.stack([rows(c) for c in chunks]).reshape(6 * P, DC * 512),
        "w_ga": rows(ga),
        "w_a2b": np.concatenate([np.asarray(w_a2)[0], np.asarray(b_a)], 0),
        "w_out": rows(np.asarray(w_out)[0]),
        "cols": np.concatenate(gains, 1),
        "k_gain": np.asarray(a_k_gain)[0],
        "lam": np.stack([np.asarray(v)[0] for v in (lambda_q1, lambda_k1, lambda_q2, lambda_k2)]),
        "w_r": rows(np.concatenate([np.asarray(w_group)[0], np.asarray(w_erouter)[0]], 1)),
        "b_r": np.concatenate([np.asarray(b_group)[0], np.asarray(b_erouter)[0]]),
        "w_gu": gu.reshape(NE * P, GU_W),
        "w_dn": wd.reshape(NE, 2, P, D).transpose(0, 2, 1, 3).reshape(NE * P, DN_W),
    }
    ck = np.asarray(cache_k)[0]
    ins["cache_kt"] = ck.transpose(0, 3, 4, 2, 1).reshape(NB, P, H, PAST)
    nc = bacc.Bacc("TRN2", target_bir_lowering=False, num_devices=1)
    arrays, args = {}, []
    for name, a in ins.items():
        a = np.ascontiguousarray(a)
        arrays[f"in_{name}"] = a
        args.append(nc.dram_tensor(f"in_{name}", a.shape, F32, kind="ExternalInput").ap())
    for name, shape in _OUTS:
        args.append(nc.dram_tensor(name, shape, F32, kind="ExternalOutput").ap())
    args.append(nc.dram_tensor("hn_dram", (NT * P, D), F32, kind="Internal").ap())
    args.append(nc.dram_tensor("ye_dram", (2 * NT * P, D), F32, kind="Internal").ap())
    build(nc, *args)
    r = run_bass_kernel_spmd(nc, [arrays], core_ids=[0]).results[0]
    y, k, v, s1, s2 = (r[name] for name, _ in _OUTS)
    y, k, v = y.reshape(NT * P, D), k.reshape(NT * P, 512), v.reshape(NT * P, 512)
    n = NP * P
    return (y[:n].reshape(1, n, D), y[n:].reshape(NB, Q, D),
            k[:n].reshape(1, 1, n, H, 2, DH), v[:n].reshape(1, 1, n, H, DV),
            s1.reshape(2, DH, 2, DV).transpose(2, 0, 1, 3).reshape(1, 1, H, DH, DV),
            k[n:].reshape(1, NB, Q, H, 2, DH), v[n:].reshape(1, NB, Q, H, DV),
            s2.reshape(2, DH, NB, 2, DV).transpose(2, 3, 0, 1, 4).reshape(1, NB, H, DH, DV))
```

```python
from contextlib import ExitStack

import concourse.bass as bass
from concourse import mybir

F32 = mybir.dt.float32
F32R = mybir.dt.float32r
I32 = mybir.dt.int32
U32 = mybir.dt.uint32
ALU = mybir.AluOpType
ACT = mybir.ActivationFunctionType
AX = mybir.AxisListType

P = 128
D = 1024
DC = D // P
NT = 5
NP = 4
CHUNK = 64
NB = 8
Q = 16
PAST = 512
H = 4
DH = 64
DV = 128
RANK = 16
EPS = 1e-6
LAM_INIT = 0.8 - 0.6 * 1.0
NG = 4
EPG = 8
NE = NG * EPG
FE = 256
CAP = 64
PAIRS = NE // 2
ROUNDS = NT * P // CAP
SLOTS = NE * CAP
GU_W = DC * 2 * FE
DN_W = 2 * D
EXP_W = GU_W + DN_W
CW = NT * 512
NEG = -1e30
C_G, C_GV, C_GR, C_K, C_Q, C_V = range(6)


def build(nc, x, cache_kt, cache_v, state, w_main, w_ga, w_a2b, w_out, cols, k_gain, lam, w_r, b_r,
          w_gu, w_dn, y_out, k_out, v_out, sp_out, ss_out, hn_dram, ye_dram):
    ctx = ExitStack()
    with ctx:
        def sb(name, shape, dt=F32):
            return ctx.enter_context(nc.sbuf_tensor(name, shape, dt))

        def sem(name):
            return ctx.enter_context(nc.semaphore(name))

        bank = [ctx.enter_context(nc.psum_tensor(f"bank{i}", [P, 512], F32)) for i in range(8)]

        X = sb("X", [P, NT, D])
        def overlay(name, words):
            with nc.sbuf_tensor(f"{name}_r", [P, words], F32R) as r:
                pass
            return r, sb(name, [P, words])

        Zpad_r, Zpad = overlay("Zpad", EXP_W - 2 * CW + 6 * CW)
        hbuf_r, hbuf = overlay("hbuf", DC * NT * P)
        W_r, W = overlay("W", 8192)
        G_r, G = overlay("G", 8192)
        R0_r, R0 = overlay("R0", EXP_W)
        Z0 = EXP_W - 2 * CW

        def z(c, i, a=0, b=512):
            o = Z0 + c * CW + i * 512
            return Zpad[:, o + a:o + b]

        def zall(c):
            return Zpad[:, Z0 + c * CW:Z0 + (c + 1) * CW]

        ident = sb("ident", [P, P])
        tri64 = sb("tri64", [P, P])
        tri16 = sb("tri16", [P, P])
        strict = sb("strict", [P, P])
        ones = sb("ones", [P, P])
        iota128 = sb("iota128", [P, P])
        iota_i = sb("iota_i", [P, P], I32)
        desc_i = sb("desc_i", [P, EPG], I32)
        desc = sb("desc", [P, EPG])
        thr = sb("thr", [P, ROUNDS - 1])
        tok_i = sb("tok_i", [P, NT], I32)
        tok = sb("tok", [P, NT])
        bmask = sb("bmask", [P, NB])
        C0 = sb("C0", [P, H * Q])
        C1 = sb("C1", [P, H * Q])
        Cm = sb("Cm", [P, H * Q])
        Cb = sb("Cb", [P, 2, P])
        mA = sb("mA", [P, P])
        mB = sb("mB", [P, CHUNK])
        epsc = sb("epsc", [P, 1])
        colt = sb("colt", [P, 2 * DC + 3])
        g1, g2 = colt[:, 0:DC], colt[:, DC:2 * DC]
        qg, ag, gg = colt[:, 16:17], colt[:, 17:18], colt[:, 18:19]
        ag8 = sb("ag8", [P, 1])
        kg = sb("kg", [P, DH])
        wr = sb("wr", [P, DC, NG + NE])
        br = sb("br", [P, NG + NE])
        ssx = sb("ssx", [P, NT])
        stdx = sb("stdx", [P, NT])
        rx = sb("rx", [P, NT])
        sskq = sb("sskq", [P, 2, NT, 8])
        rkq = sb("rkq", [P, 2, NT, 8])
        lsum = sb("lsum", [P, 2])
        lexp = sb("lexp", [P, 2])
        nlam = sb("nlam", [P, 1])
        em = sb("em", [P, 2, 16])
        gl = sb("gl", [P, 2, 16])
        sso = sb("sso", [P, NT, 8])
        ro = sb("ro", [P, NT, 8])
        junk = sb("junk", [P, DV])
        mx = sb("mx", [P, 2, 2])
        nm = sb("nm", [P, 2, 2])
        es = sb("es", [P, 2, 2])
        ri = sb("ri", [P, 2, 2])
        ss2 = sb("ss2", [P, NT])
        st2 = sb("st2", [P, NT])
        r2 = sb("r2", [P, NT])
        ovf = sb("ovf", [P, 1], I32)
        idx = sb("idx", [P, PAIRS + 1], I32)
        tk = sb("tk", [P, 2, 2, NT])
        dst = sb("dst", [P, PAIRS + 1], I32)
        wk = sb("wk", [P, 2, NT])
        cur = sb("cur", [P, 1])

        hT = G[:, 1024:1024 + DC * NT * P].rearrange("p (c i t) -> p c i t", c=DC, i=NT)
        hL = G_r[:, 1024:1024 + DC * NT * P].rearrange("p (c i t) -> p c i t", c=DC, i=NT)
        hH = hbuf_r[:, :].rearrange("p (c i t) -> p c i t", c=DC, i=NT)
        qT = hbuf[:, 0:H * NT * P].rearrange("p (h t) -> p h t", h=H)
        kT = hbuf[:, H * NT * P:].rearrange("p (h t) -> p h t", h=H)
        mixT = hbuf[:, :].rearrange("p (c t) -> p c t", c=DC)
        xn = [Zpad[:, Z0 + C_Q * CW + k * D:Z0 + C_Q * CW + (k + 1) * D] for k in range(2)]
        xjunk = Zpad[:, Z0 + C_V * CW:Z0 + C_V * CW + D]
        GA0 = 1024 + DC * NT * P
        wga = G[:, GA0:GA0 + DC * RANK]
        wgaL = G_r[:, GA0:GA0 + DC * RANK]
        wgaH = G_r[:, GA0 + DC * RANK:GA0 + 2 * DC * RANK]
        HW = DC // 2 * 512
        wH = [W_r[:, k * HW:(k + 1) * HW] for k in range(2)]
        win = [W[:, (2 + k) * HW:(3 + k) * HW] for k in range(2)]
        wL = [W_r[:, (2 + k) * HW:(3 + k) * HW] for k in range(2)]
        kqsq = [G[:, k * 512:(k + 1) * 512] for k in range(2)]
        la = R0[:, 0:1280].rearrange("p (i n) -> p i n", i=NT)
        gz = R0[:, 1280:2560]
        gt = R0[:, 2560:3840]
        gaT = R0[:, 3840:4480]
        wa2 = R0[:, 4480:4736]
        lamv = R0[:, 4736:4992].rearrange("p (a n) -> p a n", a=4)
        lamp = R0[:, 4992:5120].rearrange("p (a n) -> p a n", a=2)
        bT = W[:, 0:1280].rearrange("p (h t) -> p h t", h=2)
        Ep = W[:, 1280:2560].rearrange("p (h t) -> p h t", h=2)
        Em = W[:, 2560:3840].rearrange("p (h t) -> p h t", h=2)
        qt = W[:, 3840:5120].rearrange("p (h t) -> p h t", h=2)
        kt = W[:, 5120:6400].rearrange("p (h t) -> p h t", h=2)
        ktok = W[:, 6400:7680].rearrange("p (i n) -> p i n", i=NT)
        St = G[:, 0:2048].rearrange("p (c h v) -> p c h v", c=8, h=2)
        S0 = G[:, 2048:4096].rearrange("p (b h v) -> p b h v", b=NB, h=2)
        Ss = G[:, 4096:6144].rearrange("p (b h v) -> p b h v", b=NB, h=2)
        kz = G[:, 6144:8192].rearrange("p (b n) -> p b n", b=NB)
        AT = R0[:, 0:2560].rearrange("p (i h e t) -> p i h e t", i=NT, h=2, e=2)
        qz = R0[:, 2560:4608].rearrange("p (h b t) -> p h b t", h=2, b=NB)
        S = R0[:, 4864:5120].rearrange("p (h v) -> p h v", h=2)
        tmpS = [R0[:, 5120 + k * 512:5632 + k * 512].rearrange("p (b h v) -> p b h v", b=2, h=2) for k in range(2)]
        NER = 3
        E = [[G[:, (2 * k + m) * 512:(2 * k + m + 1) * 512] for m in range(2)] for k in range(NER)]
        PT = [G[:, 3072 + k * 640:3712 + k * 640] for k in range(2)]
        enew = G[:, 4352:5376].rearrange("p (b t) -> p b t", b=NB)
        qbd = G[:, 5376:6400].rearrange("p (b h m q) -> p b h m q", b=NB, h=H, m=2)
        NKV = 5
        Kc = [r.rearrange("p (h t) -> p h t", h=H) for r in
              (W[:, 0:2048], W[:, 4096:6144], R0[:, 0:2048], Zpad[:, 0:2048], R0[:, 4096:6144])]
        Vc = [r.rearrange("p (j n) -> p j n", j=4) for r in
              (W[:, 2048:4096], W[:, 6144:8192], R0[:, 2048:4096], Zpad[:, 2048:4096], Zpad[:, 4096:6144])]
        wo = W[:, :].rearrange("p (c n) -> p c n", c=DC)
        WO_ORDER = (0, 4, 2, 6)
        woL = W_r[:, :].rearrange("p (c n) -> p c n", c=DC)
        KR0 = Z0 + C_K * CW
        woH = {0: [(0, 3 * 512, Zpad_r[:, KR0:KR0 + 3 * 512]), (3 * 512, 512, G_r[:, 11 * 512:12 * 512])],
               4: [(0, 2 * D, R0_r[:, 4 * D:6 * D])], 2: [(0, 2 * D, R0_r[:, 0:2 * D])],
               6: [(0, 2 * D, R0_r[:, 2 * D:4 * D])]}

        def wo_high_of(c0, o):
            for a, n, place in woH[c0]:
                if a <= o < a + n:
                    return place[:, o - a:o - a + 512]

        mixH = G_r[:, 0:DC * NT * P].rearrange("p (c t) -> p c t", c=DC)
        mixL = hbuf_r[:, :].rearrange("p (c t) -> p c t", c=DC)
        hn = [G[:, 6144 + k * D:6144 + (k + 1) * D] for k in range(2)]
        GR0 = Z0 + C_GR * CW
        h2T = [Zpad[:, GR0 + k * D:GR0 + (k + 1) * D].rearrange("p (c t) -> p c t", c=DC) for k in range(2)]

        at = [GR0 + 2048]

        def tmp(n):
            at[0] += n
            assert at[0] <= GR0 + CW
            return Zpad[:, at[0] - n:at[0]]

        NL = NG + NE
        Lg = tmp(NT * NL).rearrange("p (i n) -> p i n", i=NT)
        at[0] = GR0
        gmax = tmp(NT)
        ge = tmp(NT * NG).rearrange("p (i g) -> p i g", i=NT)
        gs = tmp(NT)
        goh = tmp(NT * NG).rearrange("p (i g) -> p i g", i=NT)
        gm2 = tmp(NT)
        egs = tmp(NT * NE).rearrange("p (i g e) -> p i g e", i=NT, g=NG)
        esel = [tmp(NT * EPG).rearrange("p (i e) -> p i e", i=NT) for _ in range(2)]
        oh = [tmp(NT * EPG).rearrange("p (i e) -> p i e", i=NT) for _ in range(2)]
        mk = tmp(2 * NT).rearrange("p (k i) -> p k i", k=2)
        mk2 = tmp(NT)
        dm = tmp(NT)
        den = tmp(NT)
        M = tmp(2 * NT * NE).rearrange("p (k i g e) -> p k i g e", k=2, i=NT, g=NG)
        Ms = tmp((NT + 1) * NE)
        rk = tmp(2 * NT).rearrange("p (k i) -> p k i", k=2)
        pk = tmp(2 * NT).rearrange("p (k i) -> p k i", k=2)
        rn = tmp(2 * NT).rearrange("p (k i) -> p k i", k=2)
        loc = tmp(2 * NT).rearrange("p (k i) -> p k i", k=2)
        qk = tmp(2 * NT).rearrange("p (k i) -> p k i", k=2)
        cmpr = tmp(2 * NT * (ROUNDS - 1)).rearrange("p (m j) -> p m j", m=2 * NT)
        mprod = tmp(2 * NT * NE).rearrange("p (k n) -> p k n", k=2)
        Mp = tmp(4 * NT * PAIRS).rearrange("p (a k i n) -> p a k i n", a=2, k=2, i=NT)
        rmask = tmp(2 * NT).rearrange("p (k i) -> p k i", k=2)
        none = tmp(2 * (PAIRS + 1))
        cnt = tmp(1)
        ovf_f = tmp(1)
        assert at[0] <= GR0 + 2048
        OH0 = KR0
        Rt = hbuf[:, 0:4 * NT * (PAIRS + 1)].rearrange("p (k i a n) -> p k i a n", k=2, i=NT, a=2)
        OH = Zpad[:, OH0:OH0 + 1280].rearrange("p (n s) -> p n s", n=2 * NT)

        ebuf = [R0[:, :], Zpad[:, 0:EXP_W], Zpad[:, Z0 + 6 * CW - EXP_W:], G[:, 0:EXP_W]]
        egu = [e[:, 0:GU_W].rearrange("p (c n) -> p c n", c=DC) for e in ebuf]
        edn = [e[:, GU_W:EXP_W].rearrange("p (f n) -> p f n", f=2) for e in ebuf]
        gu4 = hbuf[:, D:D + GU_W].rearrange("p (c n) -> p c n", c=DC)
        dn4 = G[:, EXP_W:EXP_W + DN_W].rearrange("p (f n) -> p f n", f=2)
        NXS = 2
        xs = [W[:, k * D:(k + 1) * D] for k in range(NXS)]
        xsT = [W[:, (2 + k) * D:(3 + k) * D].rearrange("p (c s) -> p c s", c=DC) for k in range(2)]
        ysb = [W[:, (4 + k) * D:(5 + k) * D] for k in range(2)]
        sil = [W[:, (6 + k) * D:(6 + k) * D + FE] for k in range(2)]
        hs = [W[:, (6 + k) * D + 256:(6 + k) * D + 256 + FE] for k in range(2)]
        hTs = [W[:, (6 + k) * D + 512:(6 + k) * D + 768].rearrange("p (f s) -> p f s", f=2) for k in range(2)]
        yg = [R0[:, k * 2 * D:(k + 1) * 2 * D] for k in range(3)] + [Zpad[:, k * 2 * D:(k + 1) * 2 * D] for k in range(2)]

        ld_x = [sem(f"ld_x{i}") for i in range(NT)]
        ld_cols = sem("ld_cols")
        ld_small = sem("ld_small")
        ld_win = [sem(f"ld_win{k}") for k in range(2)]
        ld_state = sem("ld_state")
        ld_k = [sem(f"ld_k{k}") for k in range(NKV)]
        ld_v = [sem(f"ld_v{k}") for k in range(NKV)]
        woH_ready = sem("woH_ready")
        woL_ready = sem("woL_ready")
        mixH_ready = sem("mixH_ready")
        mixL_ready = sem("mixL_ready")
        ld_gu = [sem(f"ld_gu{k}") for k in range(4)]
        ld_dn = [sem(f"ld_dn{k}") for k in range(4)]
        pool_step = sem("pool_step")
        pool_seen = sem("pool_seen")
        consts = sem("consts")
        dve_step = sem("dve_step")
        act_step = sem("act_step")
        ssq1 = sem("ssq1")
        std1 = sem("std1")
        rstd1 = sem("rstd1")
        xn_ready = sem("xn_ready")
        xT_done = sem("xT_done")
        hT_ready = sem("hT_ready")
        ga_done = sem("ga_done")
        wgaH_ready = sem("wgaH_ready")
        wgaL_ready = sem("wgaL_ready")
        gaT_ready = sem("gaT_ready")
        pre_done = sem("pre_done")
        gabs_ready = sem("gabs_ready")
        gln_ready = sem("gln_ready")
        la_ready = sem("la_ready")
        lam_mid = sem("lam_mid")
        lam_exp = sem("lam_exp")
        hH_ready = sem("hH_ready")
        hL_ready = sem("hL_ready")
        wH_ready = sem("wH_ready")
        wL_ready = sem("wL_ready")
        half_done = sem("half_done")
        proj_done = sem("proj_done")
        z_free = sem("z_free")
        kqss_ready = sem("kqss_ready")
        kqstd = sem("kqstd")
        k_ready = sem("k_ready")
        q_ready = sem("q_ready")
        b_done = sem("b_done")
        b_ready = sem("b_ready")
        dec_in = sem("dec_in")
        dec_ready = sem("dec_ready")
        at_zero = sem("at_zero")
        qkT_done = sem("qkT_done")
        kT_ready = sem("kT_ready")
        qT_ready = sem("qT_ready")
        gT_done = sem("gT_done")
        gqk_ready = sem("gqk_ready")
        qz_ready = sem("qz_ready")
        ktok_done = sem("ktok_done")
        ktok_ready = sem("ktok_ready")
        kz_ready = sem("kz_ready")
        sc_done = sem("sc_done")
        AT_ready = sem("AT_ready")
        U_done = sem("U_done")
        U_used = sem("U_used")
        St_ready = sem("St_ready")
        Ss_ready = sem("Ss_ready")
        go_done = sem("go_done")
        go_sq = sem("go_sq")
        go_ready = sem("go_ready")
        silu_ready = sem("silu_ready")
        sp_ready = sem("sp_ready")
        ss_ready = sem("ss_ready")
        st_states = sem("st_states")
        st_kv = sem("st_kv")
        att_zero = sem("att_zero")
        s_done = sem("s_done")
        nm_ready = sem("nm_ready")
        e_ready = sem("e_ready")
        p_ready = sem("p_ready")
        pt_done = sem("pt_done")
        pt_ready = sem("pt_ready")
        o_done = sem("o_done")
        o_sq = sem("o_sq")
        ao_ready = sem("ao_ready")
        qbd_ready = sem("qbd_ready")
        d_s_done = sem("d_s_done")
        d_nm_ready = sem("d_nm_ready")
        d_e_ready = sem("d_e_ready")
        cb_ready = sem("cb_ready")
        d_pt_done = sem("d_pt_done")
        d_pt_ready = sem("d_pt_ready")
        d_pv_done = sem("d_pv_done")
        ostd = sem("ostd")
        mix_ready = sem("mix_ready")
        mT_done = sem("mT_done")
        mT_a = sem("mT_a")
        mT_g = sem("mT_g")
        out_done = sem("out_done")
        x2_ready = sem("x2_ready")
        ssq2 = sem("ssq2")
        std2 = sem("std2")
        rstd2 = sem("rstd2")
        hn_ready = sem("hn_ready")
        st_hn = [sem(f"st_hn{k}") for k in range(2)]
        h2_done = sem("h2_done")
        h2_ready = sem("h2_ready")
        lg_done = sem("lg_done")
        gexp_in = sem("gexp_in")
        gexp_out = sem("gexp_out")
        m_ready = sem("m_ready")
        rank_done = sem("rank_done")
        tab_step = sem("tab_step")
        tab_in = sem("tab_in")
        tab_done = sem("tab_done")
        idx_ready = sem("idx_ready")
        ovf_ready = sem("ovf_ready")
        gath = [sem(f"gath{k}") for k in range(NXS)]
        xsT_done = sem("xsT_done")
        xsT_ready = sem("xsT_ready")
        gu_done = sem("gu_done")
        sil_ready = sem("sil_ready")
        h_ready = sem("h_ready")
        hT_done = sem("hT_done")
        hTs_ready = sem("hTs_ready")
        dn_done = sem("dn_done")
        ysb_ready = sem("ysb_ready")
        st_y = [sem(f"st_y{k}") for k in range(2)]
        ygath = [sem(f"ygath{i}") for i in range(NT)]
        ysum = sem("ysum")
        st_out = sem("st_out")

        block = ctx.enter_context(nc.Block())

        def gu_rows(e):
            return w_gu[bass.ds(e * P, P), :].rearrange("p (c n) -> p c n", c=DC)

        def dn_rows(e):
            return w_dn[bass.ds(e * P, P), :].rearrange("p (f n) -> p f n", f=2)

        @block.sync
        def _(sp):
            for i in range(2):
                sp.dma_start(X[:, i, :], x[i]).then_inc(ld_x[i], 16)
            sp.dma_start(colt[:, :], cols).then_inc(ld_cols, 16)
            for i in range(2, NT):
                sp.dma_start(X[:, i, :], x[i]).then_inc(ld_x[i], 16)
            sp.dma_start(wga, w_ga).then_inc(ld_small, 16)
            sp.dma_start(wa2[0:RANK + 1, :], w_a2b).then_inc(ld_small, 16)
            sp.dma_start(lamv, lam.partition_broadcast(P)).then_inc(ld_small, 16)
            sp.dma_start(kg[:, :], k_gain.partition_broadcast(P)).then_inc(ld_small, 16)
            sp.dma_start(br[:, :], b_r.partition_broadcast(P)).then_inc(ld_small, 16)
            sp.dma_start(wr[:, :, :], w_r).then_inc(ld_small, 16)
            def w_half(c, k):
                sp.dma_start(win[k], w_main[bass.ds(c * P, P), k * HW:(k + 1) * HW]).then_inc(ld_win[k], 16)

            for k in range(2):
                w_half(0, k)
            with sp.Fori(1, 6) as c:
                sp.wait_ge(half_done, c)
                w_half(c, 0)
                sp.wait_ge(proj_done, NT * c)
                w_half(c, 1)
            sp.wait_ge(proj_done, NT * 6)
            sp.dma_start(S0, state).then_inc(ld_state, 16)
            sp.wait_ge(go_done, NT)
            sp.wait_ge(ss_ready, 1)
            for b in range(NKV):
                if b == 2:
                    sp.wait_ge(st_states, 2 * 16)
                sp.dma_start(Kc[b], cache_kt[b]).then_inc(ld_k[b], 16)
                sp.dma_start(Vc[b], cache_v[b]).then_inc(ld_v[b], 16)
            for b in range(NKV, NB):
                sp.wait_ge(d_s_done, b - NKV + 1)
                sp.dma_start(Kc[b % NKV], cache_kt[b]).then_inc(ld_k[b % NKV], 16)
            for b in range(NKV, NB):
                sp.wait_ge(d_pv_done, b - NKV + 1)
                sp.dma_start(Vc[b % NKV], cache_v[b]).then_inc(ld_v[b % NKV], 16)
            for n, c in enumerate(WO_ORDER):
                sp.wait_ge(d_s_done if n < 2 else d_pv_done, NKV + n % 2 + 1)
                sp.dma_start(wo[:, c:c + 2, :], w_out[:, c:c + 2, :]).then_inc(ld_x[n], 16)
            sp.wait_ge(d_s_done, NB)
            sp.wait_ge(d_pv_done, NB)
            sp.dma_start(egu[1], gu_rows(1)).then_inc(ld_gu[1], 16)
            sp.dma_start(edn[1], dn_rows(1)).then_inc(ld_dn[1], 16)
            sp.wait_ge(mT_done, 2 * NT)
            sp.wait_ge(st_kv, 2 * NT * 16)
            for e in (2, 0, 3):
                if e == 0:
                    sp.wait_ge(out_done, 2 * NT)
                sp.dma_start(egu[e], gu_rows(e)).then_inc(ld_gu[e], 16)
                sp.dma_start(edn[e], dn_rows(e)).then_inc(ld_dn[e], 16)

            sp.wait_ge(ld_gu[0], 16)
            sp.wait_ge(ld_dn[0], 16)
            sp.dma_start(gu4, gu_rows(4)).then_inc(ld_gu[0], 16)
            for k in range(2):
                sp.wait_ge(st_hn[k], (3 - k) * 16)
            sp.wait_ge(h2_done, 2 * NT)
            sp.dma_start(dn4, dn_rows(4)).then_inc(ld_dn[0], 16)

            def experts(g0, g, k0=0):
                for k in range(k0, 4):
                    if k % 2 == 0 or k == k0:
                        sp.wait_ge(gu_done, (g0 + g) * 2 + k // 2 - 1)
                    sp.dma_start(egu[k], gu_rows(g * 4 + k)).then_inc(ld_gu[k], 16)
                for k in range(k0, 4):
                    if k % 2 == 0 or k == k0:
                        sp.wait_ge(dn_done, (g0 + g) * 2 + k // 2 - 1)
                    sp.dma_start(edn[k], dn_rows(g * 4 + k)).then_inc(ld_dn[k], 16)

            experts(0, 1, k0=1)
            with sp.Fori(2, NE // 4) as g:
                experts(0, g)
            sp.wait_ge(ovf_ready, 1)
            with sp.If(sp.value_load(ovf[0:1, 0:1]) > 0):
                with sp.Fori(1, ROUNDS) as r:
                    with sp.Fori(0, NE // 4) as g:
                        experts(r * 8, g)
                for k in range(2):
                    sp.wait_ge(st_y[k], ROUNDS * (PAIRS // 2) * 16)
            for k in range(2):
                sp.wait_ge(st_y[k], PAIRS // 2 * 16)
            sp.wait_ge(dn_done, PAIRS)
            for i in range(NT):
                sp.dma_start(yg[i], ye_dram[2 * P * i:2 * P * (i + 1), :].rearrange("(p k) d -> p (k d)", k=2)
                             ).then_inc(ygath[i], 16)
            sp.wait_ge(st_kv, 2 * NT * 16)
            sp.wait_ge(st_states, 2 * 16)

        @block.gpsimd
        def _(pool):
            n = [0]

            def step(ins):
                n[0] += 1
                ins.then_inc(pool_step, 1)
                pool.wait_ge(pool_step, n[0])

            pool.memset(epsc[:, :], EPS)
            pool.memset(ones[:, :], 1.0)
            pool.memset(gaT[0:RANK + 1, :], 1.0)
            pool.memset(C0[:, :], 0.0)
            pool.memset(C1[:, :], 0.0)
            pool.memset(mA[:, :], 0.0)
            pool.memset(mB[:, :], NEG)
            pool.memset(strict[:, :], 1.0)
            pool.memset(bmask[:, :], 1.0)
            pool.memset(tri64[:, :], 1.0 / 16)
            step(pool.memset(ident[:, :], 0.0))
            step(pool.affine_select(out=ident[:, :], in_=ident[:, :], compare_op=ALU.not_equal, fill=1.0,
                                    base=0, pattern=[[-1, P]], channel_multiplier=1))
            step(pool.affine_select(out=tri64[:, :], in_=tri64[:, :], compare_op=ALU.is_ge, fill=0.0,
                                    base=0, pattern=[[1, P]], channel_multiplier=-1))
            t16 = tri16[:, :].rearrange("p (b t) -> p b t", b=NB)
            step(pool.affine_select(out=t16, in_=tri64[:, :].rearrange("p (b t) -> p b t", b=NB),
                                    compare_op=ALU.is_ge, fill=0.0,
                                    base=0, pattern=[[-Q, NB], [0, Q]], channel_multiplier=1))
            step(pool.memset(tri64[0:CHUNK, CHUNK:P], 0.0))
            step(pool.affine_select(out=strict[:, :], in_=strict[:, :], compare_op=ALU.is_gt, fill=0.0,
                                    base=0, pattern=[[1, P]], channel_multiplier=-1))
            step(pool.affine_select(out=bmask[:, :], in_=bmask[:, :], compare_op=ALU.is_ge, fill=0.0,
                                    base=0, pattern=[[-Q, NB]], channel_multiplier=1))
            step(pool.affine_select(out=bmask[:, :], in_=bmask[:, :], compare_op=ALU.is_ge, fill=0.0,
                                    base=Q - 1, pattern=[[Q, NB]], channel_multiplier=-1))
            for m, c in ((0, C0), (1, C1)):
                cv = c[:, :].rearrange("p (h q) -> p h q", h=H)
                step(pool.affine_select(out=cv, in_=cv, compare_op=ALU.not_equal, fill=1.0,
                                        base=-Q * m, pattern=[[-2 * Q, H], [-1, Q]], channel_multiplier=1))
            pool.memset(mA[0:1, 0:CHUNK], 1.0)
            step(pool.memset(mA[CHUNK:CHUNK + 1, 0:CHUNK], 1.0))
            pool.iota(iota_i[:, :], pattern=[[1, P]], base=0, channel_multiplier=0)
            step(pool.iota(tok_i[:, :], pattern=[[P, NT]], base=0, channel_multiplier=1))
            step(pool.iota(desc_i[:, :], pattern=[[-1, EPG]], base=EPG, channel_multiplier=0))
            pool.tensor_copy(iota128[:, :], iota_i[:, :])
            pool.tensor_copy(desc[:, :], desc_i[:, :])
            pool.memset(cur[:, :], 0.0)
            step(pool.tensor_copy(tok[:, :], tok_i[:, :]))
            step(pool.tensor_scalar(thr[:, :], iota128[:, 1:ROUNDS], float(CAP), None, ALU.mult))
            for k in range(2):
                pool.tensor_scalar(tk[:, 0, k, :], tok[:, :], 1.0, None, ALU.add)
                step(pool.tensor_scalar(tk[:, 1, k, :], tok[:, :], 2.0, float(k + 1), ALU.mult, ALU.add))
            pool.nop().then_inc(consts, 1)
            for i in range(NT):
                pool.wait_ge(k_ready, i + 1)
                pool.dma_start(k_out[i], z(C_K, i)).then_inc(st_kv, 16)
            for i in range(NT):
                pool.wait_ge(z_free, 5 + 25 + i + 1)
                pool.dma_start(v_out[i], z(C_V, i)).then_inc(st_kv, 16)
            pool.wait_ge(b_done, 1)
            pool.memset(R0[:, 0:2560], 0.0).then_inc(at_zero, 1)
            pool.memset(R0[:, 2560:4608], 0.0).then_inc(at_zero, 1)
            pool.wait_ge(sp_ready, 1)
            pool.dma_start(sp_out, S).then_inc(st_states, 16)
            pool.wait_ge(ss_ready, 1)
            pool.dma_start(ss_out, S0).then_inc(st_states, 16)
            pool.wait_ge(go_done, NT)
            pool.memset(G[:, 4352:6400], 0.0).then_inc(att_zero, 1)
            pool.memset(Cb[:, :, :], 0.0).then_inc(att_zero, 1)
            for i in range(NT):
                pool.wait_ge(hn_ready, i + 1)
                pool.dma_start(hn_dram[i * P:(i + 1) * P, :], hn[i % 2]).then_inc(st_hn[i % 2], 16)
            pool.wait_ge(out_done, 2 * NT)
            step(pool.memset(W[:, 0:NXS * D], 0.0))
            pool.wait_ge(st_hn[0], 3 * 16)
            pool.wait_ge(st_hn[1], 2 * 16)

            def pairs(r):
                def seen():
                    if not isinstance(r, int):
                        pool.sem_inc(pool_seen, 1)

                def scatter(p):
                    pool.wait_ge(ysb_ready, r * 2 * PAIRS + 2 * (p + 1))
                    seen()
                    pool.indirect_dma_start(
                        out=ye_dram, out_offset=bass.IndirectOffsetOnAxis(ap=dst[:, p:p + 1], axis=0),
                        in_=ysb[p % 2], in_offset=None, bounds_check=2 * NT * P - 1, oob_is_err=False,
                    ).then_inc(st_y[p % 2], 16)

                pool.wait_ge(idx_ready, r + 1)
                seen()
                for p in range(PAIRS + 1):
                    if p >= NXS:
                        pool.wait_ge(xsT_done, r * 2 * (PAIRS + 1) + 2 * (p - NXS + 1))
                        seen()
                    pool.indirect_dma_start(
                        out=xs[p % NXS], out_offset=None, in_=hn_dram,
                        in_offset=bass.IndirectOffsetOnAxis(ap=idx[:, p:p + 1], axis=0),
                        bounds_check=NT * P - 1, oob_is_err=False,
                    ).then_inc(gath[p % NXS], 16)
                    if p >= 3:
                        scatter(p - 3)
                for p in range(PAIRS - 2, PAIRS):
                    scatter(p)

            pairs(0)
            pool.wait_ge(ovf_ready, 1)
            with pool.If(pool.value_load(ovf[0:1, 0:1]) > 0):
                with pool.Fori(1, ROUNDS) as r:
                    pool.wait_ge(xsT_done, r * 2 * (PAIRS + 1))
                    pairs(r)

        @block.scalar
        def _(act):
            n = [0]

            def step(ins):
                n[0] += 1
                ins.then_inc(act_step, 1)
                act.wait_ge(act_step, n[0])

            act.wait_ge(consts, 1)
            act.wait_ge(ld_cols, 16)

            def root(i):
                act.wait_ge(ssq1, i + 1)
                act.activation(stdx[:, i:i + 1], ssx[:, i:i + 1], ACT.Sqrt, bias=epsc[:, 0:1],
                               scale=1.0 / D).then_inc(std1, 1)

            def h_high(i):
                act.wait_ge(hT_ready, 2 * i + 2)
                act.activation(hH[:, :, i, :], hT[:, :, i, :], ACT.Copy).then_inc(hH_ready, 1)

            def w_high(c, k):
                act.wait_ge(ld_win[k], (c + 1) * 16)
                act.activation(wH[k], win[k], ACT.Copy).then_inc(wH_ready, 1)

            root(0)
            for i in range(NT):
                if i + 1 < NT:
                    root(i + 1)
                act.wait_ge(rstd1, i + 1)
                if i >= 2:
                    act.wait_ge(xT_done, 2 * (i - 1))
                act.activation(xn[i % 2], X[:, i, :], ACT.Copy, scale=rx[:, i:i + 1]).then_inc(xn_ready, 1)
                if i >= 1:
                    h_high(i - 1)
                if i == 2:
                    w_high(0, 0)
            for i in range(NT):
                act.nop().then_inc(z_free, 1)
            h_high(NT - 1)
            w_high(0, 1)
            act.wait_ge(ld_small, 6 * 16)
            act.activation(wgaH, wga, ACT.Copy).then_inc(wgaH_ready, 1)
            act.wait_ge(lam_mid, 1)
            act.activation(lexp[:, :], lsum[:, :], ACT.Exp).then_inc(lam_exp, 1)
            def evac(c, n_before, i):
                act.wait_ge(proj_done, n_before + i + 1)
                o = c * CW + (Z0 + i * 512)
                act.activation(Zpad[:, bass.ds(o, 512)], bank[i][:, :], ACT.Copy).then_inc(z_free, 1)

            def chunk(c):
                for i in range(2):
                    evac(c, NT * c, i)
                w_high(c + 1, 0)
                for i in range(2, NT):
                    evac(c, NT * c, i)
                w_high(c + 1, 1)

            chunk(0)
            chunk(1)
            act.wait_ge(gabs_ready, 1)
            step(act.activation(gt, gt, ACT.Exp))
            act.activation(gt, gt, ACT.Ln, bias=1.0).then_inc(gln_ready, 1)
            with act.Fori(2, 4) as c:
                chunk(c)
            chunk(4)
            evac(5, 25, 0)
            act.wait_ge(kqss_ready, 1)
            act.activation(rkq[:, :, :, :], sskq[:, :, :, :], ACT.Sqrt, bias=epsc[:, 0:1],
                           scale=1.0 / DH).then_inc(kqstd, 1)
            for i in range(1, NT):
                evac(5, 25, i)
            act.wait_ge(b_done, 1)
            for k in range(3):
                w = 2 if k < 2 else 1
                act.activation(bT[:, :, 256 * k:256 * k + 128 * w].rearrange("p h (i t) -> p i h t", i=w),
                               bank[5 + k][:, 0:256 * w].rearrange("p (i h t) -> p i h t", i=w, h=2),
                               ACT.Copy).then_inc(b_ready, 1)
            act.wait_ge(b_ready, 3)
            act.activation(em[:, :, 0:8], bT[:, :, 0:512].rearrange("p h (c t) -> p h c t", c=8)[:, :, :, 31],
                           ACT.Exp).then_inc(dec_ready, 1)
            act.activation(em[:, :, 8:16], bT[:, :, 512:640].rearrange("p h (c t) -> p h c t", c=8)[:, :, :, 7],
                           ACT.Exp).then_inc(dec_ready, 1)
            act.wait_ge(dec_in, 2)
            act.activation(Ep, kt, ACT.Exp).then_inc(dec_ready, 1)
            act.activation(Em, kt, ACT.Exp, scale=-1.0).then_inc(dec_ready, 1)
            for i in range(NT):
                act.wait_ge(qkT_done, NT + i + 1)
                act.activation(qT[:, :, i * P:(i + 1) * P],
                               bank[(NT + i) % 4][:, :].rearrange("p (h t) -> p h t", h=H),
                               ACT.Copy, scale=qg).then_inc(qT_ready, 1)
            for i in range(NT):
                act.wait_ge(ktok_done, i + 1)
                act.activation(ktok[:, i, :], bank[6 + i % 2][:, 0:256], ACT.Copy).then_inc(ktok_ready, 1)
            act.wait_ge(z_free, 7 * NT)
            act.activation(zall(C_GR), zall(C_GR), ACT.Silu).then_inc(silu_ready, 1)
            for i in range(NT):
                act.wait_ge(go_done, i + 1)
                for h in range(H):
                    step(act.activation(junk[:, :], bank[2 * (i % 2) + h % 2][:, (h // 2) * P:(h // 2 + 1) * P],
                                        ACT.Square, accum_out=sso[:, i, H + h:H + h + 1]))
                act.nop().then_inc(go_sq, 1)
            items = [(i, h) for i in range(NP) for h in range(H)]
            NI = len(items)
            act.wait_ge(st_states, 2 * 16)

            def exps(m):
                i, h = items[m]
                L = (i + 1) * P
                act.wait_ge(nm_ready, m + 1)
                if m >= NER:
                    act.wait_ge(pt_done, m - NER + 1)
                if m >= 2:
                    act.wait_ge(p_ready, m - 1)
                for mm in range(2):
                    act.activation(E[m % NER][mm][:, 0:L], bank[2 * (m % 2) + mm][:, 0:L], ACT.Exp,
                                   bias=nm[:, m % 2, mm:mm + 1], scale=DH ** -0.5,
                                   accum_out=es[:, m % 2, mm:mm + 1]).then_inc(e_ready, 1)

            def pts(m):
                i, h = items[m]
                L = (i + 1) * P
                act.wait_ge(pt_done, m + 1)
                if m >= 2:
                    act.wait_ge(o_done, m - 1)
                act.activation(PT[m % 2][:, 0:L], bank[4 + m % 2][:, 0:L], ACT.Copy).then_inc(pt_ready, 1)

            def osq(i, src, done, value):
                act.wait_ge(done, value)
                for h in range(H):
                    step(act.activation(junk[:, :], src[:, h * P:(h + 1) * P], ACT.Square,
                                        accum_out=sso[:, i, h:h + 1]))
                act.nop().then_inc(o_sq, 1)

            for m in range(NI + 3):
                if m < NI:
                    exps(m)
                if 2 <= m < NI + 2:
                    pts(m - 2)
                if m >= 3 and (m - 3) % H == H - 1:
                    i = (m - 3) // H
                    osq(i, bank[6 + i % 2], o_done, m - 2)

            def d_exps(b):
                act.wait_ge(d_nm_ready, b + 1)
                if b < NER:
                    act.wait_ge(pt_done, NI)
                else:
                    act.wait_ge(d_pt_done, b - NER + 1)
                if b < 2:
                    act.wait_ge(p_ready, NI)
                else:
                    act.wait_ge(cb_ready, b - 1)
                act.activation(E[b % NER][0], bank[2 * (b % 2)][:, :], ACT.Exp, bias=nm[:, b % 2, 0:1],
                               scale=DH ** -0.5, accum_out=es[:, b % 2, 0:1]).then_inc(d_e_ready, 1)
                act.activation(enew[:, b, b * Q:(b + 1) * Q], bank[2 * (b % 2) + 1][:, 0:Q], ACT.Exp,
                               bias=nm[:, b % 2, 0:1], scale=DH ** -0.5,
                               accum_out=es[:, b % 2, 1:2]).then_inc(d_e_ready, 1)

            def d_pts(b):
                act.wait_ge(d_pt_done, b + 1)
                if b >= 2:
                    act.wait_ge(d_pv_done, b - 1)
                act.activation(PT[b % 2][:, 0:512], bank[4 + b % 2][:, :], ACT.Copy).then_inc(d_pt_ready, 1)
                act.activation(PT[b % 2][:, 512:640], bank[7][:, 0:P], ACT.Copy).then_inc(d_pt_ready, 1)

            def wo_high(n):
                act.wait_ge(ld_x[n], 2 * 16)
                if n == 0:
                    act.wait_ge(st_kv, 2 * NT * 16)
                    act.wait_ge(d_s_done, NB)
                if n == 2:
                    act.wait_ge(d_s_done, NB)
                if n == 3:
                    act.wait_ge(d_pv_done, NB)
                c = WO_ORDER[n]
                for a, w, place in woH[c]:
                    ins = act.activation(place, W[:, c * D + a:c * D + a + w], ACT.Copy)
                ins.then_inc(woH_ready, 1)

            def mix_g(i):
                act.wait_ge(mT_done, 2 * i + 2)
                act.activation(mixT[:, H:2 * H, i * P:(i + 1) * P],
                               bank[2 * (i % 2) + 1][:, :].rearrange("p (c t) -> p c t", c=H),
                               ACT.Copy, scale=gg).then_inc(mT_g, 1)
                act.wait_ge(mT_g, i + 1)
                act.wait_ge(mT_a, i + 1)
                act.activation(mixH[:, :, i * P:(i + 1) * P], mixT[:, :, i * P:(i + 1) * P],
                               ACT.Copy).then_inc(mixH_ready, 1)

            act.wait_ge(o_sq, NP)
            act.wait_ge(go_sq, NT)
            act.activation(ro[:, 0:NP, :], sso[:, 0:NP, :], ACT.Sqrt, bias=epsc[:, 0:1],
                           scale=1.0 / DV).then_inc(ostd, 1)
            act.activation(ro[:, NP, H:], sso[:, NP, H:], ACT.Sqrt, bias=epsc[:, 0:1],
                           scale=1.0 / DV).then_inc(ostd, 1)
            for b in range(NB + 2):
                if b < NB:
                    d_exps(b)
                if b >= 2:
                    d_pts(b - 2)
                if b >= NB:
                    wo_high(b - NB)
            mix_g(0)
            wo_high(2)
            wo_high(3)
            osq(NP, bank[6], d_pv_done, NB)
            act.wait_ge(o_sq, NT)
            act.activation(ro[:, NP, 0:H], sso[:, NP, 0:H], ACT.Sqrt, bias=epsc[:, 0:1],
                           scale=1.0 / DV).then_inc(ostd, 1)
            for i in range(1, NT):
                mix_g(i)
            for i in range(NT):
                act.wait_ge(ssq2, i + 1)
                act.activation(st2[:, i:i + 1], ss2[:, i:i + 1], ACT.Sqrt, bias=epsc[:, 0:1],
                               scale=1.0 / D).then_inc(std2, 1)
                act.wait_ge(rstd2, i + 1)
                if i >= 2:
                    act.wait_ge(st_hn[i % 2], 16 * (i // 2))
                    act.wait_ge(h2_done, 2 * (i - 1))
                act.activation(hn[i % 2], X[:, i, :], ACT.Copy, scale=r2[:, i:i + 1]).then_inc(hn_ready, 1)
            act.wait_ge(gexp_in, 1)
            act.activation(ge, ge, ACT.Exp).then_inc(gexp_out, 1)
            act.wait_ge(gexp_in, 2)
            act.activation(dm, dm, ACT.Exp).then_inc(gexp_out, 1)

            def silu(r, g, q):
                act.wait_ge(gu_done, (r * 8 + g) * 2 + q + 1)
                act.activation(sil[q], bank[2 + q][:, 0:FE], ACT.Silu).then_inc(sil_ready, 1)

            def hidden(r, g, q):
                act.wait_ge(hT_done, (r * 8 + g) * 2 + q + 1)
                act.activation(hTs[q].rearrange("p f s -> p (f s)"), bank[2 + q][:, 0:FE], ACT.Copy).then_inc(hTs_ready, 1)

            def rows(r, g, q, first):
                act.wait_ge(dn_done, (r * 8 + g) * 2 + q + 1)
                if not first:
                    act.wait_ge(st_y[q], (r * 8 + g) * 16)
                for hf in range(2):
                    act.activation(ysb[q][:, hf * 512:(hf + 1) * 512], bank[4 + 2 * q + hf][:, :],
                                   ACT.Copy).then_inc(ysb_ready, 1)

            def group(r, g, first=False):
                for q in range(2):
                    silu(r, g, q)
                    hidden(r, g, q)
                for q in range(2):
                    rows(r, g, q, first)

            group(0, 0, first=True)
            with act.Fori(1, NE // 4) as g:
                group(0, g)
            act.wait_ge(ovf_ready, 1)
            with act.If(act.value_load(ovf[0:1, 0:1]) > 0):
                with act.Fori(1, ROUNDS) as r:
                    with act.Fori(0, NE // 4) as g:
                        group(r, g)
            for i in range(NT):
                act.wait_ge(ysum, 2 * (i + 1))
                act.dma_start(y_out[i], X[:, i, :]).then_inc(st_out, 16)
            act.wait_ge(st_out, NT * 16)

        @block.vector
        def _(dve):
            n = [0]

            def step(ins):
                n[0] += 1
                ins.then_inc(dve_step, 1)
                dve.wait_ge(dve_step, n[0])

            def bc(ap, shape):
                return ap.unsqueeze(len(ap.shape)).broadcast_to(shape)

            def squares(i):
                dve.wait_ge(ld_x[i], 16)
                if i:
                    dve.wait_ge(ssq1, i)
                dve.tensor_tensor_reduce(out=xjunk, in0=X[:, i, :], in1=X[:, i, :], scale=1.0, scalar=0.0,
                                         op0=ALU.mult, op1=ALU.add, accum_out=ssx[:, i:i + 1]).then_inc(ssq1, 1)

            def hT_out(i):
                for q in range(2):
                    dve.wait_ge(xT_done, 2 * i + q + 1)
                    ins = dve.tensor_tensor(hT[:, 4 * q:4 * q + 4, i, :],
                                            bank[2 * (i % 2) + q][:, :].rearrange("p (c t) -> p c t", c=4),
                                            bc(g1[:, 4 * q:4 * q + 4], [P, 4, P]), ALU.mult)
                    ins.then_inc(hT_ready, 1)

            def h_low(i):
                dve.wait_ge(hH_ready, i + 1)
                dve.tensor_tensor(hL[:, :, i, :], hT[:, :, i, :], hH[:, :, i, :].bitcast(F32),
                                  ALU.subtract).then_inc(hL_ready, 1)

            def w_low(c, k):
                dve.wait_ge(wH_ready, 2 * c + k + 1)
                dve.tensor_tensor(wL[k], win[k], wH[k].bitcast(F32), ALU.subtract).then_inc(wL_ready, 1)

            squares(0)
            dve.wait_ge(ld_cols, 16)
            for i in range(NT):
                if i + 1 < NT:
                    squares(i + 1)
                dve.wait_ge(std1, i + 1)
                dve.reciprocal(rx[:, i:i + 1], stdx[:, i:i + 1]).then_inc(rstd1, 1)
                if i >= 1:
                    hT_out(i - 1)
                if i >= 2:
                    h_low(i - 2)
            hT_out(NT - 1)
            w_low(0, 0)
            h_low(NT - 2)
            h_low(NT - 1)
            w_low(0, 1)
            dve.wait_ge(wgaH_ready, 1)
            dve.tensor_tensor(wgaL, wga, wgaH.bitcast(F32), ALU.subtract).then_inc(wgaL_ready, 1)
            dve.wait_ge(ld_small, 6 * 16)
            step(dve.tensor_tensor(lamp, lamv[:, 0:4:2, :], lamv[:, 1:4:2, :], ALU.mult))
            dve.tensor_reduce(lsum[:, :], lamp, AX.X, ALU.add).then_inc(lam_mid, 1)
            dve.wait_ge(lam_exp, 1)
            step(dve.scalar_tensor_tensor(out=nlam[:, :], in0=lexp[:, 1:2], scalar=-LAM_INIT, in1=lexp[:, 0:1],
                                          op0=ALU.add, op1=ALU.subtract))
            dve.scalar_tensor_tensor(out=Cm[:, :], in0=C1[:, :], scalar=nlam[:, 0:1], in1=C0[:, :],
                                     op0=ALU.mult, op1=ALU.add)
            step(dve.tensor_scalar(ag8[:, :], ag, 1.0 - LAM_INIT, None, ALU.mult))
            for k in range(2):
                w_low(1, k)
            dve.wait_ge(ga_done, 1)
            dve.tensor_copy(gaT[0:RANK, 0:512], bank[5][0:RANK, :]).then_inc(gaT_ready, 1)
            dve.tensor_copy(gaT[0:RANK, 512:640], bank[6][0:RANK, 0:P]).then_inc(gaT_ready, 1)
            for k in range(2):
                w_low(2, k)
            dve.wait_ge(pre_done, 1)
            dve.tensor_copy(gz[:, 0:512], bank[5][:, :])
            dve.tensor_copy(gz[:, 512:1024], bank[6][:, :])
            step(dve.tensor_copy(gz[:, 1024:1280], bank[7][:, 0:256]))
            dve.scalar_tensor_tensor(out=gt, in0=gz, scalar=-1.0, in1=gz, op0=ALU.mult, op1=ALU.min).then_inc(gabs_ready, 1)
            dve.wait_ge(gln_ready, 1)
            dve.scalar_tensor_tensor(out=la.rearrange("p i n -> p (i n)"), in0=gz, scalar=0.0, in1=gt,
                                     op0=ALU.min, op1=ALU.subtract).then_inc(la_ready, 1)
            for k in range(2):
                w_low(C_K, k)
            for c, kq in ((C_K, 0), (C_Q, 1)):
                w_low(c + 1, 0)
                for i in range(NT):
                    dve.wait_ge(z_free, 5 + 5 * c + i + 1)
                    step(dve.tensor_tensor(kqsq[i % 2], z(c, i), z(c, i), ALU.mult))
                    step(dve.tensor_reduce(sskq[:, kq, i, :], kqsq[i % 2].rearrange("p (g d) -> p g d", g=8),
                                           AX.X, ALU.add))
                w_low(c + 1, 1)
            dve.nop().then_inc(kqss_ready, 1)
            dve.wait_ge(kqstd, 1)
            step(dve.reciprocal(rkq[:, :, :, :], rkq[:, :, :, :]))
            for i in range(NT):
                kv = z(C_K, i).rearrange("p (g d) -> p g d", g=8)
                step(dve.tensor_tensor(kv, kv, bc(rkq[:, 0, i, :], [P, 8, DH]), ALU.mult))
                dve.tensor_tensor(kv, kv, kg[:, :].unsqueeze(1).broadcast_to([P, 8, DH]), ALU.mult).then_inc(k_ready, 1)
            for i in range(NT):
                qv = z(C_Q, i).rearrange("p (g d) -> p g d", g=8)
                dve.tensor_tensor(qv, qv, bc(rkq[:, 1, i, :], [P, 8, DH]), ALU.mult).then_inc(q_ready, 1)
            dve.wait_ge(b_ready, 3)
            for a, L, mid in ((0, CHUNK, CHUNK // 2 - 1), (512, Q, Q // 2 - 1)):
                bv = bT[:, :, a:a + 8 * L].rearrange("p h (c t) -> p h c t", c=8)
                dv = kt[:, :, a:a + 8 * L].rearrange("p h (c t) -> p h c t", c=8)
                for hp in range(2):
                    ins = dve.tensor_tensor(dv[:, hp], bv[:, hp], bv[:, hp, :, mid:mid + 1].broadcast_to([P, 8, L]),
                                            ALU.subtract)
                ins.then_inc(dec_in, 1)
            for i in range(NT):
                dve.wait_ge(qkT_done, i + 1)
                dve.tensor_copy(kT[:, :, i * P:(i + 1) * P],
                                bank[i % 4][:, :].rearrange("p (h t) -> p h t", h=H)).then_inc(kT_ready, 1)
            dve.wait_ge(dec_ready, 4)
            elp = Ep[:, :, 0:512].rearrange("p h (c t) -> p h c t", c=8)[:, :, :, CHUNK - 1]
            els = Ep[:, :, 512:640].rearrange("p h (c t) -> p h c t", c=8)[:, :, :, Q - 1]
            dve.tensor_tensor(gl[:, :, 0:8], em[:, :, 0:8], elp, ALU.mult)
            step(dve.tensor_tensor(gl[:, :, 8:16], em[:, :, 8:16], els, ALU.mult))
            for i in range(NT):
                dve.wait_ge(gT_done, i + 1)
                ts = slice(i * P, (i + 1) * P)
                b4 = bank[4 + i % 2][:, :].rearrange("p (a h t) -> p a h t", a=2, h=2)
                dve.scalar_tensor_tensor(out=qt[:, :, ts], in0=b4[:, 0], scalar=DH ** -0.5, in1=Ep[:, :, ts],
                                         op0=ALU.mult, op1=ALU.mult).then_inc(gqk_ready, 1)
                dve.tensor_tensor(kt[:, :, ts], b4[:, 1], Em[:, :, ts], ALU.mult).then_inc(gqk_ready, 1)
            dve.wait_ge(gqk_ready, 2 * NT)
            dve.wait_ge(at_zero, 2)

            def stream_operands():
                for hp in range(2):
                    dve.tensor_copy(bass.AP(qz.tensor, qz[:, hp, 0, 0:Q].offset, [qz.ap[0], [P + Q, NB], [1, Q]]),
                                    qt[:, hp, 512:640].rearrange("p (b t) -> p b t", b=NB)).then_inc(qz_ready, 1)
                dve.wait_ge(ld_state, 16)
                for hp in range(2):
                    dve.tensor_tensor(Ss[:, :, hp, :], S0[:, :, hp, :], bc(em[:, hp, 8:16], [P, NB, DV]),
                                      ALU.mult).then_inc(Ss_ready, 1)
                dve.wait_ge(ktok_ready, NT)
                for b in range(NB):
                    dve.tensor_scalar(kz[:, b, :], ktok[:, NP, :], bmask[:, b:b + 1], None, ALU.mult).then_inc(kz_ready, 1)

            def masked(i):
                tri = tri64 if i < NP else tri16
                for h2 in range(2):
                    dve.wait_ge(sc_done, 2 * i + h2 + 1)
                    for hp in range(2):
                        ins = dve.copy_predicated(AT[:, i, hp, h2, :], tri[:, :].bitcast(U32),
                                                  bank[6 + h2][:, hp * P:(hp + 1) * P])
                    ins.then_inc(AT_ready, 1)

            def states(i):
                dve.wait_ge(U_done, i + 1)
                tmpU = tmpS[i % 2]
                for j in range(2):
                    el = Ep[:, :, (2 * i + j) * CHUNK + CHUNK - 1]
                    ins = dve.tensor_tensor(tmpU[:, j], bank[4 + j][:, 0:256].rearrange("p (h v) -> p h v", h=2),
                                            bc(el, [P, 2, DV]), ALU.mult)
                ins.then_inc(U_used, 1)
                dve.wait_ge(U_used, i + 1)
                for j in range(2):
                    c = 2 * i + j
                    if c >= 1:
                        for hp in range(2):
                            ins = dve.tensor_scalar(St[:, c, hp, :], S[:, hp, :], em[:, hp, c:c + 1], None, ALU.mult)
                    else:
                        ins = dve.nop()
                    ins.then_inc(St_ready, 1)
                    for hp in range(2):
                        if c == 0:
                            ins = dve.tensor_copy(S[:, hp, :], tmpU[:, j, hp, :])
                        else:
                            ins = dve.scalar_tensor_tensor(out=S[:, hp, :], in0=S[:, hp, :], scalar=gl[:, hp, c:c + 1],
                                                           in1=tmpU[:, j, hp, :], op0=ALU.mult, op1=ALU.add)
                    step(ins)

            def go_out(i):
                dve.wait_ge(go_sq, i + 1)
                dve.wait_ge(silu_ready, 1)
                gv = z(C_GR, i).rearrange("p (h e v) -> p h e v", h=2, e=2)
                for h2 in range(2):
                    ins = dve.tensor_tensor(gv[:, :, h2, :], gv[:, :, h2, :],
                                            bank[2 * (i % 2) + h2][:, 0:256].rearrange("p (h v) -> p h v", h=2), ALU.mult)
                    ins.then_inc(go_ready, 1)

            for i in range(NT):
                masked(i)
                if i < NP:
                    states(i)
                if i == 0:
                    stream_operands()
                if i == 1:
                    dve.wait_ge(Ss_ready, 2)
                    for hp in range(2):
                        step(dve.tensor_tensor(S0[:, :, hp, :], S0[:, :, hp, :], bc(gl[:, hp, 8:16], [P, NB, DV]), ALU.mult))
                if i >= 2:
                    go_out(i - 2)
                if i == NP:
                    dve.nop().then_inc(sp_ready, 1)
                    for b2 in range(4):
                        dve.wait_ge(U_done, NP + b2 + 1)
                        u = bank[4 + b2][:, :].rearrange("p (b h v) -> p b h v", b=2, h=2)
                        els2 = els[:, :, 2 * b2:2 * b2 + 2].rearrange("p h b -> p b h")
                        step(dve.tensor_tensor(tmpS[b2 % 2], u, bc(els2, [P, 2, 2, DV]), ALU.mult))
                        sb2 = S0[:, 2 * b2:2 * b2 + 2]
                        ins = dve.tensor_tensor(sb2, sb2, tmpS[b2 % 2], ALU.add)
                    step(ins)
                    dve.nop().then_inc(ss_ready, 1)
            go_out(NP - 1)
            go_out(NP)
            items = [(i, h) for i in range(NP) for h in range(H)]
            NI = len(items)

            def maxes(m):
                i, h = items[m]
                L = (i + 1) * P
                dve.wait_ge(s_done, m + 1)
                if m >= 2:
                    dve.wait_ge(e_ready, 2 * (m - 1))
                for mm in range(2):
                    ins = dve.tensor_reduce(mx[:, m % 2, mm:mm + 1], bank[2 * (m % 2) + mm][:, 0:L], AX.X, ALU.max)
                step(ins)
                dve.tensor_scalar(nm[:, m % 2, :], mx[:, m % 2, :], -DH ** -0.5, None, ALU.mult).then_inc(nm_ready, 1)

            def combine(m):
                i, h = items[m]
                L = (i + 1) * P
                e0, e1 = E[m % NER][0][:, 0:L], E[m % NER][1][:, 0:L]
                dve.wait_ge(e_ready, 2 * m + 2)
                step(dve.reciprocal(ri[:, m % 2, :], es[:, m % 2, :]))
                step(dve.tensor_scalar(e1, e1, ri[:, m % 2, 1:2], nlam[:, 0:1], ALU.mult, ALU.mult))
                dve.scalar_tensor_tensor(out=e0, in0=e0, scalar=ri[:, m % 2, 0:1], in1=e1,
                                         op0=ALU.mult, op1=ALU.add).then_inc(p_ready, 1)

            def ao_out(i, src):
                dve.wait_ge(o_sq, i + 1)
                dve.tensor_copy(z(C_Q, i), src[:, :]).then_inc(ao_ready, 1)

            for m in range(NI + 3):
                if m < NI:
                    maxes(m)
                if 1 <= m <= NI:
                    combine(m - 1)
                if m >= 3 and (m - 3) % H == H - 1:
                    i = (m - 3) // H
                    ao_out(i, bank[6 + i % 2])
            dve.wait_ge(kT_ready, NT)
            dve.wait_ge(qT_ready, NT)
            dve.wait_ge(att_zero, 2)
            for mm in range(2):
                for h in range(H):
                    src = qT[64 * mm:64 * mm + 64, h, 512:640].rearrange("p (b q) -> p b q", b=NB)
                    ins = dve.tensor_copy(qbd[64 * mm:64 * mm + 64, :, h, mm, :], src)
            ins.then_inc(qbd_ready, 1)

            def d_max(b):
                dve.wait_ge(d_s_done, b + 1)
                if b >= 2:
                    dve.wait_ge(d_e_ready, 2 * (b - 1))
                dve.tensor_reduce(mx[:, b % 2, 0:1], bank[2 * (b % 2)][:, :], AX.X, ALU.max)
                step(dve.tensor_reduce(mx[:, b % 2, 1:2], bank[2 * (b % 2) + 1][:, 0:Q], AX.X, ALU.max))
                dve.tensor_scalar(nm[:, b % 2, 0:1], mx[:, b % 2, 0:1], mx[:, b % 2, 1:2], -DH ** -0.5,
                                  ALU.max, ALU.mult).then_inc(d_nm_ready, 1)

            def d_comb(b):
                dve.wait_ge(d_e_ready, 2 * b + 2)
                if b >= 2:
                    dve.wait_ge(d_pt_done, b - 1)
                step(dve.tensor_tensor(ri[:, b % 2, 0:1], es[:, b % 2, 0:1], es[:, b % 2, 1:2], ALU.add))
                step(dve.reciprocal(ri[:, b % 2, 1:2], ri[:, b % 2, 0:1]))
                cv = Cb[:, b % 2, :].rearrange("p (h e q) -> p h e q", h=H, e=2)[:, :, b % 2, :]
                dve.tensor_scalar(cv, Cm[:, :].rearrange("p (h q) -> p h q", h=H), ri[:, b % 2, 1:2], None,
                                  ALU.mult).then_inc(cb_ready, 1)

            def normed(n):
                i, gla = (n // 2, n % 2) if n < 2 * NP else (NP, 2 * NP + 1 - n)
                c, a = (C_GR, H) if gla else (C_Q, 0)
                v = z(c, i).rearrange("p (h v) -> p h v", h=H)
                dve.tensor_tensor(v, v, bc(ro[:, i, a:a + H], [P, H, DV]), ALU.mult).then_inc(mix_ready, 1)

            def wo_low(n):
                dve.wait_ge(woH_ready, n + 1)
                c = WO_ORDER[n]
                for a, w, place in woH[c]:
                    part = slice(c * D + a, c * D + a + w)
                    ins = dve.tensor_tensor(W_r[:, part], W[:, part], place.bitcast(F32), ALU.subtract)
                ins.then_inc(woL_ready, 1)

            def mix_a(i):
                dve.wait_ge(mT_done, 2 * i + 1)
                if i < NP:
                    dve.tensor_scalar(mixT[:, 0:H, i * P:(i + 1) * P],
                                      bank[2 * (i % 2)][:, :].rearrange("p (c t) -> p c t", c=H),
                                      ag8[:, 0:1], None, ALU.mult).then_inc(mT_a, 1)
                else:
                    for b2 in range(NB // 2):
                        ins = dve.tensor_scalar(mixT[:, 0:H, NP * P + 32 * b2:NP * P + 32 * b2 + 32],
                                                bank[0][:, b2 * P:(b2 + 1) * P].rearrange("p (h t) -> p h t", h=H),
                                                ag8[:, 0:1], None, ALU.mult)
                    ins.then_inc(mT_a, 1)
                dve.wait_ge(mixH_ready, i + 1)
                ts = slice(i * P, (i + 1) * P)
                dve.tensor_tensor(mixL[:, :, ts], mixT[:, :, ts], mixH[:, :, ts].bitcast(F32),
                                  ALU.subtract).then_inc(mixL_ready, 1)

            dve.wait_ge(ostd, 2)
            dve.wait_ge(go_ready, 2 * NT)
            dve.wait_ge(ao_ready, NP)
            dve.reciprocal(ro[:, 0:NP, :], ro[:, 0:NP, :])
            step(dve.reciprocal(ro[:, NP, H:], ro[:, NP, H:]))
            for b in range(NB + 1):
                if b < NB:
                    d_max(b)
                if b >= 1:
                    d_comb(b - 1)
                normed(b)
            wo_low(0)
            wo_low(1)
            mix_a(0)
            wo_low(2)
            wo_low(3)
            ao_out(NP, bank[6])
            dve.wait_ge(ostd, 3)
            dve.wait_ge(ao_ready, NT)
            step(dve.reciprocal(ro[:, NP, 0:H], ro[:, NP, 0:H]))
            normed(2 * NP + 1)
            for i in range(1, NT):
                mix_a(i)

            def h2_out(i):
                for q in range(2):
                    dve.wait_ge(h2_done, 2 * i + q + 1)
                    if i >= 2:
                        dve.wait_ge(lg_done, i - 1)
                    dve.tensor_tensor(h2T[i % 2][:, 4 * q:4 * q + 4, :],
                                      bank[q][:, :].rearrange("p (c t) -> p c t", c=4),
                                      bc(g2[:, 4 * q:4 * q + 4], [P, 4, P]), ALU.mult).then_inc(h2_ready, 1)

            for i in range(NT):
                for hf in range(2):
                    dve.wait_ge(out_done, 2 * i + hf + 1)
                    ins = dve.tensor_tensor(X[:, i, hf * 512:(hf + 1) * 512], X[:, i, hf * 512:(hf + 1) * 512],
                                            bank[4 + 2 * (i % 2) + hf][:, :], ALU.add)
                    ins.then_inc(x2_ready, 1)
                dve.wait_ge(x2_ready, 2 * i + 2)
                if i >= 2:
                    dve.wait_ge(st_hn[i % 2], 16 * (i // 2))
                    dve.wait_ge(h2_done, 2 * (i - 1))
                dve.tensor_tensor_reduce(out=hn[i % 2], in0=X[:, i, :], in1=X[:, i, :], scale=1.0, scalar=0.0,
                                         op0=ALU.mult, op1=ALU.add, accum_out=ss2[:, i:i + 1]).then_inc(ssq2, 1)
                dve.wait_ge(std2, i + 1)
                dve.reciprocal(r2[:, i:i + 1], st2[:, i:i + 1]).then_inc(rstd2, 1)
                h2_out(i)
            step(dve.memset(Rt, 0.0))
            dve.wait_ge(lg_done, NT)
            step(dve.memset(Ms[:, NT * NE:], 0.0))
            step(dve.tensor_tensor(Lg, bank[3][:, 0:NT * NL].rearrange("p (i n) -> p i n", i=NT),
                                   br[:, :].unsqueeze(1).broadcast_to([P, NT, NL]), ALU.add))
            gl4 = Lg[:, :, 0:NG]
            ev = Lg[:, :, NG:NL].rearrange("p i (g e) -> p i g e", g=NG)

            def first_max(val, mxout, ohout, m2, w):
                step(dve.tensor_reduce(mxout, val, AX.X, ALU.max))
                step(dve.tensor_tensor(ohout, val, bc(mxout, [P, NT, w]), ALU.is_equal))
                step(dve.tensor_tensor(ohout, ohout, desc[:, 0:w].unsqueeze(1).broadcast_to([P, NT, w]), ALU.mult))
                step(dve.tensor_reduce(m2, ohout, AX.X, ALU.max))
                step(dve.tensor_tensor(ohout, ohout, bc(m2, [P, NT, w]), ALU.is_equal))

            first_max(gl4, gmax, goh, gm2, NG)
            dve.tensor_tensor(ge, gl4, bc(gmax, [P, NT, NG]), ALU.subtract).then_inc(gexp_in, 1)
            step(dve.tensor_tensor(egs, ev, bc(goh, [P, NT, NG, EPG]), ALU.mult))
            step(dve.tensor_reduce(esel[0], egs.rearrange("p i g e -> p i e g"), AX.X, ALU.add))
            first_max(esel[0], mk[:, 0], oh[0], mk2, EPG)
            step(dve.scalar_tensor_tensor(out=esel[1], in0=oh[0], scalar=NEG, in1=esel[0], op0=ALU.mult, op1=ALU.add))
            first_max(esel[1], mk[:, 1], oh[1], mk2, EPG)
            dve.tensor_tensor(dm, mk[:, 1], mk[:, 0], ALU.subtract).then_inc(gexp_in, 1)
            for k in range(2):
                ins = dve.tensor_tensor(M[:, k], bc(goh, [P, NT, NG, EPG]),
                                        oh[k].unsqueeze(2).broadcast_to([P, NT, NG, EPG]), ALU.mult)
            step(ins)
            Mf = M.rearrange("p k i g e -> p k (i g e)")
            dve.tensor_tensor(Ms[:, 0:NT * NE], Mf[:, 0], Mf[:, 1], ALU.add).then_inc(m_ready, 1)
            dve.wait_ge(gexp_out, 2)
            step(dve.tensor_reduce(gs, ge, AX.X, ALU.add))
            step(dve.scalar_tensor_tensor(out=den, in0=dm, scalar=1.0, in1=gs, op0=ALU.add, op1=ALU.mult))
            step(dve.reciprocal(wk[:, 0, :], den))
            step(dve.tensor_tensor(wk[:, 1, :], wk[:, 0, :], dm, ALU.mult))
            for k in range(2):
                mf = M[:, k].rearrange("p i g (n e) -> p i (g n) e", e=2)
                dve.tensor_reduce(pk[:, k], mf[:, :, :, 1], AX.X, ALU.add)
                ins = dve.tensor_reduce(Mp[:, 1, k], mf, AX.X, ALU.add)
            step(ins)
            for k in range(2):
                ins = dve.tensor_tensor(Mp[:, 0, k], Mp[:, 1, k], bc(tk[:, 0, k, :], [P, NT, PAIRS]), ALU.mult)
            step(ins)
            for k in range(2):
                ins = dve.tensor_tensor(Mp[:, 1, k], Mp[:, 1, k], bc(tk[:, 1, k, :], [P, NT, PAIRS]), ALU.mult)
            step(ins)
            dve.wait_ge(rank_done, 1)
            step(dve.tensor_tensor(mprod, Mf, bank[0][:, 0:NT * NE].unsqueeze(1).broadcast_to([P, 2, NT * NE]),
                                   ALU.mult))
            step(dve.tensor_reduce(rk, mprod.rearrange("p k (i n) -> p k i n", i=NT), AX.X, ALU.add))
            dve.tensor_reduce(cnt, bank[0][:, NT * NE:(NT + 1) * NE], AX.X, ALU.max)
            step(dve.tensor_tensor(cmpr, bc(rk.rearrange("p k i -> p (k i)"), [P, 2 * NT, ROUNDS - 1]),
                                   thr[:, :].unsqueeze(1).broadcast_to([P, 2 * NT, ROUNDS - 1]), ALU.is_ge))
            step(dve.tensor_reduce(rn.rearrange("p k i -> p (k i)"), cmpr, AX.X, ALU.add))
            step(dve.scalar_tensor_tensor(out=loc, in0=rn, scalar=-float(CAP), in1=rk, op0=ALU.mult, op1=ALU.add))
            step(dve.scalar_tensor_tensor(out=qk, in0=pk, scalar=float(CAP), in1=loc, op0=ALU.mult, op1=ALU.add))
            step(dve.tensor_tensor(OH, iota128[:, :].unsqueeze(1).broadcast_to([P, 2 * NT, P]),
                                   bc(qk.rearrange("p k i -> p (k i)"), [P, 2 * NT, P]), ALU.is_equal))
            TS = 4

            def tables(r, later):
                def tstep(k, ins):
                    ins.then_inc(tab_step, 1)
                    dve.wait_ge(tab_step, r * TS + k)

                if later:
                    for q in range(2):
                        dve.wait_ge(st_y[q], r * (PAIRS // 2 * 16))
                tstep(1, dve.tensor_scalar(rmask, rn, cur[:, 0:1], None, ALU.is_equal))
                tstep(2, dve.tensor_scalar(cur[:, :], cur[:, :], 1.0, None, ALU.add))
                for a in range(2):
                    for k in range(2):
                        ins = dve.tensor_tensor(Rt[:, k, :, a, 0:PAIRS], Mp[:, a, k], bc(rmask[:, k], [P, NT, PAIRS]),
                                                ALU.mult)
                tstep(3, ins)
                dve.nop().then_inc(tab_in, 1)
                if not later:
                    step(dve.tensor_scalar(ovf_f, cnt, float(CAP), None, ALU.is_gt))
                    dve.tensor_copy(ovf[:, :], ovf_f).then_inc(ovf_ready, 1)
                dve.wait_ge(tab_done, r + 1)
                n1 = PAIRS + 1
                tstep(4, dve.tensor_scalar(none, bank[0][:, 0:2 * n1], 0.0, 4096.0, ALU.is_equal, ALU.mult))
                for t, a in ((dst, n1), (idx, 0)):
                    ins = dve.scalar_tensor_tensor(out=t[:, :], in0=bank[0][:, a:a + n1], scalar=-1.0,
                                                   in1=none[:, a:a + n1], op0=ALU.add, op1=ALU.add)
                ins.then_inc(idx_ready, 1)

            def xsT_out(r, p, q):
                for hf in range(2):
                    dve.wait_ge(xsT_done, r * 2 * (PAIRS + 1) + 2 * p + hf + 1)
                    dve.tensor_tensor(xsT[q][:, 4 * hf:4 * hf + 4, :],
                                      bank[hf][:, :].rearrange("p (c s) -> p c s", c=4),
                                      bc(g2[:, 4 * hf:4 * hf + 4], [P, 4, P]), ALU.mult).then_inc(xsT_ready, 1)

            def gated(r, g, q):
                dve.wait_ge(sil_ready, (r * 8 + g) * 2 + q + 1)
                dve.tensor_tensor(hs[q], sil[q], bank[2 + q][:, FE:2 * FE], ALU.mult).then_inc(h_ready, 1)

            def moe(r, later):
                tables(r, later)
                xsT_out(r, 0, 0)
                with dve.Fori(0, NE // 4) as g:
                    gated(r, g, 0)
                    xsT_out(r, 2 * g + 1, 1)
                    gated(r, g, 1)
                    xsT_out(r, 2 * g + 2, 0)

            moe(0, False)
            dve.wait_ge(ovf_ready, 1)
            with dve.If(dve.value_load(ovf[0:1, 0:1]) > 0):
                with dve.Fori(1, ROUNDS) as r:
                    moe(r, True)
            for i in range(NT):
                dve.wait_ge(ygath[i], 16)
                for k in range(2):
                    if 2 * i + k:
                        dve.wait_ge(ysum, 2 * i + k)
                    dve.scalar_tensor_tensor(out=X[:, i, :], in0=yg[i][:, k * D:(k + 1) * D],
                                             scalar=wk[:, k, i:i + 1], in1=X[:, i, :], op0=ALU.mult,
                                             op1=ALU.add).then_inc(ysum, 1)

        @block.tensor
        def _(pe):
            pe.wait_ge(consts, 1)
            for i in range(NT):
                pe.wait_ge(xn_ready, i + 1)
                if i >= 2:
                    pe.wait_ge(hT_ready, 2 * (i - 1))
                for q in range(2):
                    for c in range(4):
                        ins = pe.transpose(bank[2 * (i % 2) + q][:, c * P:(c + 1) * P],
                                           xn[i % 2][:, (4 * q + c) * P:(4 * q + c + 1) * P], ident[:, :])
                    ins.then_inc(xT_done, 1)

            def z_chunk(c, first=False):
                for k in range(2):
                    pe.wait_ge(wL_ready, 2 * c + k + 1)
                    for i in range(NT):
                        if first and k == 0:
                            pe.wait_ge(hL_ready, i + 1)
                        if k == 0:
                            pe.wait_ge(z_free, NT * c + i + 1)
                        for s in range(DC // 2):
                            cols = slice(s * 512, (s + 1) * 512)
                            d = k * DC // 2 + s
                            pe.matmul(bank[i][:, :], hH[:, d, i, :], wH[k][:, cols], start=(d == 0), stop=False)
                            pe.matmul(bank[i][:, :], hH[:, d, i, :], wL[k][:, cols], start=False, stop=False)
                            ins = pe.matmul(bank[i][:, :], hL[:, d, i, :], wH[k][:, cols], start=False,
                                            stop=(d == DC - 1))
                        if k == 1:
                            ins.then_inc(proj_done, 1)
                    if k == 0:
                        ins.then_inc(half_done, 1)

            pe.wait_ge(hT_ready, 2 * NT)
            z_chunk(0, first=True)
            pe.wait_ge(wgaL_ready, 1)
            for d in range(DC):
                r = slice(d * RANK, (d + 1) * RANK)
                for n, (w, h) in enumerate(((wgaH, hH), (wgaH, hL), (wgaL, hH))):
                    first, last = d == 0 and n == 0, d == DC - 1 and n == 2
                    pe.matmul(bank[5][0:RANK, :], w[:, r], h[:, d, 0:NP, :].rearrange("p i t -> p (i t)"),
                              start=first, stop=last)
                    ins = pe.matmul(bank[6][0:RANK, 0:P], w[:, r], h[:, d, NP, :], start=first, stop=last)
            ins.then_inc(ga_done, 1)
            z_chunk(1)
            pe.wait_ge(gaT_ready, 2)
            for i in range(NT):
                ins = pe.matmul(bank[5 + i // 2][:, (i % 2) * 256:(i % 2) * 256 + 256],
                                gaT[0:RANK + 1, i * P:(i + 1) * P], wa2[0:RANK + 1, :], start=True, stop=True)
            ins.then_inc(pre_done, 1)
            with pe.Fori(2, 6) as c:
                z_chunk(c)

            pe.wait_ge(la_ready, 1)
            for i in range(NT):
                for hp in range(2):
                    o = (i % 2) * 256 + hp * P
                    ins = pe.matmul(bank[5 + i // 2][:, o:o + P], la[:, i, hp * P:(hp + 1) * P],
                                    (tri64 if i < NP else tri16)[:, :], start=True, stop=True)
            ins.then_inc(b_done, 1)
            for m in range(2 * NT):
                i = m % NT
                if m < NT:
                    pe.wait_ge(k_ready, i + 1)
                else:
                    pe.wait_ge(q_ready, i + 1)
                if m < 4:
                    pe.wait_ge(z_free, 5 + 25 + m + 1)
                elif m < NT + 4:
                    pe.wait_ge(kT_ready, m - 3)
                else:
                    pe.wait_ge(qT_ready, m - 3 - NT)
                for h in range(H):
                    ins = pe.transpose(bank[m % 4][:, h * P:(h + 1) * P],
                                       z(C_K if m < NT else C_Q, i, h * P, (h + 1) * P), ident[:, :])
                ins.then_inc(qkT_done, 1)

            def g_tr(i):
                if i == 0:
                    pe.wait_ge(z_free, 5 + 30)
                    pe.wait_ge(b_ready, 3)
                if i >= 2:
                    pe.wait_ge(gqk_ready, 2 * (i - 1))
                for t in range(4):
                    ins = pe.transpose(bank[4 + i % 2][:, t * P:(t + 1) * P], z(C_G, i, t * P, (t + 1) * P), ident[:, :])
                ins.then_inc(gT_done, 1)

            def ktok_tr(i):
                pe.wait_ge(gqk_ready, 2 * i + 2)
                if i >= 2:
                    pe.wait_ge(ktok_ready, i - 1)
                for hp in range(2):
                    ins = pe.transpose(bank[6 + i % 2][:, hp * P:(hp + 1) * P], kt[:, hp, i * P:(i + 1) * P], ident[:, :])
                ins.then_inc(ktok_done, 1)

            g_tr(0)
            for i in range(NT):
                if i + 1 < NT:
                    g_tr(i + 1)
                ktok_tr(i)

            def scores(i):
                if i == 0:
                    pe.wait_ge(ktok_ready, NT)
                else:
                    pe.wait_ge(AT_ready, 2 * i)
                for h2 in range(2):
                    rows = slice(64 * h2, 64 * h2 + 64)
                    for hp in range(2):
                        ins = pe.matmul(bank[6 + h2][:, hp * P:(hp + 1) * P], kt[rows, hp, i * P:(i + 1) * P],
                                        qt[rows, hp, i * P:(i + 1) * P], start=True, stop=True)
                    ins.then_inc(sc_done, 1)

            def updates(i):
                pe.wait_ge(ktok_ready, NT)
                if i >= 1:
                    pe.wait_ge(U_used, i)
                for j in range(2):
                    rows = slice(64 * j, 64 * j + 64)
                    for hp in range(2):
                        for h2 in range(2):
                            o = hp * P + 64 * h2
                            ins = pe.matmul(bank[4 + j][64 * h2:64 * h2 + 64, hp * P:(hp + 1) * P],
                                            ktok[rows, i, o:o + 64],
                                            z(C_GV, i)[rows, (2 * hp + h2) * P:(2 * hp + h2 + 1) * P],
                                            start=True, stop=True)
                ins.then_inc(U_done, 1)

            def s_updates(b2):
                pe.wait_ge(kz_ready, NB)
                if b2 == 0:
                    pe.wait_ge(U_used, NP)
                if b2 == 2:
                    pe.wait_ge(AT_ready, 2 * NT)
                for b in (2 * b2, 2 * b2 + 1):
                    for hp in range(2):
                        for h2 in range(2):
                            o = hp * P + 64 * h2
                            c = (b % 2) * 256 + hp * P
                            ins = pe.matmul(bank[4 + b2][64 * h2:64 * h2 + 64, c:c + P], kz[:, b, o:o + 64],
                                            z(C_GV, NP, (2 * hp + h2) * P, (2 * hp + h2 + 1) * P), start=True, stop=True)
                ins.then_inc(U_done, 1)

            def outputs(i):
                pe.wait_ge(AT_ready, 2 * i + 2)
                if i < 2:
                    pe.wait_ge(kT_ready, NT)
                    pe.wait_ge(qT_ready, NT)
                else:
                    pe.wait_ge(go_sq, i - 1)
                    pe.wait_ge(go_ready, 2 * (i - 1))
                if i < NP:
                    pe.wait_ge(St_ready, 2 * i + 2)
                else:
                    pe.wait_ge(Ss_ready, 2)
                    pe.wait_ge(qz_ready, 2)
                for h2 in range(2):
                    rows = slice(64 * h2, 64 * h2 + 64)
                    for hp in range(2):
                        o = bank[2 * (i % 2) + h2]
                        v = slice(hp * P, (hp + 1) * P)
                        h = 2 * hp + h2
                        pe.matmul(o[:, v], AT[:, i, hp, h2, :], z(C_GV, i, h * P, (h + 1) * P), start=True, stop=False,
                                  skip_group_check=True)
                        if i < NP:
                            for j in range(2):
                                if 2 * i + j:
                                    t = i * P + j * CHUNK
                                    ins = pe.matmul(o[64 * j:64 * j + 64, v], qt[rows, hp, t:t + CHUNK],
                                                    St[rows, 2 * i + j, hp, :], start=False, stop=True,
                                                    skip_group_check=True)
                        else:
                            for b in range(NB):
                                ins = pe.matmul(o[:, v], qz[rows, hp, b, :], Ss[rows, b, hp, :], start=False,
                                                stop=(b == NB - 1), skip_group_check=True)
                ins.then_inc(go_done, 1)

            for i in range(NT):
                scores(i)
                if i < NP:
                    updates(i)
                else:
                    for b2 in range(4):
                        s_updates(b2)
                if i:
                    outputs(i - 1)
            outputs(NP)

            items = [(i, h) for i in range(NP) for h in range(H)]
            NI = len(items)

            def att_scores(m):
                i, h = items[m]
                L = (i + 1) * P
                if m < 2:
                    pe.wait_ge(go_sq, NT)
                    pe.wait_ge(go_ready, 2 * NT)
                else:
                    pe.wait_ge(e_ready, 2 * (m - 1))
                for mm in range(2):
                    rows = slice(64 * mm, 64 * mm + 64)
                    o = bank[2 * (m % 2) + mm]
                    pe.matmul(o[:, 0:L], qT[rows, h, i * P:(i + 1) * P], kT[rows, h, 0:L], start=True, stop=False,
                              skip_group_check=True)
                    ins = pe.matmul(o[:, L - CHUNK:L], mA[rows, :], mB[rows, :], start=False, stop=True,
                                    skip_group_check=True)
                ins.then_inc(s_done, 1)

            def att_pt(m):
                i, h = items[m]
                pe.wait_ge(p_ready, m + 1)
                if m >= 2:
                    pe.wait_ge(pt_ready, m - 1)
                else:
                    pe.wait_ge(ss_ready, 1)
                for j in range(i + 1):
                    ins = pe.transpose(bank[4 + m % 2][:, j * P:(j + 1) * P], E[m % NER][0][:, j * P:(j + 1) * P],
                                       ident[:, :])
                ins.then_inc(pt_done, 1)

            def att_pv(m):
                i, h = items[m]
                pe.wait_ge(pt_ready, m + 1)
                if h == 0 and i >= 2:
                    pe.wait_ge(o_sq, i - 1)
                    pe.wait_ge(ao_ready, i - 1)
                for j in range(i + 1):
                    ins = pe.matmul(bank[6 + i % 2][:, h * P:(h + 1) * P], PT[m % 2][:, j * P:(j + 1) * P],
                                    z(C_V, j, h * P, (h + 1) * P), start=(j == 0), stop=(j == i))
                ins.then_inc(o_done, 1)

            for m in range(NI + 3):
                if m < NI:
                    att_scores(m)
                if 2 <= m < NI + 2:
                    att_pt(m - 2)
                if m >= 3:
                    att_pv(m - 3)

            def d_scores(b):
                pe.wait_ge(ld_k[b % NKV], 16 * (b // NKV + 1))
                if b < 2:
                    pe.wait_ge(e_ready, 2 * NI)
                    pe.wait_ge(qbd_ready, 1)
                else:
                    pe.wait_ge(d_e_ready, 2 * (b - 1))
                w = [qbd[:, b, h, :, :].rearrange("p m q -> p (m q)") for h in range(H)]
                for h in range(H):
                    pe.matmul(bank[2 * (b % 2)][32 * h:32 * h + 32, :], w[h], Kc[b % NKV][:, h, :], start=True, stop=True,
                              tile_position=(0, 32 * h))
                for h in range(H):
                    ins = pe.matmul(bank[2 * (b % 2) + 1][32 * h:32 * h + 32, 0:Q], w[h],
                                    kT[:, h, 512 + b * Q:512 + (b + 1) * Q], start=True, stop=True,
                                    tile_position=(0, 32 * h))
                ins.then_inc(d_s_done, 1)

            def d_pt(b):
                pe.wait_ge(cb_ready, b + 1)
                if b >= 2:
                    pe.wait_ge(d_pt_ready, 2 * (b - 1))
                else:
                    pe.wait_ge(pt_ready, NI)
                for j in range(4):
                    pe.matmul(bank[4 + b % 2][:, j * P:(j + 1) * P], E[b % NER][0][:, j * P:(j + 1) * P],
                              Cb[:, b % 2, :], start=True, stop=True)
                if b == 0:
                    pe.wait_ge(o_sq, NP)
                    pe.wait_ge(ao_ready, NP)
                else:
                    pe.wait_ge(d_pt_ready, 2 * b)
                pe.matmul(bank[7][:, 0:P], enew[:, b, :], Cb[:, b % 2, :], start=True, stop=True).then_inc(d_pt_done, 1)

            def d_pv(b):
                pe.wait_ge(d_pt_ready, 2 * b + 2)
                pe.wait_ge(ld_v[b % NKV], 16 * (b // NKV + 1))
                for j in range(5):
                    for h in range(H):
                        rhs = Vc[b % NKV][:, j, h * P:(h + 1) * P] if j < 4 else z(C_V, NP, h * P, (h + 1) * P)
                        o = j * P + 32 * h
                        ins = pe.matmul(bank[6][32 * h:32 * h + 32, (b // 2) * P:(b // 2 + 1) * P],
                                        PT[b % 2][:, o:o + 32], rhs, start=(b % 2 == 0 and j == 0),
                                        stop=(b % 2 == 1 and j == 4), tile_position=(0, 32 * h), skip_group_check=True)
                ins.then_inc(d_pv_done, 1)

            for b in range(NB + 3):
                if b < NB:
                    d_scores(b)
                if 2 <= b < NB + 2:
                    d_pt(b - 2)
                if b >= 3:
                    d_pv(b - 3)

            def mix_tr(i):
                for q, c in ((0, C_Q), (1, C_GR)):
                    pe.wait_ge(mix_ready, 2 * i + q + 1 if i < NP else 2 * NT)
                    if i >= 2:
                        pe.wait_ge(mT_a, i - 1)
                        pe.wait_ge(mT_g, i - 1)
                    for h in range(H):
                        ins = pe.transpose(bank[2 * (i % 2) + q][:, h * P:(h + 1) * P], z(c, i, h * P, (h + 1) * P),
                                           ident[:, :])
                    ins.then_inc(mT_done, 1)

            def out_proj(i, hf):
                if hf == 0:
                    pe.wait_ge(mixL_ready, i + 1)
                if i == 1:
                    pe.wait_ge(o_sq, NT)
                    pe.wait_ge(ao_ready, NT)
                if i >= 2:
                    pe.wait_ge(x2_ready, 2 * (i - 2) + hf + 1)
                out = bank[4 + 2 * (i % 2) + hf][:, :]
                ts, cols = slice(i * P, (i + 1) * P), slice(hf * 512, (hf + 1) * 512)
                for n, c0 in enumerate(WO_ORDER):
                    if i == 0 and hf == 0:
                        pe.wait_ge(woL_ready, n + 1)
                    for j in range(2):
                        wh = wo_high_of(c0, j * D + hf * 512)
                        pe.matmul(out, mixH[:, c0 + j, ts], wh, start=(n == 0 and j == 0), stop=False)
                        pe.matmul(out, mixH[:, c0 + j, ts], woL[:, c0 + j, cols], start=False, stop=False)
                        ins = pe.matmul(out, mixL[:, c0 + j, ts], wh, start=False, stop=(n == 3 and j == 1))
                ins.then_inc(out_done, 1)

            def h2_tr(i):
                pe.wait_ge(hn_ready, i + 1)
                if i == 0:
                    pe.wait_ge(mT_a, NT)
                    pe.wait_ge(mT_g, NT)
                for q in range(2):
                    if i >= 1:
                        pe.wait_ge(h2_ready, 2 * (i - 1) + q + 1)
                    for c in range(4):
                        ins = pe.transpose(bank[q][:, c * P:(c + 1) * P], hn[i % 2][:, (4 * q + c) * P:(4 * q + c + 1) * P],
                                           ident[:, :])
                    ins.then_inc(h2_done, 1)

            def router(i):
                pe.wait_ge(h2_ready, 2 * i + 2)
                for c in range(DC):
                    ins = pe.matmul(bank[3][:, i * NL:(i + 1) * NL], h2T[i % 2][:, c, :], wr[:, c, :],
                                    start=(c == 0), stop=(c == DC - 1))
                ins.then_inc(lg_done, 1)

            mix_tr(0)
            mix_tr(1)
            out_proj(0, 0)
            mix_tr(2)
            out_proj(0, 1)
            mix_tr(3)
            mix_tr(4)
            out_proj(1, 0)
            out_proj(1, 1)
            h2_tr(0)
            for i in range(1, NT):
                if i + 1 < NT:
                    out_proj(i + 1, 0)
                if i == 1:
                    router(0)
                h2_tr(i)
                if i + 1 < NT:
                    out_proj(i + 1, 1)
                router(i)
            pe.wait_ge(m_ready, 1)
            pe.matmul(bank[0][:, 0:(NT + 1) * NE], strict[:, :], Ms, start=True, stop=False, skip_group_check=True)
            for d in range(1, NT + 1):
                ins = pe.matmul(bank[0][:, d * NE:(NT + 1) * NE], ones[:, :], Ms[:, 0:(NT + 1 - d) * NE],
                                start=False, stop=(d == NT), skip_group_check=True)
            ins.then_inc(rank_done, 1)

            def tables(r):
                pe.wait_ge(tab_in, r + 1)
                for m in range(2 * NT):
                    ins = pe.matmul(bank[0][:, 0:2 * (PAIRS + 1)], OH[:, m, :],
                                    Rt[:, m // NT, m % NT].rearrange("p a n -> p (a n)"), start=(m == 0),
                                    stop=(m == 2 * NT - 1))
                ins.then_inc(tab_done, 1)

            def xs_tr(r, p, q, half_p):
                pe.wait_ge(gath[q], (r * (PAIRS // 2 + 1 - q) + half_p + 1) * 16)
                for hf in range(2):
                    if not (isinstance(p, int) and isinstance(r, int) and p == 0 and r == 0):
                        pe.wait_ge(xsT_ready, (r * (PAIRS + 1) + p) * 2 + hf - 1)
                    for c in range(4):
                        ins = pe.transpose(bank[hf][:, c * P:(c + 1) * P],
                                           xs[q][:, (4 * hf + c) * P:(4 * hf + c + 1) * P], ident[:, :])
                    ins.then_inc(xsT_done, 1)

            def gate_up(r, g, q, early=False):
                wgu = [gu4 if early and j == 0 else egu[2 * q + j] for j in range(2)]
                for j in range(2):
                    pe.wait_ge(ld_gu[2 * q + j], (r * 8 + g + 1) * 16)
                pe.wait_ge(xsT_ready, (r * (PAIRS + 1) + 2 * g + q + 1) * 2)
                for c in range(DC):
                    for j in range(2):
                        ins = pe.matmul(bank[2 + q][CAP * j:CAP * j + CAP, :], xsT[q][:, c, j * CAP:(j + 1) * CAP],
                                        wgu[j][:, c, :], start=(c == 0), stop=(c == DC - 1),
                                        tile_position=(0, CAP * j))
                ins.then_inc(gu_done, 1)

            def hidden_tr(r, g, q):
                pe.wait_ge(h_ready, (r * 8 + g) * 2 + q + 1)
                for f in range(2):
                    ins = pe.transpose(bank[2 + q][:, f * P:(f + 1) * P], hs[q][:, f * P:(f + 1) * P], ident[:, :])
                ins.then_inc(hT_done, 1)

            def down_proj(r, g, q, first, early=False):
                wdn = [dn4 if early and j == 0 else edn[2 * q + j] for j in range(2)]
                pe.wait_ge(hTs_ready, (r * 8 + g) * 2 + q + 1)
                for j in range(2):
                    pe.wait_ge(ld_dn[2 * q + j], (r * 8 + g + 1) * 16)
                if not first:
                    pe.wait_ge(ysb_ready, r * 2 * PAIRS + g * 4 + 2 * q - 2)
                for hf in range(2):
                    for f in range(2):
                        for j in range(2):
                            ins = pe.matmul(bank[4 + 2 * q + hf][CAP * j:CAP * j + CAP, :],
                                            hTs[q][:, f, j * CAP:(j + 1) * CAP],
                                            wdn[j][:, f, hf * 512:(hf + 1) * 512], start=(f == 0),
                                            stop=(f == 1), tile_position=(0, CAP * j))
                ins.then_inc(dn_done, 1)

            def group(r, g, first=False, early=False):
                gate_up(r, g, 0, early)
                xs_tr(r, 2 * g + 1, 1, g)
                hidden_tr(r, g, 0)
                gate_up(r, g, 1)
                down_proj(r, g, 0, first, early)
                xs_tr(r, 2 * g + 2, 0, g + 1)
                hidden_tr(r, g, 1)
                down_proj(r, g, 1, first)

            tables(0)
            xs_tr(0, 0, 0, 0)
            group(0, 0, first=True)
            group(0, 1, early=True)
            with pe.Fori(2, NE // 4) as g:
                group(0, g)
            pe.wait_ge(ovf_ready, 1)
            with pe.If(pe.value_load(ovf[0:1, 0:1]) > 0):
                with pe.Fori(1, ROUNDS) as r:
                    tables(r)
                    xs_tr(r, 0, 0, 0)
                    with pe.Fori(0, NE // 4) as g:
                        group(r, g)


_OUTS = [("y_out", (NT, P, D)), ("k_out", (NT, P, 512)), ("v_out", (NT, P, 512)),
         ("sp_out", (P, 2, DV)), ("ss_out", (P, NB, 2, DV))]


def kernel(x_prompt, x_sample, cache_k, cache_v, state_gla, norm1_gain, w_in, a_q_gain, a_k_gain,
           lambda_q1, lambda_k1, lambda_q2, lambda_k2, a_out_gain, w_a2, b_a, g_out_gain, w_out,
           norm2_gain, w_group, b_group, w_erouter, b_erouter, w_gate, w_up, w_down):
    import numpy as np
    import concourse.bacc as bacc
    from concourse.bass_utils import run_bass_kernel_spmd

    def rows(w):
        return w.reshape(-1, P, w.shape[-1]).transpose(1, 0, 2)

    wi = np.asarray(w_in)[0]
    cuts = np.cumsum([512, 512, 512, 256, 256, 512, RANK])
    aq, ak, av, gq, gk, gv, ga, gr = np.split(wi, cuts, axis=1)
    chunks = [np.concatenate([gq, gk], 1), gv, gr, ak, aq, av]
    x = np.concatenate([np.asarray(x_prompt).reshape(-1, D), np.asarray(x_sample).reshape(-1, D)]).reshape(NT, P, D)
    gains = [np.asarray(norm1_gain)[0].reshape(DC, P).T, np.asarray(norm2_gain)[0].reshape(DC, P).T,
             np.concatenate([np.asarray(a_q_gain)[0]] * 2)[:, None],
             np.asarray(a_out_gain)[0][:, None], np.asarray(g_out_gain)[0][:, None]]
    wg, wu, wd = np.asarray(w_gate)[0], np.asarray(w_up)[0], np.asarray(w_down)[0]
    gu = np.concatenate([wg, wu], 2).reshape(NE, DC, P, 2 * FE).transpose(0, 2, 1, 3)
    ins = {
        "x": x,
        "cache_kt": np.asarray(cache_k)[0].transpose(0, 3, 4, 2, 1).reshape(NB, P, H, PAST),
        "cache_v": np.asarray(cache_v)[0].reshape(NB, 4, P, 512).transpose(0, 2, 1, 3),
        "state": np.asarray(state_gla)[0].reshape(NB, 2, P, DV).transpose(2, 0, 1, 3),
        "w_main": np.stack([rows(c) for c in chunks]).reshape(6 * P, DC * 512),
        "w_ga": rows(ga).reshape(P, DC * RANK),
        "w_a2b": np.concatenate([np.asarray(w_a2)[0], np.asarray(b_a)], 0),
        "w_out": rows(np.asarray(w_out)[0]),
        "cols": np.concatenate(gains, 1),
        "k_gain": np.asarray(a_k_gain)[0],
        "lam": np.stack([np.asarray(v)[0] for v in (lambda_q1, lambda_k1, lambda_q2, lambda_k2)]),
        "w_r": rows(np.concatenate([np.asarray(w_group)[0], np.asarray(w_erouter)[0]], 1)),
        "b_r": np.concatenate([np.asarray(b_group)[0], np.asarray(b_erouter)[0]]),
        "w_gu": gu.reshape(NE * P, GU_W),
        "w_dn": wd.reshape(NE, 2, P, D).transpose(0, 2, 1, 3).reshape(NE * P, DN_W),
    }
    nc = bacc.Bacc("TRN2", target_bir_lowering=False, num_devices=1)
    arrays, args = {}, []
    for name, a in ins.items():
        a = np.ascontiguousarray(a)
        arrays[f"in_{name}"] = a
        args.append(nc.dram_tensor(f"in_{name}", a.shape, F32, kind="ExternalInput").ap())
    for name, shape in _OUTS:
        args.append(nc.dram_tensor(name, shape, F32, kind="ExternalOutput").ap())
    args.append(nc.dram_tensor("hn_dram", (NT * P, D), F32, kind="Internal").ap())
    args.append(nc.dram_tensor("ye_dram", (2 * NT * P, D), F32, kind="Internal").ap())
    build(nc, *args)
    r = run_bass_kernel_spmd(nc, [arrays], core_ids=[0]).results[0]
    y, k, v, s1, s2 = (r[name] for name, _ in _OUTS)
    y, k, v = y.reshape(NT * P, D), k.reshape(NT * P, 512), v.reshape(NT * P, 512)
    n = NP * P
    return (y[:n].reshape(1, n, D), y[n:].reshape(NB, Q, D),
            k[:n].reshape(1, 1, n, H, 2, DH), v[:n].reshape(1, 1, n, H, DV),
            s1.reshape(2, DH, 2, DV).transpose(2, 0, 1, 3).reshape(1, 1, H, DH, DV),
            k[n:].reshape(1, NB, Q, H, 2, DH), v[n:].reshape(1, NB, Q, H, DV),
            s2.reshape(2, DH, NB, 2, DV).transpose(2, 3, 0, 1, 4).reshape(1, NB, H, DH, DV))
```
